# Optimizing a Trainium2 kernel written in Bass

```python
import jax, jax.numpy as jnp
from jax import lax
import numpy as np

D_MODEL = 1024
BATCH = 1
SEQ = 128
DEPTH = 2
DEC_BATCH = 1
DEC_SEQ = 256
PAST_LEN = 128

GRID_W = 64
N_EVEN = (DEPTH + 1) // 2
N_ODD = DEPTH // 2
NORM_EPS = 1e-6
ROPE_BASE = 10000.0
HA = 4
DKA = 128
DVA = 128
GLA_CHUNK = 16
HB = 4
DKB = 128
DVB = 128
MLSTM_CHUNK = 64
HQ_C = 8
HKV_C = 2
G_C = HQ_C // HKV_C
HD_C = 64
WINDOW = 128
BAND_BLOCK = 128
H_D = 8
D_CQ = 384
D_C = 256
NOPE = 64
ROPE = 32
VD = 64
Q_BLOCK = 128
D_FF = -(-8 * D_MODEL // (3 * 256)) * 256
MIX_EVEN = HA * DVA + HB * DVB
MIX_ODD = HQ_C * HD_C + H_D * VD
EVEN_SPLITS = (HA * DKA, HA * DKA, HA * DKA, HA * DVA, HA * DVA, HB * DKB, HB * DKB, HB * DVB, HB * DVB, 4 * HB)
ODD_SPLITS = (HQ_C * HD_C, HKV_C * HD_C, HKV_C * HD_C, D_CQ, D_C, ROPE)
P_EVEN = sum(EVEN_SPLITS)
P_ODD = sum(ODD_SPLITS)
F32 = jnp.float32

kernel_name = 'hybrid_diffusion_prefix_trunk_step'

def rms_norm(x, g):
    x32 = x.astype(F32)
    y = x32 * lax.rsqrt(jnp.mean(x32 * x32, axis=-1, keepdims=True) + NORM_EPS)
    return y.astype(x.dtype) * g

def split_cols(p, sizes):
    return jnp.split(p, np.cumsum(sizes)[:-1].tolist(), axis=-1)

def axial_rope(x):
    T, d = x.shape[1], x.shape[-1]
    n_rows = T // GRID_W
    rows = jnp.repeat(jnp.arange(n_rows, dtype=F32), GRID_W)
    cols = jnp.tile(jnp.arange(GRID_W, dtype=F32), n_rows)
    d_ax = d // 2
    inv_freq = ROPE_BASE ** (-jnp.arange(0, d_ax, 2, dtype=F32) / d_ax)
    bshape = (1, T) + (1,) * (x.ndim - 3) + (d_ax // 2,)

    def rotate(xh, pos):
        ang = pos[:, None] * inv_freq[None, :]
        cos, sin = jnp.cos(ang).reshape(bshape), jnp.sin(ang).reshape(bshape)
        x1, x2 = jnp.split(xh, 2, axis=-1)
        return jnp.concatenate([x1 * cos - x2 * sin, x1 * sin + x2 * cos], axis=-1)

    x32 = x.astype(F32)
    out = jnp.concatenate([rotate(x32[..., :d_ax], rows), rotate(x32[..., d_ax:], cols)], axis=-1)
    return out.astype(x.dtype)

def gla_chunked(q, k, v, logf, s0):
    B, T, H, K = q.shape
    L = GLA_CHUNK
    N = T // L
    q, k, v, logf = [a.astype(F32).reshape((B, N, L, H, a.shape[-1])) for a in (q, k, v, logf)]
    b = jnp.cumsum(logf, axis=2)
    causal = jnp.tril(jnp.ones((L, L), bool))[None, None, :, :, None, None]
    diff = b[:, :, :, None] - b[:, :, None, :]
    decay = jnp.exp(jnp.where(causal, diff, -jnp.inf))
    attn = jnp.einsum('bntshk,bnthk,bnshk->bnhts', decay, q, k)
    o_intra = jnp.einsum('bnhts,bnshv->bnthv', attn, v)
    b_last = b[:, :, -1]
    kv = jnp.einsum('bnshk,bnshv->bnhkv', k * jnp.exp(b_last[:, :, None] - b), v)

    def step(S, inp):
        g, kv_c = inp
        return g[..., None] * S + kv_c, S

    s_fin, s_prev = lax.scan(step, s0.astype(F32), (jnp.moveaxis(jnp.exp(b_last), 1, 0), jnp.moveaxis(kv, 1, 0)))
    o_inter = jnp.einsum('bnthk,bnhkv->bnthv', q * jnp.exp(b), jnp.moveaxis(s_prev, 0, 1))
    return (o_intra + o_inter).reshape(B, T, H, -1), s_fin

def mlstm_chunked(q, k, v, ig, logf, c0, n0, m0):
    B, T, H, K = q.shape
    L = MLSTM_CHUNK
    N = T // L
    chunk = lambda a: jnp.moveaxis(a.astype(F32).reshape((B, N, L) + a.shape[2:]), 1, 0)
    causal = jnp.tril(jnp.ones((L, L), bool))[None, :, :, None]

    def step(carry, inp):
        C, n, m = carry
        qc, kc, vc, ic, fc = inp
        b = jnp.cumsum(fc, axis=1)
        w_state = b + m[:, None, :]
        w_in = jnp.where(causal, b[:, :, None, :] - b[:, None, :, :] + ic[:, None, :, :], -jnp.inf)
        m_t = jnp.maximum(w_state, jnp.max(w_in, axis=2))
        qk = jnp.einsum('bthk,bshk->btsh', qc, kc) * jnp.exp(w_in - m_t[:, :, None, :])
        s_state = jnp.exp(w_state - m_t)
        num = jnp.einsum('btsh,bshv->bthv', qk, vc) + s_state[..., None] * jnp.einsum('bthk,bhkv->bthv', qc, C)
        den = jnp.sum(qk, axis=2) + s_state * jnp.einsum('bthk,bhk->bth', qc, n)
        h = num / jnp.maximum(jnp.abs(den), jnp.exp(-m_t))[..., None]
        b_last = b[:, -1]
        w_end = b_last[:, None, :] - b + ic
        m_new = jnp.maximum(b_last + m, jnp.max(w_end, axis=1))
        a_state = jnp.exp(b_last + m - m_new)
        a_in = jnp.exp(w_end - m_new[:, None, :])
        c_new = a_state[..., None, None] * C + jnp.einsum('bsh,bshk,bshv->bhkv', a_in, kc, vc)
        n_new = a_state[..., None] * n + jnp.einsum('bsh,bshk->bhk', a_in, kc)
        return (c_new, n_new, m_new), h

    (C, n, m), h = lax.scan(step, (c0.astype(F32), n0.astype(F32), m0.astype(F32)),
                            (chunk(q), chunk(k), chunk(v), chunk(ig), chunk(logf)))
    return jnp.moveaxis(h, 0, 1).reshape(B, T, H, -1), C, n, m

def attend_dense(q, k, v, scale, sink=None):
    B, Tq, Hk, G, dq = q.shape
    nb = Tq // Q_BLOCK
    qb = jnp.moveaxis(q.reshape(B, nb, Q_BLOCK, Hk, G, dq), 1, 0)

    def one_block(qblk):
        s = jnp.einsum('bqhgd,bkhd->bhgqk', qblk, k).astype(F32) * scale
        if sink is not None:
            s_sink = jnp.broadcast_to(sink.astype(F32)[None, :, :, None, None], s.shape[:-1] + (1,))
            p = jax.nn.softmax(jnp.concatenate([s, s_sink], axis=-1), axis=-1)[..., :-1]
        else:
            p = jax.nn.softmax(s, axis=-1)
        return jnp.einsum('bhgqk,bkhv->bqhgv', p.astype(v.dtype), v)

    o = lax.map(one_block, qb)
    return jnp.moveaxis(o, 0, 1).reshape(B, Tq, Hk, G, -1)

def attend_window_with_context(q, k, v, k_ctx, v_ctx, sink, scale):
    B, T, Hk, G, d = q.shape
    P = k_ctx.shape[1]
    nb = T // BAND_BLOCK
    qb = q.reshape(B, nb, BAND_BLOCK, Hk, G, d)

    def band(a):
        ap = jnp.pad(a, ((0, 0), (BAND_BLOCK, BAND_BLOCK), (0, 0), (0, 0)))
        ap = ap.reshape(B, nb + 2, BAND_BLOCK, Hk, a.shape[-1])
        return jnp.concatenate([ap[:, :nb], ap[:, 1:nb + 1], ap[:, 2:]], axis=2)

    kb, vb = band(k), band(v)
    qi = jnp.arange(BAND_BLOCK)[:, None]
    kj = jnp.arange(3 * BAND_BLOCK)[None, :]
    kpos = jnp.arange(nb)[:, None, None] * BAND_BLOCK - BAND_BLOCK + kj[None]
    valid = (jnp.abs(kj - BAND_BLOCK - qi)[None] <= WINDOW) & (kpos >= 0) & (kpos < T)
    s_band = jnp.einsum('bnqhgd,bnkhd->bnhgqk', qb, kb).astype(F32) * scale
    s_band = jnp.where(valid[None, :, None, None], s_band, -jnp.inf)
    s_ctx = jnp.einsum('bnqhgd,bphd->bnhgqp', qb, k_ctx).astype(F32) * scale
    s_sink = jnp.broadcast_to(sink.astype(F32).reshape(1, 1, Hk, G, 1, 1), s_band.shape[:-1] + (1,))
    p = jax.nn.softmax(jnp.concatenate([s_band, s_ctx, s_sink], axis=-1), axis=-1)
    p_band = p[..., :3 * BAND_BLOCK].astype(v.dtype)
    p_ctx = p[..., 3 * BAND_BLOCK:3 * BAND_BLOCK + P].astype(v.dtype)
    o = jnp.einsum('bnhgqk,bnkhd->bnqhgd', p_band, vb) + jnp.einsum('bnhgqp,bphd->bnqhgd', p_ctx, v_ctx)
    return o.reshape(B, T, Hk, G, d)

def adaln(cond, w, b):
    m = jax.nn.silu(cond) @ w + b
    if m.ndim == 2:
        m = m[:, None, :]
    return jnp.split(m, 6, axis=-1)

def swiglu(h, w1, w3, w2):
    return (jax.nn.silu(h @ w1) * (h @ w3)) @ w2

def even_mixer(h, w_in, lb, hgrn_g, gate_bias, mlstm_g, w_out, s_hgrn, s_c, s_n, s_m):
    B, T, _ = h.shape
    qa, fa_f, fa_b, ia, ga, qb, kb, vb, ob, gates = split_cols(h @ w_in, EVEN_SPLITS)
    heads = lambda a, n: a.astype(F32).reshape(B, T, n, -1)
    qa = heads(jax.nn.silu(qa), HA)
    ia = heads(ia, HA)

    def hgrn_dir(f_raw, lbd, s0, flip):
        f = heads(lbd + (1.0 - lbd) * jax.nn.sigmoid(f_raw.astype(F32)), HA)
        args = (qa, 1.0 - f, ia, jnp.log(f))
        if flip:
            args = tuple(jnp.flip(a, axis=1) for a in args)
        o, s = gla_chunked(*args, s0)
        return (jnp.flip(o, axis=1) if flip else o), s

    oa_f, sa_f = hgrn_dir(fa_f, lb[0], s_hgrn[:, 0], False)
    oa_b, sa_b = hgrn_dir(fa_b, lb[1], s_hgrn[:, 1], True)
    oa = rms_norm(oa_f + oa_b, hgrn_g) * jax.nn.silu(heads(ga, HA))
    qb = heads(qb, HB) * (DKB ** -0.5)
    kb = heads(kb, HB)
    vb = heads(vb, HB)
    g = gates.astype(F32).reshape(B, T, 4, HB) + gate_bias.astype(F32)

    def mlstm_dir(ig, fg, c0, n0, m0, flip):
        args = (qb, kb, vb, ig, jax.nn.log_sigmoid(fg))
        if flip:
            args = tuple(jnp.flip(a, axis=1) for a in args)
        o, C, n, m = mlstm_chunked(*args, c0, n0, m0)
        return (jnp.flip(o, axis=1) if flip else o), C, n, m

    hb_f, c_f, n_f, m_f = mlstm_dir(g[:, :, 0], g[:, :, 1], s_c[:, 0], s_n[:, 0], s_m[:, 0], False)
    hb_b, c_b, n_b, m_b = mlstm_dir(g[:, :, 2], g[:, :, 3], s_c[:, 1], s_n[:, 1], s_m[:, 1], True)
    hb = rms_norm(hb_f + hb_b, mlstm_g) * jax.nn.sigmoid(heads(ob, HB))
    mix = jnp.concatenate([oa.reshape(B, T, -1), hb.reshape(B, T, -1)], axis=-1).astype(h.dtype)
    new = (jnp.stack([sa_f, sa_b], 1), jnp.stack([c_f, c_b], 1), jnp.stack([n_f, n_b], 1), jnp.stack([m_f, m_b], 1))
    return mix @ w_out, new

def odd_project(h, w_in, q_norm_g, w_uq, kv_norm_g):
    B, T, _ = h.shape
    qc, kc, vc, cq, ckv, kr = split_cols(h @ w_in, ODD_SPLITS)
    qc = qc.reshape(B, T, HKV_C, G_C, HD_C)
    kc = kc.reshape(B, T, HKV_C, HD_C)
    vc = vc.reshape(B, T, HKV_C, HD_C)
    qm = (rms_norm(cq, q_norm_g) @ w_uq).reshape(B, T, H_D, NOPE + ROPE)
    return qc, kc, vc, qm, rms_norm(ckv, kv_norm_g), kr

def mla_kv(ckv, kr, w_uk, w_uv):
    B, T, _ = ckv.shape
    k_nope = (ckv @ w_uk).reshape(B, T, H_D, NOPE)
    k = jnp.concatenate([k_nope, jnp.broadcast_to(kr[:, :, None, :], (B, T, H_D, ROPE)).astype(k_nope.dtype)], axis=-1)
    return k, (ckv @ w_uv).reshape(B, T, H_D, VD)

def odd_mixer_context(h, w_in, sink, q_norm_g, w_uq, kv_norm_g, w_uk, w_uv, w_out):
    B, T, _ = h.shape
    qc, kc, vc, qm, ckv, kr = odd_project(h, w_in, q_norm_g, w_uq, kv_norm_g)
    oc = attend_dense(qc, kc, vc, HD_C ** -0.5, sink.reshape(HKV_C, G_C))
    km, vm = mla_kv(ckv, kr, w_uk, w_uv)
    od = attend_dense(qm[:, :, :, None, :], km, vm, (NOPE + ROPE) ** -0.5)
    mix = jnp.concatenate([oc.reshape(B, T, -1), od.reshape(B, T, -1)], axis=-1)
    return mix @ w_out, kc, vc, ckv, kr

def odd_mixer_latent(h, w_in, sink, q_norm_g, w_uq, kv_norm_g, w_uk, w_uv, w_out, k_ctx, v_ctx, ckv_ctx, kr_ctx):
    B, T, _ = h.shape
    qc, kc, vc, qm, ckv, kr = odd_project(h, w_in, q_norm_g, w_uq, kv_norm_g)
    oc = attend_window_with_context(axial_rope(qc), axial_rope(kc), vc, k_ctx, v_ctx,
                                    sink.reshape(HKV_C, G_C), HD_C ** -0.5)
    qm = jnp.concatenate([qm[..., :NOPE], axial_rope(qm[..., NOPE:])], axis=-1)
    km, vm = mla_kv(jnp.concatenate([ckv, ckv_ctx.astype(ckv.dtype)], axis=1),
                    jnp.concatenate([axial_rope(kr), kr_ctx.astype(kr.dtype)], axis=1), w_uk, w_uv)
    od = attend_dense(qm[:, :, :, None, :], km, vm, (NOPE + ROPE) ** -0.5)
    mix = jnp.concatenate([oc.reshape(B, T, -1), od.reshape(B, T, -1)], axis=-1)
    return mix @ w_out

def setup_inputs(seed: int = 0) -> dict:
    key = jax.random.key(seed)
    ks = iter(jax.random.split(key, 48))
    nrm = lambda shape, s: s * jax.random.normal(next(ks), shape, F32)
    gain = lambda shape: 1.0 + nrm(shape, 0.02)
    fb = jnp.linspace(3.0, 6.0, HB, dtype=F32)
    gate_sel = jnp.array([0.0, 1.0, 0.0, 1.0], F32)
    return {
        'x_prompt': nrm((BATCH, SEQ, D_MODEL), 1.0),
        'x_sample': nrm((DEC_BATCH, DEC_SEQ, D_MODEL), 1.0),
        'state_hgrn': nrm((DEC_BATCH, N_EVEN, 2, HA, DKA, DVA), 0.5),
        'state_mlstm_c': nrm((DEC_BATCH, N_EVEN, 2, HB, DKB, DVB), 0.5),
        'state_mlstm_n': nrm((DEC_BATCH, N_EVEN, 2, HB, DKB), 0.5),
        'state_mlstm_m': nrm((DEC_BATCH, N_EVEN, 2, HB), 1.0),
        'cache_swa_k': nrm((DEC_BATCH, N_ODD, PAST_LEN, HKV_C, HD_C), 1.0),
        'cache_swa_v': nrm((DEC_BATCH, N_ODD, PAST_LEN, HKV_C, HD_C), 1.0),
        'cache_mla_ckv': nrm((DEC_BATCH, N_ODD, PAST_LEN, D_C), 1.0),
        'cache_mla_krope': nrm((DEC_BATCH, N_ODD, PAST_LEN, ROPE), 1.0),
        'c': nrm((DEC_BATCH, D_MODEL), 1.0),
        'c_ctx': nrm((D_MODEL,), 1.0),
        'w_in_even': nrm((N_EVEN, D_MODEL, P_EVEN), D_MODEL ** -0.5),
        'hgrn_lower_bounds': nrm((N_EVEN + 1, 2, HA * DKA), 0.5),
        'hgrn_norm_g': gain((N_EVEN, DVA)),
        'mlstm_gate_bias': nrm((N_EVEN, 4, HB), 0.1) + gate_sel[None, :, None] * fb[None, None, :],
        'mlstm_norm_g': gain((N_EVEN, DVB)),
        'w_out_even': nrm((N_EVEN, MIX_EVEN, D_MODEL), MIX_EVEN ** -0.5),
        'w_in_odd': nrm((N_ODD, D_MODEL, P_ODD), D_MODEL ** -0.5),
        'swa_sink': nrm((N_ODD, HQ_C), 1.0),
        'mla_q_norm_g': gain((N_ODD, D_CQ)),
        'mla_w_uq': nrm((N_ODD, D_CQ, H_D * (NOPE + ROPE)), D_CQ ** -0.5),
        'mla_kv_norm_g': gain((N_ODD, D_C)),
        'mla_w_uk': nrm((N_ODD, D_C, H_D * NOPE), D_C ** -0.5),
        'mla_w_uv': nrm((N_ODD, D_C, H_D * VD), D_C ** -0.5),
        'w_out_odd': nrm((N_ODD, MIX_ODD, D_MODEL), MIX_ODD ** -0.5),
        'ada_w': nrm((DEPTH, D_MODEL, 6 * D_MODEL), D_MODEL ** -0.5),
        'ada_b': nrm((DEPTH, 6 * D_MODEL), 0.02),
        'norm1_g': gain((DEPTH, D_MODEL)),
        'norm2_g': gain((DEPTH, D_MODEL)),
        'ffn_w1': nrm((DEPTH, D_MODEL, D_FF), D_MODEL ** -0.5),
        'ffn_w3': nrm((DEPTH, D_MODEL, D_FF), D_MODEL ** -0.5),
        'ffn_w2': nrm((DEPTH, D_FF, D_MODEL), D_FF ** -0.5),
        'final_norm_g': gain((D_MODEL,)),
    }

def reference(x_prompt, x_sample, state_hgrn, state_mlstm_c, state_mlstm_n, state_mlstm_m,
              cache_swa_k, cache_swa_v, cache_mla_ckv, cache_mla_krope, c, c_ctx,
              w_in_even, hgrn_lower_bounds, hgrn_norm_g, mlstm_gate_bias, mlstm_norm_g, w_out_even,
              w_in_odd, swa_sink, mla_q_norm_g, mla_w_uq, mla_kv_norm_g, mla_w_uk, mla_w_uv, w_out_odd,
              ada_w, ada_b, norm1_g, norm2_g, ffn_w1, ffn_w3, ffn_w2, final_norm_g):
    lb_all = jnp.cumsum(jax.nn.softmax(hgrn_lower_bounds.astype(F32), axis=0), axis=0)
    even_p = lambda j: (w_in_even[j], lb_all[j], hgrn_norm_g[j], mlstm_gate_bias[j], mlstm_norm_g[j], w_out_even[j])
    odd_p = lambda j: (w_in_odd[j], swa_sink[j], mla_q_norm_g[j], mla_w_uq[j], mla_kv_norm_g[j],
                       mla_w_uk[j], mla_w_uv[j], w_out_odd[j])

    x = x_prompt
    bp = x.shape[0]
    hg, mc, mn, mm, sk, sv, ck, cr = ([] for _ in range(8))
    for l in range(DEPTH):
        j = l // 2
        sh1, sc1, g1, sh2, sc2, g2 = adaln(c_ctx, ada_w[l], ada_b[l])
        h = rms_norm(x, norm1_g[l]) * (1.0 + sc1) + sh1
        if l % 2 == 0:
            out, (s_h, s_c, s_n, s_m) = even_mixer(
                h, *even_p(j),
                jnp.zeros((bp, 2, HA, DKA, DVA), F32), jnp.zeros((bp, 2, HB, DKB, DVB), F32),
                jnp.zeros((bp, 2, HB, DKB), F32), jnp.zeros((bp, 2, HB), F32))
            hg.append(s_h)
            mc.append(s_c)
            mn.append(s_n)
            mm.append(s_m)
        else:
            out, kc, vc, ckv, kr = odd_mixer_context(h, *odd_p(j))
            sk.append(kc)
            sv.append(vc)
            ck.append(ckv)
            cr.append(kr)
        x = x + g1 * out
        h = rms_norm(x, norm2_g[l]) * (1.0 + sc2) + sh2
        x = x + g2 * swiglu(h, ffn_w1[l], ffn_w3[l], ffn_w2[l])
    y_prompt = rms_norm(x, final_norm_g)

    x = x_sample
    for l in range(DEPTH):
        j = l // 2
        sh1, sc1, g1, sh2, sc2, g2 = adaln(c, ada_w[l], ada_b[l])
        h = rms_norm(x, norm1_g[l]) * (1.0 + sc1) + sh1
        if l % 2 == 0:
            out, _ = even_mixer(h, *even_p(j), state_hgrn[:, j], state_mlstm_c[:, j],
                                state_mlstm_n[:, j], state_mlstm_m[:, j])
        else:
            out = odd_mixer_latent(h, *odd_p(j), cache_swa_k[:, j], cache_swa_v[:, j],
                                   cache_mla_ckv[:, j], cache_mla_krope[:, j])
        x = x + g1 * out
        h = rms_norm(x, norm2_g[l]) * (1.0 + sc2) + sh2
        x = x + g2 * swiglu(h, ffn_w1[l], ffn_w3[l], ffn_w2[l])
    y_sample = rms_norm(x, final_norm_g)

    new_state_hgrn = jnp.stack(hg, axis=1)
    new_state_mlstm_c = jnp.stack(mc, axis=1)
    new_state_mlstm_n = jnp.stack(mn, axis=1)
    new_state_mlstm_m = jnp.stack(mm, axis=1)
    new_cache_swa_k = jnp.stack(sk, axis=1)
    new_cache_swa_v = jnp.stack(sv, axis=1)
    new_cache_mla_ckv = jnp.stack(ck, axis=1)
    new_cache_mla_krope = jnp.stack(cr, axis=1)
    return (y_prompt, y_sample, new_state_hgrn, new_state_mlstm_c, new_state_mlstm_n, new_state_mlstm_m,
            new_cache_swa_k, new_cache_swa_v, new_cache_mla_ckv, new_cache_mla_krope)


_drawn_inputs = setup_inputs


def setup_inputs(seed=0):
    import zlib

    import numpy as np

    out = dict(_drawn_inputs(seed))
    spreads = {}
    factors = {'state_hgrn': 8.0,
     'state_mlstm_c': 3.391,
     'state_mlstm_n': 6.303,
     'state_mlstm_m': 5.712,
     'cache_mla_ckv': 3.389,
     'cache_mla_krope': 6.416,
     'hgrn_norm_g': 7.891,
     'mlstm_norm_g': 8.0,
     'swa_sink': 8.0,
     'mla_q_norm_g': 8.0,
     'mla_kv_norm_g': 9.917,
     'norm2_g': 3.098,
     'final_norm_g': 7.813,
     'cache_swa_k': 8.0,
     'cache_swa_v': 8.0}
    for name, (base, spread) in spreads.items():
        noise = np.random.default_rng([zlib.crc32(name.encode()), seed]).standard_normal(out[name].shape)
        drawn = base * np.exp(spread * noise) if base else spread * noise
        out[name] = __import__('jax').numpy.asarray(drawn.astype(out[name].dtype))
    for name, factor in factors.items():
        out[name] = (out[name] * factor).astype(out[name].dtype)
    return out
```

```python
from contextlib import ExitStack

import numpy as np
import concourse.bass as bass
from concourse import mybir

F32 = mybir.dt.float32
F32R = mybir.dt.float32r
I32 = mybir.dt.int32
ALU = mybir.AluOpType
ACT = mybir.ActivationFunctionType
AX = mybir.AxisListType

P = 128
D = 1024
DT = D // P
TC = 128
TL = 256
T = TC + TL
NCH = T // P
H = 4
FF = 2816
FT = FF // P
WE = 4624
WO = 1440
EPS = 1e-6
HS = 8
TK = T + P
BIG = 1e30
LEVELS = [0, 1, 2, 4, 8, 16, 32, 64]

ROWS = {}
_n = 0
for _name, _k in (("norm1_g", 16), ("norm2_g", 16), ("final_norm_g", 8), ("c", 8), ("c_ctx", 8),
                  ("hgrn_lower_bounds", 16), ("hgrn_norm_g", 1), ("mlstm_norm_g", 1),
                  ("mla_q_norm_g", 3), ("mla_kv_norm_g", 2), ("state_mlstm_n", 8)):
    ROWS[_name] = (_n, _k)
    _n += _k
NROWS = _n

CONSTS = {}
_n = 0
for _name, _k in (("ident", 128), ("ones", 128), ("swa_cos", 256), ("swa_sin", 256), ("mla_cos", 256),
                  ("mla_sin", 256), ("swa_turn", 128), ("mla_turn", 128), ("levels", 8 * 128),
                  ("tri_f", 128), ("tri_b", 128), ("big_f", 128), ("big_b", 128), ("band0", 128),
                  ("band1", 128), ("rep", 128)):
    CONSTS[_name] = (_n, _k)
    _n += _k
NCONST = _n


def shape_constants():
    out = np.zeros((P, NCONST), np.float32)

    def put(name, value):
        a, k = CONSTS[name]
        out[:value.shape[0], a:a + k] = value.reshape(value.shape[0], k)

    put("ident", np.eye(P, dtype=np.float32))
    put("ones", np.ones((P, P), np.float32))
    pos = np.arange(TL)
    rows, cols = (pos // 64).astype(np.float32), (pos % 64).astype(np.float32)
    for name, d, n in (("swa", 64, 2), ("mla", 32, 4)):
        ax, half = d // 2, d // 4
        inv = (10000.0 ** (-np.arange(0, ax, 2, dtype=np.float32) / ax)).astype(np.float32)
        cos, sin = np.zeros((d, TL), np.float32), np.zeros((d, TL), np.float32)
        turn = np.zeros((d, d), np.float32)
        for a, at in ((0, rows), (1, cols)):
            ang = (at[None, :] * inv[:, None]).astype(np.float32)
            for s in (0, 1):
                r = a * ax + s * half
                cos[r:r + half], sin[r:r + half] = np.cos(ang), np.sin(ang)
            for i in range(half):
                x1, x2 = a * ax + i, a * ax + half + i
                turn[x2, x1] = -1.0
                turn[x1, x2] = 1.0
        put(name + "_cos", np.tile(cos, (n, 1)))
        put(name + "_sin", np.tile(sin, (n, 1)))
        put(name + "_turn", np.kron(np.eye(n, dtype=np.float32), turn))
    s, t = np.arange(P)[:, None], np.arange(P)[None, :]
    lv = [(s == t)] + [(s // (2 * L) == t // (2 * L)) & (s // L != t // L) for L in LEVELS[1:]]
    put("levels", np.stack(lv, 1).astype(np.float32))
    put("tri_f", (s <= t).astype(np.float32))
    put("tri_b", (s >= t).astype(np.float32))
    put("big_f", np.where(s > t, BIG, 0).astype(np.float32))
    put("big_b", np.where(s < t, BIG, 0).astype(np.float32))
    put("band0", np.where(t > s, -BIG, 0).astype(np.float32))
    put("band1", np.where(t < s, -BIG, 0).astype(np.float32))
    rep = np.zeros((P, P), np.float32)
    rep[96:] = np.tile(np.eye(32, dtype=np.float32), (1, 4))
    put("rep", rep)
    return out


def plan_units():
    units = []
    add = lambda name, n, kt, cols: units.extend((name, i, kt, cols) for i in range(n))
    for l in range(2):
        ada = lambda a, b: units.extend((f"ada{l}", i, DT, 256) for i in range(4 * a, 4 * b))
        ada(0, 2)
        if l == 0:
            add("in0", 18, DT, 256)
            units.append(("gates", 0, DT, 16))
            ada(2, 5)
            add("out0", 4, DT, 256)
        else:
            add("in1", 5, DT, 256)
            units.append(("in1", 5, DT, 160))
            add("uq", 2, 3, 384)
            add("uk", 2, 2, 256)
            add("uv", 2, 2, 256)
            ada(2, 5)
            add("out1", 4, DT, 256)
        add(f"up{l}", FT, DT, 256)
        ada(5, 6)
        add(f"down{l}", 16, 11, 128)
    return units


def build(nc, I, O):
    units = plan_units()
    RAW, SPLIT = 3, 2
    number = {(n, i): u for u, (n, i, _, _) in enumerate(units)}
    native = [n.startswith("ada") for n, _, _, _ in units]
    split_units = [u for u in range(len(units)) if not native[u]]
    split_index = {u: s for s, u in enumerate(split_units)}
    native_index = {u: s for s, u in enumerate(u for u in range(len(units)) if native[u])}

    ctx = ExitStack()
    with ctx:
        def sb(name, shape, dt=F32):
            return ctx.enter_context(nc.sbuf_tensor(name, shape, dt))

        def sem(name):
            return ctx.enter_context(nc.semaphore(name))

        X = sb("X", [P, DT, T])
        h_hi = sb("h_hi", [P, DT, T], F32R)
        h_lo = sb("h_lo", [P, DT, T], F32R)
        raw = [sb(f"raw{i}", [P, 2048]) for i in range(RAW)]
        w_hi = [sb(f"w_hi{i}", [P, 2048], F32R) for i in range(SPLIT)]
        w_lo = [sb(f"w_lo{i}", [P, 2048], F32R) for i in range(SPLIT)]
        const = sb("const", [P, NCONST])
        vec = sb("vec", [P, NROWS])
        ada_b_col = sb("ada_b_col", [P, 96])
        cond = sb("cond", [P, DT, 2])
        ada_row = sb("ada_row", [2, 1024])
        mod = sb("mod", [P, 2, 48, 2])
        gain = sb("gain", [P, 4, DT, 2])
        lb = sb("lb", [P, 8])
        oml = sb("oml", [P, 8])
        lbt = sb("lbt", [P, 3, 8])
        row_in = sb("row_in", [1, 32])
        rowb = sb("rowb", [P, 32])
        m0_col = sb("m0_col", [4, 2])
        sq = sb("sq", [P, 2, T])
        rstd = sb("rstd", [P, 2, T])
        ht = sb("ht", [P, 2, T])
        eps_col = sb("eps_col", [P, 1])
        neg_sink = sb("neg_sink", [P, 8])

        def overlay(tensors):
            with ExitStack() as phase:
                return [phase.enter_context(nc.sbuf_tensor(n, s, dt)) for n, s, dt in tensors]

        xtok, vec_rows, ada_rows = overlay([
            ("xtok", [P, NCH, D], F32), ("vec_rows", [P, P], F32), ("ada_rows", [96, P], F32)])
        HB = [P, H, T]
        (q, PF, SI, kf, kb, SF, PX, Qd, Kd, Am, S0, C0, va, vb, ga, qm, km) = overlay(
            [(n, HB, F32) for n in ("q", "PF", "SI", "kf", "kb", "SF", "PX", "Qd", "Kd")]
            + [("Am", [P, NCH, H, P], F32), ("S0", [P, 2, H, P], F32), ("C0", [P, 2, H, P], F32), ("va", [P, NCH, 512], F32), ("vb", [P, NCH, 512], F32)]
            + [(n, HB, F32) for n in ("ga", "qm", "km")])
        (qc, kT, vt, cqf, ckvf, cq_hi, cq_lo, ckv_hi, ckv_lo, kr4, qn, qr, kn, vm, krr, rt, pr, pT,
         cin_k, cin_c, cin_r, out_k, out_c, out_r, st) = overlay([
            ("qc", [P, 4, T], F32), ("kT", [P, TK], F32), ("vt", [P, 4, P], F32), ("cqf", [P, 3, T], F32),
            ("ckvf", [P, 2, T], F32), ("cq_hi", [P, 3, T], F32R), ("cq_lo", [P, 3, T], F32R),
            ("ckv_hi", [P, 2, TK], F32R), ("ckv_lo", [P, 2, TK], F32R), ("kr4", [P, TK], F32),
            ("qn", [P, 4, T], F32), ("qr", [P, 2, T], F32), ("kn", [P, 4, TK], F32), ("vm", [P, 4, 512], F32),
            ("krr", [P, T], F32), ("rt", [P, 2, TL], F32), ("pr", [P, 2, 512], F32), ("pT", [P, 2, 512], F32),
            ("cin_k", [P, P], F32), ("cin_c", [P, 256], F32), ("cin_r", [P, 4, 32], F32),
            ("out_k", [P, P], F32), ("out_c", [P, 256], F32), ("out_r", [P, 32], F32), ("st", [P, 2, 5, 4], F32)])
        u_hi, u_lo, sa, uf = overlay([
            ("u_hi", [P, FT, T], F32R), ("u_lo", [P, FT, T], F32R), ("sa", [P, 2, T], F32), ("uf", [P, 2, T], F32)])

        def cst(name):
            a, k = CONSTS[name]
            return const[:, a:a + k]

        ident, ones = cst("ident"), cst("ones")

        flat = lambda t: t[:].rearrange("p a b -> p (a b)")
        kt4 = [flat(kf)[:, 0:512], flat(kf)[:, 512:1024], flat(kf)[:, 1024:1536], flat(q)[:, 1024:1536]]
        ob = kb
        S1 = flat(q)[:, 0:1024].rearrange("p (d h v) -> p d h v", d=2, h=H)
        Sout = flat(PX)[:, 0:1024].rearrange("p (d h v) -> p d h v", d=2, h=H)
        o_hg = SF
        hm = PX
        rows = flat(q)[0:4, :].rearrange("p (k t) -> p k t", k=4)
        ss_row = flat(PF)[0:4, 0:512].rearrange("p (d t) -> p d t", d=2)
        row_copy = flat(Kd)[0:4, 0:T]
        k_tok = flat(PF)[:, 512:1024]
        k_in = flat(PF)[:, 1024:1280].rearrange("p (b k) -> p b k", b=2)
        G = flat(SI)[:, 0:48].rearrange("p (c j) -> p c j", c=NCH)
        LF = flat(SI)[:, 64:88].rearrange("p (c d h) -> p c d h", c=NCH, d=2)
        LE = flat(SI)[:, 96:120].rearrange("p (c d h) -> p c d h", c=NCH, d=2)
        GB = flat(SI)[:, 128:176].rearrange("p (c k h) -> p c k h", c=NCH, k=4)
        m_out = flat(SI)[0:4, 192:194]
        n_out = flat(SI)[0:1, 512:1536].rearrange("p (d h k) -> p d h k", d=2, h=H)
        QK = flat(kf)[:, 0:640]
        Ew = flat(SF)[:, 0:1024].rearrange("p (b n) -> p b n", b=2)
        Aw = flat(Qd)[:, 0:1024].rearrange("p (b n) -> p b n", b=2)
        em = flat(Kd)[:, 0:384]
        qs = flat(Kd)[:, 384:640]
        den = flat(Kd)[:, 640:1024]
        hf = flat(Kd)[:, 1024:1408]
        Cout = Am[:].rearrange("p c h t -> p (c h t)")[:, 0:1024].rearrange("p (d h v) -> p d h v", d=2, h=H)

        bank = [ctx.enter_context(nc.psum_tensor(f"bank{i}", [P, 512], F32)) for i in range(8)]

        class Ring:

            def __init__(self, name, banks):
                self.name, self.banks, self.n, self.at = name, banks, len(banks), {}
                self.done = sem(name + "_filled")
                self.free = [sem(f"{name}{b}_read") for b in banks]

            def fill(self, pe, key):
                m = self.at[key] = len(self.at)
                if m >= self.n:
                    pe.wait_ge(self.free[m % self.n], m // self.n)
                return bank[self.banks[m % self.n]]

            def filled(self, eng, key):
                eng.wait_ge(self.done, self.at[key] + 1)
                return bank[self.banks[self.at[key] % self.n]]

            def read(self, key):
                return self.free[self.at[key] % self.n]

            def was_read(self, eng, key):
                eng.wait_ge(self.read(key), self.at[key] // self.n + 1)

        dense = Ring("dense", [0, 1, 2, 3])
        misc = Ring("misc", [5, 6, 7])
        pvs = Ring("pv", [4])
        STAT = bank[4]
        S = {}

        def signal(*names):
            for n in names:
                S[n] = sem(n)

        signal("raw_in0", "raw_in1", "raw_in2", "hi_ready", "lo_ready", "half_used")
        signal("const_in", "rest_in", "rows_in", "adab_in", "small_in", "x_in", "state_in", "c0_in", "cache_in")
        signal("lb_exp", "cond_ready")
        signal("sq_ready", "stat_done", "stat_read", "rstd_ready", "ht_ready", "hhi_ready", "h_ready")
        signal("uhi_ready", "u_ready")
        signal("pe_own", "dve_own", "act_own")
        signal("raw_f", "level_ready", "kfin_ready", "qi_ready",
               "s_out")
        signal("gates_log", "gates_ready", "gates_abs", "rows_m", "rows_done", "A_ready", "k_in_ready", "h_done", "m_sent", "c_sent")
        signal("mo_sq", "mo_rstd", "mo_t")
        signal("roped", "cq_sq", "cq_rstd", "cq_t", "cqhi", "cq_ready", "ckv_ready", "cache_ready", "odd_sent",
               "neg_max", "p_ready", "pv_hi")
        signal("y_ready", "y_sent")
        release = {}
        raw_need, seen = [], [0] * RAW
        pieces = {u: (2 if n.startswith("up") else 6 if n == "uq" else 4 if n == "in1" and i < 2 else 1)
                  for u, (n, i, _, _) in enumerate(units)}
        for u in range(len(units)):
            seen[u % RAW] += 16 * pieces[u]
            raw_need.append(seen[u % RAW])
        raw_in = [S["raw_in0"], S["raw_in1"], S["raw_in2"]]
        block = ctx.enter_context(nc.Block())

        def mix_part(h, tile):
            kind, part, j = tile
            base = 0 if kind == "swa" else 4
            return h[:, base + 2 * j:base + 2 * j + 2, 0:P] if part == "ctx" else h[:, base + j, P:T]

        def mix_bank(bk, tile):
            return bk[:, 0:2 * P].rearrange("p (j t) -> p j t", j=2) if tile[1] == "ctx" else bk[:, 0:2 * P]

        marks = {}

        def mark(mm, key):
            marks[key] = len(marks) + 1
            mm.then_inc(S["half_used"], 1)

        jobs, job_tile = [], []
        for kind, base in (("swa", 0), ("mla", 4)):
            for g in range(2):
                jobs.append((kind, [4 * g + i for i in range(4)], 0, 0, P))
                job_tile.append((kind, "ctx", g))
            for j in range(4):
                for h in (2 * j, 2 * j + 1):
                    for t in (1, 2):
                        jobs.append((kind, [h], t, P, T))
                        job_tile.append((kind, "lat", j))
        ends = [(n == 0 or job_tile[n - 1] != job_tile[n], n == len(jobs) - 1 or job_tile[n + 1] != job_tile[n])
                for n in range(len(jobs))]

        def pv_at(n, h):
            kind, heads, t, _, _ = jobs[n]
            return (h - heads[0]) // 2 * P if t == 0 else (t - 1) * P

        starts = []
        for n, (kind, heads, t, _, _) in enumerate(jobs):
            starts.append({(i, 0) for i in range(2)} if t == 0 else ({(0, 0)} if t == 1 else set()))

        @block.tensor
        def _(pe):
            def raw_unit(u):
                pe.wait_ge(raw_in[u % RAW], raw_need[u])
                return raw[u % RAW][:, 0:2048].rearrange("p (k n) -> p k n", k=DT)

            def weight(u, kt, k, c, n=P):
                at = units[u][3] * k + c
                return w_hi[split_index[u] % SPLIT][:, at:at + n], w_lo[split_index[u] % SPLIT][:, at:at + n]

            def three(out, terms, first=True, last=True):
                for j, (s_hi, s_lo, m_hi, m_lo) in enumerate(terms):
                    pe.matmul(out, s_hi, m_hi, start=first and j == 0, stop=False)
                    pe.matmul(out, s_hi, m_lo, start=False, stop=False)
                    mm = pe.matmul(out, s_lo, m_hi, start=False, stop=last and j == len(terms) - 1)
                return mm

            def unit_ready(u):
                pe.wait_ge(S["lo_ready"], split_index[u] + 1)

            def features(key, u, c, k_tiles=DT, x=(h_hi, h_lo), n=T, ready=None):
                out = dense.fill(pe, key)[:, 0:n]
                unit_ready(u)
                if ready is not None:
                    for k in range(k_tiles):
                        pe.wait_ge(S["h_ready"], ready + k + 1)
                        w1, w2 = weight(u, k_tiles, k, c)
                        mm = three(out, [(w1, w2, x[0][:, k, :], x[1][:, k, :])], k == 0, k == k_tiles - 1)
                else:
                    mm = three(out, [(*weight(u, k_tiles, k, c), x[0][:, k, 0:n], x[1][:, k, 0:n])
                                     for k in range(k_tiles)])
                mm.then_inc(dense.done, 1)
                release[u] = (dense.done, dense.at[key] + 1)

            def tokens(key, u, c, n, chunk, k_tiles=DT, x=(h_hi, h_lo), out=None, more=False, last=True):
                bk = dense.fill(pe, key) if out is None else out[0]
                at = 0 if out is None else out[1]
                unit_ready(u)
                terms = []
                for k in range(k_tiles):
                    w1, w2 = weight(u, k_tiles, k, c, n)
                    s = slice(chunk * P, chunk * P + P)
                    terms.append((x[0][:, k, s], x[1][:, k, s], w1, w2))
                for j, (s_hi, s_lo, m_hi, m_lo) in enumerate(terms):
                    pe.matmul(bk[:, at:at + n], s_hi, m_hi, start=j == 0, stop=False)
                    pe.matmul(bk[:, at:at + n], s_hi, m_lo, start=False, stop=False)
                    mm = pe.matmul(bk[:, at:at + n], s_lo, m_hi, start=False, stop=j == k_tiles - 1)
                if last:
                    mm.then_inc(dense.done, 1)
                    release[u] = (dense.done, dense.at[key] + 1)
                return bk

            def turn(ring, key, parts):
                bk = ring.fill(pe, key)
                for at, src in parts:
                    rows, cols = src.shape
                    tr = pe.transpose(bk[0:cols, at:at + rows], src, const[0:rows, 0:rows])
                tr.then_inc(ring.done, 1)

            def modulation(l, first, end):
                for i in range(first, end):
                    u = number[(f"ada{l}", i)]
                    w = raw_unit(u)
                    out = misc.fill(pe, ("ada", l, i))
                    for k in range(DT):
                        mm = pe.matmul(out[0:2, 0:256], cond[:, k, :], w[:, k, :], start=k == 0, stop=k == DT - 1)
                    mm.then_inc(misc.done, 1)
                    release[u] = (misc.done, misc.at[("ada", l, i)] + 1)
                    if i % 4 == 3:
                        g = i // 4
                        out = misc.fill(pe, ("mod", l, g))
                        misc.was_read(pe, ("ada", l, i))
                        for j in range(8):
                            tr = pe.transpose(out[:, 2 * j:2 * j + 2], ada_row[:, j * P:(j + 1) * P], const[0:2, 0:2])
                        tr.then_inc(misc.done, 1)

            def stat(n, m):
                pe.wait_ge(S["sq_ready"], 8 * n + m + 1)
                if m == 0 and n:
                    pe.wait_ge(S["stat_read"], n)
                pe.matmul(bank[4][:, 0:T], ones, sq[:, m % 2, :], start=m == 0, stop=m == DT - 1)\
                    .then_inc(S["stat_done"], 1)

            def out_projection(l, ready, n):
                for m in range(DT):
                    features(("out", l, m), number[(f"out{l}", m // 2)], m % 2 * P, ready=None if m else ready)
                    if m:
                        stat(n, m - 1)
                stat(n, DT - 1)

            def ffn(l, ready, n):
                for f in range(FT):
                    u = number[(f"up{l}", f)]
                    features(("gate", l, f), u, 0, ready=ready if f == 0 else None)
                    features(("up", l, f), u, P)
                modulation(l, 20, 24)
                for m in range(DT):
                    out = dense.fill(pe, ("down", l, m))[:, 0:T]
                    for half in range(2):
                        u = number[(f"down{l}", 2 * m + half)]
                        unit_ready(u)
                        for k in range(11):
                            f = 11 * half + k
                            if m == 0:
                                pe.wait_ge(S["u_ready"], FT * l + f + 1)
                            mm = three(out, [(*weight(u, 11, k, 0), u_hi[:, f, :], u_lo[:, f, :])],
                                       f == 0, f == FT - 1)
                        if half == 0:
                            mark(mm, ("half", l, m))
                            release[u] = (S["half_used"], marks[("half", l, m)])
                    mm.then_inc(dense.done, 1)
                    release[u] = (dense.done, dense.at[("down", l, m)] + 1)
                    if m:
                        stat(n, m - 1)
                stat(n, DT - 1)

            pe.wait_ge(S["const_in"], 16)
            pe.wait_ge(S["rows_in"], 16 * len(ROWS))
            turn(misc, "vec", [(0, vec_rows[0:NROWS, :])])
            pe.wait_ge(S["adab_in"], 16)
            turn(misc, "ada_b", [(0, ada_rows[:, :])])
            pe.wait_ge(S["small_in"], 64)
            out = misc.fill(pe, "rowb")
            pe.matmul(out[:, 0:32], ones[0:1, :], row_in[:, :], start=True, stop=True).then_inc(misc.done, 1)
            pe.wait_ge(S["x_in"], 32)
            for c in range(NCH):
                for g in range(2):
                    turn(dense, ("x", c, g), [(j * P, xtok[:, c, (4 * g + j) * P:(4 * g + j + 1) * P])
                                              for j in range(4)])
            pe.wait_ge(S["cond_ready"], 1)
            modulation(0, 0, 8)
            for m in range(DT):
                stat(0, m)

            in0 = lambda c: (number[("in0", c // 256)], c % 256)
            for j in range(12):
                features(("in0", j), *in0(j * P), ready=0 if j == 0 else None)

            def level(i):
                pe.wait_ge(S["level_ready"], i + 1)
                for c in range(NCH):
                    out = misc.fill(pe, ("level", i, c))
                    for h in range(H):
                        mm = pe.matmul(out[:, h * P:(h + 1) * P], Kd[:, h, c * P:(c + 1) * P],
                                       Qd[:, h, c * P:(c + 1) * P], start=h == 0, stop=h == H - 1,
                                       skip_group_check=True)
                    mm.then_inc(misc.done, 1)

            for j in range(6, 18):
                if j in (6, 7, 14, 15):
                    for c in range(NCH):
                        tokens(("in0v", j, c), number[("in0", j)], 0, 256, c)
                else:
                    features(("in0", 2 * j), number[("in0", j)], 0)
                    features(("in0", 2 * j + 1), number[("in0", j)], P)
                if j < 14:
                    level(j - 6)
            bk = None
            for c in range(NCH):
                bk = tokens("gates", number[("gates", 0)], 0, 16, c, out=None if c == 0 else (bk, 16 * c),
                            last=c == NCH - 1)
            modulation(0, 8, 20)

            pe.wait_ge(S["kfin_ready"], 2)
            for i, (src, c) in enumerate(((SF, 0), (PX, 0), (SF, 1), (PX, 2))):
                turn(misc, ("kfin", i), [(h * P, src[:, h, c * P:(c + 1) * P]) for h in range(H)])
            for i, c in enumerate((0, 0, 1, 2)):
                misc.was_read(pe, ("kfin", i))
                out = misc.fill(pe, ("kv", i))
                for h in range(H):
                    mm = pe.matmul(out[:, h * P:(h + 1) * P], kt4[i][:, h * P:(h + 1) * P],
                                   va[:, c, h * P:(h + 1) * P], start=h == 0, stop=h == H - 1,
                                   skip_group_check=True)
                mm.then_inc(misc.done, 1)
            for c in range(NCH):
                misc.was_read(pe, ("level", len(LEVELS) - 1, c))
            for c in range(NCH):
                if c == 1:
                    misc.was_read(pe, ("kv", 2))
                    misc.was_read(pe, ("kv", 3))
                    pe.wait_ge(S["qi_ready"], 2)
                out = dense.fill(pe, ("hg_o", c))
                for h in range(H):
                    o = out[:, h * P:(h + 1) * P]
                    t = slice(c * P, (c + 1) * P)
                    terms = [(va[:, c, h * P:(h + 1) * P], Am[:, c, h, :])]
                    if c:
                        terms.append(((S0 if c == 1 else S1)[:, 0, h, :], Qd[:, h, t]))
                        terms.append(((S1 if c == 1 else S0)[:, 1, h, :], Kd[:, h, t]))
                    for a, (s, m) in enumerate(terms):
                        mm = pe.matmul(o, s, m, start=h == 0 and a == 0, stop=h == H - 1 and a == len(terms) - 1,
                                       skip_group_check=True)
                mm.then_inc(dense.done, 1)

            def mix_norm(kind, n0):
                for h in range(H):
                    pe.wait_ge(S["mo_sq"], n0 + h + 1)
                    out = misc.fill(pe, (kind, h))
                    pe.matmul(out[:, 0:T], ones, sq[:, h % 2, :], start=True, stop=True).then_inc(misc.done, 1)

            mix_norm("hg_norm", 0)

            tri_f, tri_b = cst("tri_f"), cst("tri_b")
            pe.wait_ge(S["gates_log"], 1)
            out = misc.fill(pe, "B")
            for d, tri, order in ((0, tri_f, (0, 1, 2)), (1, tri_b, (0, 2, 1))):
                for i, c in enumerate(order):
                    o = out[:, (c * 2 + d) * 4:(c * 2 + d) * 4 + 4]
                    start = d == 0 and c == 0
                    if i == 2:
                        pe.matmul(o, ones, LF[:, order[1], d, :], start=False, stop=False, skip_group_check=True)
                    mm = pe.matmul(o, tri, LF[:, c, d, :], start=start, stop=True, skip_group_check=True)
            mm.then_inc(misc.done, 1)
            misc.was_read(pe, "B")
            for c in range(NCH):
                turn(misc, ("rows", c), [(k * P, GB[:, c, k, :]) for k in range(4)])
            turn(misc, "k_tok", [(h * P, km[:, h, 0:P]) for h in range(H)])

            for h in range(H):
                bk = dense.fill(pe, ("qk", h))
                blocks = [(0, 0), (1, 1), (1, 2), (2, 2)]
                for i, (s, t) in enumerate(blocks):
                    mm = pe.matmul(bk[:, i * P:(i + 1) * P], km[:, h, s * P:(s + 1) * P], qm[:, h, t * P:(t + 1) * P],
                                   start=i == 0, stop=i == 3, skip_group_check=True)
                mm.then_inc(dense.done, 1)
                bk = dense.fill(pe, ("qk10", h))
                pe.matmul(bk[:, 0:P], km[:, h, 2 * P:3 * P], qm[:, h, P:2 * P], start=True, stop=True)\
                    .then_inc(dense.done, 1)
                for d in range(2):
                    j = 2 * h + d
                    sel = ident[0:4, h:h + 1].to_broadcast([4, P])
                    big = cst("big_f" if d == 0 else "big_b")
                    if j == 0:
                        pe.wait_ge(S["rows_done"], 2)
                        pe.wait_ge(S["c0_in"], 16)
                    bk = dense.fill(pe, ("M", j))
                    M = rows[:, d, :]
                    if d == 0:
                        pe.matmul(bk[:, 0:T], sel, M, start=True, stop=False, skip_group_check=True)
                        pe.matmul(bk[:, T:512], sel, M[:, 2 * P:T], start=False, stop=False, skip_group_check=True)
                        masked = (0, 1, 3)
                    else:
                        pe.matmul(bk[:, 0:T], sel, M, start=True, stop=False, skip_group_check=True)
                        pe.matmul(bk[:, T:512], sel, M[:, P:2 * P], start=False, stop=False, skip_group_check=True)
                        masked = (0, 1, 2)
                    for i in masked:
                        mm = pe.matmul(bk[:, i * P:(i + 1) * P], ident, big, start=False, stop=i == masked[-1],
                                       skip_group_check=True)
                    mm.then_inc(dense.done, 1)
                    bk = misc.fill(pe, ("em", j))
                    pe.matmul(bk[:, 0:T], sel, rows[:, 2 + d, :], start=True, stop=True).then_inc(misc.done, 1)
                    bk = misc.fill(pe, ("ss", j))
                    pe.matmul(bk[:, 0:TL], sel, ss_row[:, d, :], start=True, stop=True).then_inc(misc.done, 1)
                    pe.wait_ge(S["A_ready"], j + 1)
                    misc.was_read(pe, ("ss", j))
                    a = Aw[:, j % 2, :]
                    for key, lhs, st in ((("num", j), lambda c: vb[:, c, h * P:(h + 1) * P], C0[:, d, h, :]),
                                         (("den", j), lambda c: ones,
                                          vec[:, ROWS["state_mlstm_n"][0] + 4 * d + h:][:, 0:1].to_broadcast([P, P]))):
                        bk = misc.fill(pe, key) if key[0] == "num" else dense.fill(pe, key)
                        pe.matmul(bk[:, 0:P], lhs(0), a[:, 0:P], start=True, stop=False, skip_group_check=True)
                        pe.matmul(bk[:, P:T], st, qs, start=False, stop=False, skip_group_check=True)
                        if d == 0:
                            pe.matmul(bk[:, P:T], lhs(1), a[:, P:T], start=False, stop=False, skip_group_check=True)
                            mm = pe.matmul(bk[:, 2 * P:T], lhs(2), a[:, T:512], start=False, stop=True,
                                           skip_group_check=True)
                        else:
                            pe.matmul(bk[:, P:2 * P], lhs(1), a[:, P:2 * P], start=False, stop=False,
                                      skip_group_check=True)
                            pe.matmul(bk[:, 2 * P:T], lhs(2), a[:, 2 * P:T], start=False, stop=False,
                                      skip_group_check=True)
                            mm = pe.matmul(bk[:, P:2 * P], lhs(2), a[:, T:512], start=False, stop=True,
                                           skip_group_check=True)
                        mm.then_inc(misc.done if key[0] == "num" else dense.done, 1)
                    pe.wait_ge(S["k_in_ready"], j + 1)
                    bk = misc.fill(pe, ("C", j))
                    pe.matmul(bk[:, 0:P], k_in[:, j % 2, :], vb[:, 0, h * P:(h + 1) * P], start=True, stop=True,
                              skip_group_check=True)
                    at = 127 if d == 0 else 0
                    pe.matmul(bk[0:1, P:2 * P], Ew[:, j % 2, at:at + 1], k_tok[:, h * P:(h + 1) * P],
                              start=False, stop=True, skip_group_check=True).then_inc(misc.done, 1)
            mix_norm("ml_norm", 4)
            out_projection(0, 8, 1)
            ffn(0, 16, 2)

            modulation(1, 0, 8)
            in1 = lambda i: number[("in1", i)]
            for j in range(4):
                features(("qc", j), in1(j // 2), j % 2 * P, ready=24 if j == 0 else None)
            features(("kc",), in1(2), 0)
            bk = None
            for c in range(NCH):
                bk = tokens(("vc",), in1(2), P, P, c, out=None if c == 0 else (bk, P * c), last=c == 2)
            for j in range(3):
                features(("cq", j), in1(3 + j // 2), j % 2 * P)
            features(("ckv", 0), in1(4), P)
            features(("ckv", 1), in1(5), 0)
            features(("kr",), in1(5), 32)

            def norm_of(key, k_tiles, n0):
                out = misc.fill(pe, key)
                for k in range(k_tiles):
                    pe.wait_ge(S["cq_sq"], n0 + k + 1)
                    mm = pe.matmul(out[:, 0:T], ones, sq[:, k % 2, :], start=k == 0, stop=k == k_tiles - 1)
                    if k < k_tiles - 1:
                        mark(mm, (key, k))
                mm.then_inc(misc.done, 1)

            norm_of("cq_norm", 3, 0)
            norm_of("ckv_norm", 2, 3)
            turn_s, turn_m = cst("swa_turn"), cst("mla_turn")

            def rotate(key, matrix, src):
                out = misc.fill(pe, key)
                pe.matmul(out[:, 0:TL], matrix, src, start=True, stop=True).then_inc(misc.done, 1)

            for j in range(4):
                dense.was_read(pe, ("qc", j))
                rotate(("rot", j), turn_s, qc[:, j, P:T])
            dense.was_read(pe, ("kc",))
            rotate(("rot", 4), turn_s, kT[:, P:T])
            dense.was_read(pe, ("kr",))
            out = misc.fill(pe, ("rep",))
            pe.matmul(out[:, 0:T], cst("rep")[96:128, :], krr[96:128, :], start=True, stop=True).then_inc(misc.done, 1)
            misc.was_read(pe, ("rep",))
            rotate(("rot", 5), turn_m, kr4[:, P:T])
            pe.wait_ge(S["cache_in"], 16 * 7)
            turn(misc, ("cache",), [(0, cin_k[:]), (P, cin_r[:].rearrange("p a b -> p (a b)")),
                                    (2 * P, cin_c[:, 0:P]), (3 * P, cin_c[:, P:2 * P])])
            pe.wait_ge(S["cq_ready"], 3)
            for i in range(2):
                u = number[("uq", i)]
                for j in range(2):
                    features(("qn", 2 * i + j), u, j * P, 3, (cq_hi, cq_lo))
                features(("qr", i), u, 2 * P, 3, (cq_hi, cq_lo))
            for i in range(2):
                dense.was_read(pe, ("qr", i))
                rotate(("rot", 6 + i), turn_m, qr[:, i, P:T])
            pe.wait_ge(S["ckv_ready"], 2)
            misc.was_read(pe, ("cache",))
            for j in range(4):
                features(("kn", j), number[("uk", j // 2)], j % 2 * P, 2, (ckv_hi, ckv_lo), n=TK)
            for c in range(4):
                for i in range(2):
                    if i == 0:
                        bk = tokens(("vm", c), number[("uv", 0)], 0, 256, c, 2, (ckv_hi, ckv_lo), last=False)
                    else:
                        tokens(("vm", c), number[("uv", 1)], 0, 256, c, 2, (ckv_hi, ckv_lo), out=(bk, 256))
            release[number[("uv", 0)]] = release[number[("uv", 1)]]
            pe.wait_ge(S["cq_t"], 5)
            turn(misc, ("ctx_cache",), [(0, kT[:, 0:P]), (P, ckvf[:, 0, 0:P]), (2 * P, ckvf[:, 1, 0:P]),
                                        (3 * P, kr4[0:32, 0:P])])

            band = {1: cst("band0"), 2: cst("band1")}

            def scores(n, job):
                kind, heads, t, k0, nk = job
                if n == 0:
                    pe.wait_ge(S["roped"], 8)
                    dense.was_read(pe, ("vm", 3))
                    misc.was_read(pe, ("cache",))
                bk = dense.fill(pe, ("s", n))
                for i, h in enumerate(heads):
                    o = bk[:, i * nk:(i + 1) * nk]
                    tq = slice(t * P, (t + 1) * P)
                    if kind == "swa":
                        b = h // 4 * 64
                        mm = pe.matmul(o, qc[b:b + 64, h % 4, tq], kT[b:b + 64, k0:k0 + nk],
                                       start=i == 0, stop=t == 0, skip_group_check=True)
                        if t:
                            at = P if t == 1 else 0
                            mm = pe.matmul(bk[:, at:at + P], ident, band[t], start=False, stop=True,
                                           skip_group_check=True)
                    else:
                        b, r = h % 2 * 64, h % 4 * 32
                        if i:
                            pe_own[0] += 1
                            mm.then_inc(S["pe_own"], 1)
                            pe.wait_ge(S["pe_own"], pe_own[0])
                        pe.matmul(o, qn[b:b + 64, h // 2, tq], kn[b:b + 64, h // 2, k0:k0 + nk],
                                  start=i == 0, stop=False, skip_group_check=True)
                        mm = pe.matmul(o, qr[r:r + 32, h // 4, tq], kr4[r:r + 32, k0:k0 + nk],
                                       start=False, stop=True, skip_group_check=True,
                                       tile_position=(r, 0))
                mm.then_inc(dense.done, 1)

            def turned(n, job):
                kind, heads, t, k0, nk = job
                pe.wait_ge(S["p_ready"], n + 1)
                w = len(heads) * nk
                turn(misc, ("pT", n), [(i * P, pr[:, n % 2, i * P:(i + 1) * P]) for i in range(w // P)])

            def values(n, job):
                kind, heads, t, k0, nk = job
                misc.was_read(pe, ("pT", n))
                first, last = ends[n]
                if first:
                    pv_bank[0] = pvs.fill(pe, ("pv", job_tile[n]))
                for i, h in enumerate(heads):
                    b = h % 2 * 64
                    at = pv_at(n, h)
                    for k in range(nk // P):
                        chunk = k0 // P + k
                        v = (vt[:, chunk, h // 4 * 64:h // 4 * 64 + 64] if kind == "swa"
                             else vm[:, chunk, h * 64:h * 64 + 64])
                        mm = pe.matmul(pv_bank[0][b:b + 64, at:at + P], v,
                                       pT[:, n % 2, (i * nk + k * P):(i * nk + (k + 1) * P)],
                                       start=k == 0 and (i, at) in starts[n], stop=k == nk // P - 1,
                                       skip_group_check=True)
                if last:
                    mm.then_inc(pvs.done, 1)
                else:
                    mark(mm, ("pv", n))

            pv_bank = [None]
            pe_own = [0]
            for n in range(len(jobs) + 2):
                if n < len(jobs):
                    scores(n, jobs[n])
                if 1 <= n <= len(jobs):
                    turned(n - 1, jobs[n - 1])
                if n >= 2:
                    values(n - 2, jobs[n - 2])
            modulation(1, 8, 20)
            for tile in dict.fromkeys(job_tile):
                pvs.was_read(pe, ("pv", tile))
            out_projection(1, None, 3)
            ffn(1, 32, 4)
            for m in range(DT):
                pe.wait_ge(S["y_ready"], m + 1)
                turn(misc, ("y", m), [(c * P, ht[:, m % 2, c * P:(c + 1) * P]) for c in range(NCH)])

        @block.sync
        def _(sp):
            w = {"in0": I["w_in_even"][0], "in1": I["w_in_odd"][0], "out0": I["w_out_even"][0],
                 "out1": I["w_out_odd"][0], "uk": I["mla_w_uk"][0], "uv": I["mla_w_uv"][0],
                 "ada0": I["ada_w"][0], "ada1": I["ada_w"][1]}
            k_first = lambda a: a.rearrange("(k p) n -> p k n", p=P)
            for u, (name, i, kt, cols) in enumerate(units):
                if u >= RAW:
                    last = u - RAW
                    if native[last]:
                        sp.wait_ge(*release[last])
                    else:
                        sp.wait_ge(S["lo_ready"], split_index[last] + 1)
                dst = raw[u % RAW][:, 0:kt * cols].rearrange("p (k n) -> p k n", k=kt)
                if name[:2] == "up":
                    l = int(name[2])
                    pieces_of = [(dst[:, :, 0:P], k_first(I["ffn_w1"][l])[:, :, i * P:(i + 1) * P]),
                                 (dst[:, :, P:2 * P], k_first(I["ffn_w3"][l])[:, :, i * P:(i + 1) * P])]
                elif name[:4] == "down":
                    rows = slice(i % 2 * 11 * P, (i % 2 + 1) * 11 * P)
                    pieces_of = [(dst, k_first(I["ffn_w2"][int(name[4])][rows, i // 2 * P:(i // 2 + 1) * P]))]
                elif name == "gates":
                    pieces_of = [(dst, k_first(I["w_in_even"][0])[:, :, WE - 16:WE])]
                elif name == "in1" and i < 2:
                    src = k_first(w["in1"])[:, :, 0:512].rearrange("p k (g j e) -> p k g j e", g=2, j=4)
                    to = dst.rearrange("p k (j g e) -> p k g j e", j=2, g=2)
                    pieces_of = [(to[:, :, g, j], src[:, :, g, 2 * i + j]) for g in range(2) for j in range(2)]
                elif name == "uq":
                    src = k_first(I["mla_w_uq"][0])[:, :, i * 384:(i + 1) * 384].rearrange("p k (h e) -> p k h e", h=4)
                    heads = lambda a: a.rearrange("p (h e) -> p h e", h=4)
                    pieces_of = [(heads(dst[:, k, 0:256]), src[:, k, :, 0:64]) for k in range(3)]
                    pieces_of += [(heads(dst[:, k, 256:384]), src[:, k, :, 64:96]) for k in range(3)]
                else:
                    pieces_of = [(dst, k_first(w[name])[:, :, i * 256:i * 256 + cols])]
                assert len(pieces_of) == pieces[u]
                for to, src in pieces_of:
                    if name == "uq" or (name == "in1" and i < 2):
                        with nc.allow_non_contiguous_dma(reason="short runs of heads"):
                            sp.dma_start(to, src).then_inc(raw_in[u % RAW], 16)
                    else:
                        sp.dma_start(to, src).then_inc(raw_in[u % RAW], 16)

        @block.gpsimd
        def _(pool):
            for s, u in enumerate(split_units):
                n = units[u][2] * units[u][3]
                pool.wait_ge(S["hi_ready"], s + 1)
                pool.tensor_tensor(w_lo[s % SPLIT][:, 0:n], raw[u % RAW][:, 0:n],
                                   w_hi[s % SPLIT][:, 0:n].bitcast(F32), ALU.subtract).then_inc(S["lo_ready"], 1)

        @block.scalar
        def _(act):
            own = [0]
            split_at = [0]

            def step(ins):
                own[0] += 1
                ins.then_inc(S["act_own"], 1)
                act.wait_ge(S["act_own"], own[0])

            def split_to(end):
                while split_at[0] < min(end, len(split_units)):
                    s = split_at[0]
                    u = split_units[s]
                    n = units[u][2] * units[u][3]
                    act.wait_ge(raw_in[u % RAW], raw_need[u])
                    if s >= SPLIT:
                        act.wait_ge(*release[split_units[s - SPLIT]])
                    act.activation(w_hi[s % SPLIT][:, 0:n], raw[u % RAW][:, 0:n], ACT.Copy)\
                        .then_inc(S["hi_ready"], 1)
                    split_at[0] += 1

            def ahead(name, i, last=None):
                s = split_index[number[(name, i)]]
                split_to(min(s + SPLIT, last if last is not None else s + SPLIT))

            def end_of(name, n):
                return split_index[number[(name, n - 1)]] + 1

            def evacuate(ring, key, dst, src, func=ACT.Copy, **kw):
                bk = ring.filled(act, key)
                act.activation(dst, src(bk), func, **kw).then_inc(ring.read(key), 1)

            def square(src, i, sig="sq_ready"):
                act.activation(sq[:, i % 2, :], src, ACT.Square).then_inc(S[sig], 1)

            def norm(n, base, high=True):
                act.wait_ge(S["stat_done"], 8 * (n + 1))
                act.activation(rstd[:, 0, :], bank[4][:, 0:T], ACT.Ln, bias=eps_col[:, :], scale=1.0 / D)\
                    .then_inc(S["stat_read"], 1)
                act.wait_ge(S["stat_read"], n + 1)
                act.activation(rstd[:, 0, :], rstd[:, 0, :], ACT.Exp, scale=-0.5).then_inc(S["rstd_ready"], 1)
                if high:
                    for m in range(DT):
                        act.wait_ge(S["ht_ready"], base + m + 1)
                        act.activation(h_hi[:, m, :], ht[:, m % 2, :], ACT.Copy).then_inc(S["hhi_ready"], 1)

            def squares(n, m):
                if 8 * n + m >= 2:
                    act.wait_ge(S["stat_done"], 8 * n + m - 1)
                square(X[:, m, :], m)

            def out_projection(l, n):
                for m in range(DT):
                    ahead(f"out{l}", m // 2, end_of(f"up{l}", FT))
                    dense.was_read(act, ("out", l, m))
                    squares(n, m)
                split_to(split_index[number[(f"up{l}", 0)]] + SPLIT)

            def ffn(l, n):
                end = end_of(f"up{l}", FT)
                for f in range(FT):
                    ahead(f"up{l}", f, end)
                    bk = dense.filled(act, ("gate", l, f))
                    if f >= 2:
                        dense.was_read(act, ("up", l, f - 2))
                    act.activation(sa[:, f % 2, :], bk[:, 0:T], ACT.Silu).then_inc(dense.read(("gate", l, f)), 1)
                    dense.was_read(act, ("up", l, f))
                    act.activation(u_hi[:, f, :], uf[:, f % 2, :], ACT.Copy).then_inc(S["uhi_ready"], 1)
                for m in range(DT):
                    split_to(min(split_index[number[(f"down{l}", 2 * m + 1)]] + SPLIT, end_of(f"down{l}", 16)))
                    dense.was_read(act, ("down", l, m))
                    squares(n, m)

            act.dma_start(const[:, 0:256], I["shape_constants"][:, 0:256]).then_inc(S["const_in"], 16)
            for name, (at, k) in ROWS.items():
                a = I[name]
                src = {1: lambda: a.rearrange("(r e) -> r e", e=P),
                       2: lambda: a.rearrange("n (r e) -> (n r) e", e=P),
                       3: lambda: a.rearrange("n d (r e) -> (n d r) e", e=P),
                       5: lambda: a.rearrange("b n d h e -> (b n d h) e")}[len(a.shape)]()
                act.dma_start(vec_rows[at:at + k, :], src).then_inc(S["rows_in"], 16)
            act.dma_start(ada_rows[:, :], I["ada_b"].rearrange("l (r e) -> (l r) e", e=P)).then_inc(S["adab_in"], 16)
            act.dma_start(row_in[:, 0:8], I["swa_sink"]).then_inc(S["small_in"], 16)
            act.dma_start(row_in[:, 8:24], I["mlstm_gate_bias"].rearrange("n k h -> n (k h)"))\
                .then_inc(S["small_in"], 16)
            act.dma_start(row_in[:, 24:32], I["state_mlstm_m"].rearrange("b n d h -> (b n) (d h)"))\
                .then_inc(S["small_in"], 16)
            act.dma_start(xtok[:, 0, :], I["x_prompt"][0]).then_inc(S["x_in"], 16)
            act.dma_start(xtok[:, 1:3, :], I["x_sample"][0].rearrange("(c p) d -> p c d", p=P)).then_inc(S["x_in"], 16)
            act.dma_start(const[:, 256:NCONST], I["shape_constants"][:, 256:NCONST]).then_inc(S["rest_in"], 16)
            act.dma_start(S0[:], I["state_hgrn"].rearrange("b n d h k v -> k (b n d) h v")).then_inc(S["state_in"], 16)
            act.dma_start(C0[:], I["state_mlstm_c"].rearrange("b n d h k v -> k (b n d) h v"))\
                .then_inc(S["c0_in"], 16)
            with nc.allow_non_contiguous_dma(reason="eight values"):
                act.dma_start(m0_col[:, :], I["state_mlstm_m"].rearrange("b n d h -> h (b n d)"))\
                    .then_inc(S["small_in"], 16)

            misc.was_read(act, "vec")
            col = lambda name, n=None: vec[:, ROWS[name][0]:ROWS[name][0] + ROWS[name][1]]
            act.activation(cond[:, :, 0], col("c"), ACT.Silu)
            act.activation(cond[:, :, 1], col("c_ctx"), ACT.Silu).then_inc(S["cond_ready"], 1)
            for c in range(NCH):
                for g in range(2):
                    dense.was_read(act, ("x", c, g))
            act.wait_ge(S["raw_f"], 1)
            act.activation(lbt[:, 0:2, :], lbt[:, 0:2, :], ACT.Exp).then_inc(S["lb_exp"], 1)
            for m in range(DT):
                squares(0, m)
            norm(0, 0)

            end = end_of("gates", 1)
            split_to(SPLIT)
            for j in range(12):
                ahead("in0", j // 2, end)
                bk = dense.filled(act, ("in0", j))
                h = j % 4
                dst, f = ((q, ACT.Silu), (PF, ACT.Sigmoid), (SI, ACT.Sigmoid))[j // 4]
                act.activation(dst[:, h, :], bk[:, 0:T], f).then_inc(dense.read(("in0", j)), 1)
            for j in range(6, 18):
                ahead("in0", j, end)
                if j == 16:
                    act.wait_ge(S["kfin_ready"], 2)
                if j in (6, 7, 14, 15):
                    dst = va if j < 8 else vb
                    for c in range(NCH):
                        evacuate(dense, ("in0v", j, c), dst[:, c, j % 2 * 256:j % 2 * 256 + 256], lambda b: b[:, 0:256])
                else:
                    for i in (2 * j, 2 * j + 1):
                        dst, f, sc = {4: (ga, ACT.Silu, 1.0), 5: (qm, ACT.Copy, P ** -0.5), 6: (km, ACT.Copy, 1.0),
                                      8: (ob, ACT.Sigmoid, 1.0)}[i // 4]
                        evacuate(dense, ("in0", i), dst[:, i % 4, :], lambda b: b[:, 0:T], f, scale=sc)

            act.wait_ge(S["qi_ready"], 2)
            for i in range(4):
                evacuate(misc, ("kfin", i), kt4[i], lambda b: b[:, :])
            for i in range(2):
                bk = misc.filled(act, ("kv", i))
                act.activation(Sout[:, i, :, :], bk[:, :].rearrange("p (h v) -> p h v", h=H), ACT.Copy)\
                    .then_inc(misc.read(("kv", i)), 1)
            misc.was_read(act, ("kv", 1))
            act.dma_start(O[2].rearrange("b n d h k v -> k (b n d) h v"), Sout).then_inc(S["s_out"], 16)

            def mixer_out(kind, src, n0, base):
                for h in range(H + 1):
                    if h < H:
                        if h >= 2:
                            misc.filled(act, (kind, h - 2))
                        square(src[:, h, :], h, "mo_sq")
                    if h:
                        g = h - 1
                        bk = misc.filled(act, (kind, g))
                        if n0 + g >= 2:
                            act.wait_ge(S["mo_t"], n0 + g - 1)
                        act.activation(rstd[:, g % 2, :], bk[:, 0:T], ACT.Ln, bias=eps_col[:, :], scale=1.0 / P)\
                            .then_inc(misc.read((kind, g)), 1)
                        misc.was_read(act, (kind, g))
                        act.activation(rstd[:, g % 2, :], rstd[:, g % 2, :], ACT.Exp, scale=-0.5)\
                            .then_inc(S["mo_rstd"], 1)
                        act.wait_ge(S["ht_ready"], base + g + 1)
                        act.activation(h_hi[:, base - 8 + g, :], ht[:, g % 2, :], ACT.Copy)\
                            .then_inc(S["hhi_ready"], 1)

            for c in range(NCH):
                dense.was_read(act, ("hg_o", c))
            mixer_out("hg_norm", o_hg, 0, 8)

            G5 = G.rearrange("p c (d k h) -> p c d k h", d=2, k=2)
            act.wait_ge(S["gates_ready"], 1)
            step(act.activation(LE, G5[:, :, :, 1, :], ACT.Abs))
            step(act.activation(LE, LE, ACT.Exp, scale=-1.0))
            act.activation(LE, LE, ACT.Ln, bias=1.0).then_inc(S["gates_abs"], 1)
            evacuate(misc, "k_tok", k_tok, lambda b: b[:, :])
            act.wait_ge(S["rows_m"], 2)
            with nc.allow_non_contiguous_dma(reason="eight values"):
                act.dma_start(O[5].rearrange("b n d h -> h (b n d)"), m_out).then_inc(S["m_sent"], 16)
            step(act.activation(rows[:, 2:4, :], rows[:, 2:4, :], ACT.Exp, scale=-1.0))
            for d in range(2):
                act.activation(ss_row[:, d, :], rows[:, d, P:T], ACT.Exp, scale=-1.0, bias=m0_col[:, d:d + 1])\
                    .then_inc(S["rows_done"], 1)
            split_to(split_index[number[("out0", 0)]] + SPLIT)
            for h in range(H):
                if h:
                    act.wait_ge(S["A_ready"], 2 * h)
                evacuate(dense, ("qk", h), QK[:, 0:512], lambda b: b[:, :])
                evacuate(dense, ("qk10", h), QK[:, 512:640], lambda b: b[:, 0:P])
                for d in range(2):
                    j = 2 * h + d
                    bk = dense.filled(act, ("M", j))
                    if j >= 2:
                        act.wait_ge(S["k_in_ready"], j - 1)
                        misc.filled(act, ("C", j - 2))
                    cuts = (0, P, T, 512) if d == 0 else (0, P, 2 * P, 512)
                    for c in range(NCH):
                        e = act.activation(Ew[:, j % 2, cuts[c]:cuts[c + 1]], bk[:, cuts[c]:cuts[c + 1]], ACT.Exp,
                                           scale=-1.0, bias=GB[:, c, d, h:h + 1])
                    e.then_inc(dense.read(("M", j)), 1)
                    if j:
                        act.wait_ge(S["h_done"], j)
                    evacuate(misc, ("em", j), em, lambda b: b[:, 0:T])
                    evacuate(dense, ("den", j), den, lambda b: b[:, 0:T], ACT.Abs)
                    bk = misc.filled(act, ("C", j))
                    act.activation(Cout[:, d, h, :], bk[:, 0:P], ACT.Copy)
                    act.activation(n_out[:, d, h, :], bk[0:1, P:2 * P], ACT.Copy).then_inc(misc.read(("C", j)), 1)
            misc.was_read(act, ("C", 7))
            act.dma_start(O[3].rearrange("b n d h k v -> k (b n d) h v"), Cout).then_inc(S["c_sent"], 16)
            act.dma_start(O[4].rearrange("b n d h k -> (b n) d h k"), n_out).then_inc(S["c_sent"], 16)
            act.wait_ge(S["h_done"], 8)
            mixer_out("ml_norm", hm, 4, 12)
            out_projection(0, 1)
            norm(1, 16)
            act.wait_ge(S["s_out"], 16)
            act.wait_ge(S["m_sent"], 16)
            act.wait_ge(S["c_sent"], 32)
            ffn(0, 2)

            cache = [(cin_k[:], I["cache_swa_k"].rearrange("b n t h e -> (b n t) (h e)")),
                     (vt[:, 3, :], I["cache_swa_v"].rearrange("b n t h e -> (b n t) (h e)")),
                     (cin_c[:], I["cache_mla_ckv"].rearrange("b n t e -> (b n t) e"))]
            cache += [(cin_r[:, i, :], I["cache_mla_krope"].rearrange("b n t e -> (b n t) e")) for i in range(4)]
            for dst, src in cache:
                act.dma_start(dst, src).then_inc(S["cache_in"], 16)
            norm(2, 24)
            end = end_of("uv", 2)
            split_to(split_index[number[("in1", 0)]] + SPLIT)
            for j in range(4):
                ahead("in1", j // 2, end)
                evacuate(dense, ("qc", j), qc[:, j, :], lambda b: b[:, 0:T])
            ahead("in1", 2, end)
            evacuate(dense, ("kc",), kT[:, 0:T], lambda b: b[:, 0:T])
            evacuate(dense, ("vc",), vt[:, 0:3, :], lambda b: b[:, 0:T].rearrange("p (c e) -> p c e", c=3))
            for j in range(3):
                ahead("in1", 3 + j // 2, end)
                evacuate(dense, ("cq", j), cqf[:, j, :], lambda b: b[:, 0:T])
            evacuate(dense, ("ckv", 0), ckvf[:, 0, :], lambda b: b[:, 0:T])
            ahead("in1", 5, end)
            evacuate(dense, ("ckv", 1), ckvf[:, 1, :], lambda b: b[:, 0:T])
            evacuate(dense, ("kr",), krr[96:128, :], lambda b: b[96:128, 0:T])
            n = 0
            for i, (key, src, k_tiles) in enumerate((("cq_norm", cqf, 3), ("ckv_norm", ckvf, 2))):
                for k in range(k_tiles):
                    if k == 2:
                        act.wait_ge(S["half_used"], marks[(key, 0)])
                    if i == 0:
                        dense.was_read(act, ("cq", k))
                    else:
                        if k == 0:
                            misc.filled(act, "cq_norm")
                        dense.was_read(act, ("ckv", k))
                    square(src[:, k, :], k, "cq_sq")
                bk = misc.filled(act, key)
                act.activation(rstd[:, i, :], bk[:, 0:T], ACT.Ln, bias=eps_col[:, :], scale=1.0 / (k_tiles * P))\
                    .then_inc(misc.read(key), 1)
                misc.was_read(act, key)
                act.activation(rstd[:, i, :], rstd[:, i, :], ACT.Exp, scale=-0.5).then_inc(S["cq_rstd"], 1)
            for k in range(5):
                act.wait_ge(S["cq_t"], k + 1)
                dst, src = (cq_hi[:, k, :], cqf[:, k, :]) if k < 3 else (ckv_hi[:, k - 3, 0:T], ckvf[:, k - 3, :])
                act.activation(dst, src, ACT.Copy).then_inc(S["cqhi"], 1)
            evacuate(misc, ("rep",), kr4[:, 0:T], lambda b: b[:, 0:T])
            bk = misc.filled(act, ("cache",))
            act.activation(kT[:, T:TK], bk[:, 0:P], ACT.Copy)
            act.activation(kr4[:, T:TK], bk[:, P:2 * P], ACT.Copy)
            act.activation(ckv_hi[:, :, T:TK], bk[:, 2 * P:512].rearrange("p (k t) -> p k t", k=2), ACT.Copy)\
                .then_inc(S["cache_ready"], 1)
            for i in range(2):
                ahead("uq", i, end)
                for j in range(2):
                    evacuate(dense, ("qn", 2 * i + j), qn[:, 2 * i + j, :], lambda b: b[:, 0:T])
                evacuate(dense, ("qr", i), qr[:, i, :], lambda b: b[:, 0:T])
            for j in range(4):
                ahead("uk", j // 2, end)
                evacuate(dense, ("kn", j), kn[:, j, :], lambda b: b[:, :])
            split_to(end)
            for c in range(4):
                evacuate(dense, ("vm", c), vm[:, c, :], lambda b: b[:, :])
            bk = misc.filled(act, ("ctx_cache",))
            act.activation(out_k[:], bk[:, 0:P], ACT.Copy)
            act.activation(out_c[:], bk[:, P:3 * P], ACT.Copy)
            act.activation(out_r[:], bk[:, 3 * P:3 * P + 32], ACT.Copy).then_inc(misc.read(("ctx_cache",)), 1)
            misc.was_read(act, ("ctx_cache",))
            act.dma_start(O[6].rearrange("b n t h e -> (b n t) (h e)"), out_k[:]).then_inc(S["odd_sent"], 16)
            act.dma_start(O[7].rearrange("b n t h e -> (b n t) (h e)"), vt[:, 0, :]).then_inc(S["odd_sent"], 16)
            act.dma_start(O[8].rearrange("b n t e -> (b n t) e"), out_c[:]).then_inc(S["odd_sent"], 16)
            act.dma_start(O[9].rearrange("b n t e -> (b n t) e"), out_r[:]).then_inc(S["odd_sent"], 16)

            for n in range(len(jobs) + 2):
                if n < len(jobs):
                    kind, heads, t, k0, nk = jobs[n]
                    scale = 64 ** -0.5 if kind == "swa" else 96 ** -0.5
                    act.wait_ge(S["neg_max"], n + 1)
                    if n >= 2:
                        misc.filled(act, ("pT", n - 2))
                    if kind == "swa":
                        act.activation(st[:, n % 2, 3, 0:len(heads)], st[:, n % 2, 3, 0:len(heads)], ACT.Exp)
                    bk = dense.filled(act, ("s", n))
                    for i in range(len(heads)):
                        e = act.activation(pr[:, n % 2, i * nk:(i + 1) * nk], bk[:, i * nk:(i + 1) * nk], ACT.Exp,
                                           scale=scale, bias=st[:, n % 2, 1, i:i + 1],
                                           accum_out=st[:, n % 2, 2, i:i + 1])
                    e.then_inc(dense.read(("s", n)), 1)
                if 1 <= n <= len(jobs):
                    kind, heads, t, k0, nk = jobs[n - 1]
                    w = len(heads) * nk
                    if n >= 3:
                        if ("pv", n - 3) in marks:
                            act.wait_ge(S["half_used"], marks[("pv", n - 3)])
                        else:
                            pvs.filled(act, ("pv", job_tile[n - 3]))
                    evacuate(misc, ("pT", n - 1), pT[:, (n - 1) % 2, 0:w], lambda b: b[:, 0:w])
                if n >= 2 and ends[n - 2][1]:
                    tile = job_tile[n - 2]
                    bk = pvs.filled(act, ("pv", tile))
                    act.activation(mix_part(h_hi, tile), mix_bank(bk, tile), ACT.Copy).then_inc(S["pv_hi"], 1)
            split_to(split_index[number[("out1", 0)]] + SPLIT)
            out_projection(1, 3)
            norm(3, 32)
            act.wait_ge(S["odd_sent"], 64)
            ffn(1, 4)
            norm(4, 0, high=False)
            for m in range(DT):
                evacuate(misc, ("y", m), xtok[:, :, m * P:(m + 1) * P],
                         lambda b: b[:, 0:T].rearrange("p (c e) -> p c e", c=NCH))
            for m in range(DT):
                misc.was_read(act, ("y", m))
            act.dma_start(O[0][0], xtok[:, 0, :]).then_inc(S["y_sent"], 16)
            act.dma_start(O[1][0].rearrange("(c p) d -> p c d", p=P), xtok[:, 1:3, :]).then_inc(S["y_sent"], 16)
            act.wait_ge(S["y_sent"], 32)

        @block.vector
        def _(dve):
            own = [0]
            col = lambda name, i=None: (vec[:, ROWS[name][0]:ROWS[name][0] + ROWS[name][1]] if i is None
                                        else vec[:, ROWS[name][0] + i:ROWS[name][0] + i + 1])

            def step(ins):
                own[0] += 1
                ins.then_inc(S["dve_own"], 1)
                dve.wait_ge(S["dve_own"], own[0])

            def modulation(l, first, end):
                for i in range(first, end):
                    bk = misc.filled(dve, ("ada", l, i))
                    dve.tensor_copy(ada_row[:, i % 4 * 256:i % 4 * 256 + 256], bk[0:2, 0:256])\
                        .then_inc(misc.read(("ada", l, i)), 1)
                    if i % 4 == 3:
                        g = i // 4
                        bk = misc.filled(dve, ("mod", l, g))
                        dve.tensor_tensor(mod[:, l, 8 * g:8 * g + 8, :], bk[:, 0:16].rearrange("p (j c) -> p j c", c=2),
                                          ada_b_col[:, 48 * l + 8 * g:48 * l + 8 * g + 8].unsqueeze(2)
                                          .to_broadcast([P, 8, 2]), ALU.add).then_inc(misc.read(("mod", l, g)), 1)
                        misc.was_read(dve, ("mod", l, g))

            def gains(n):
                l, k = n // 2, 1 + 3 * (n % 2)
                step(dve.tensor_scalar(gain[:, n], mod[:, l, 8 * k:8 * k + 8, :], 1.0, None, ALU.add))
                g = vec[:, ROWS[f"norm{n % 2 + 1}_g"][0] + 8 * l:][:, 0:8]
                step(dve.tensor_tensor(gain[:, n], gain[:, n], g.unsqueeze(2).to_broadcast([P, 8, 2]), ALU.mult))

            def low(m, base):
                dve.wait_ge(S["hhi_ready"], base + m + 1)
                dve.tensor_tensor(h_lo[:, m, :], ht[:, m % 2, :], h_hi[:, m, :].bitcast(F32), ALU.subtract)\
                    .then_inc(S["h_ready"], 1)

            def norm(n, base):
                l, k = n // 2, 3 * (n % 2)
                gains(n)
                dve.wait_ge(S["rstd_ready"], n + 1)
                for m in range(DT):
                    if m >= 2:
                        dve.wait_ge(S["h_ready"], base + m - 1)
                    step(dve.tensor_tensor(ht[:, m % 2, :], X[:, m, :], rstd[:, 0, :], ALU.mult))
                    for c, a, b in ((1, 0, TC), (0, TC, T)):
                        ins = dve.tensor_scalar(ht[:, m % 2, a:b], ht[:, m % 2, a:b], gain[:, n, m, c:c + 1],
                                                mod[:, l, 8 * k + m, c:c + 1], ALU.mult, ALU.add)
                    ins.then_inc(S["ht_ready"], 1)
                    if m:
                        low(m - 1, base)
                low(DT - 1, base)

            def residual(key, l, m, k):
                bk = dense.filled(dve, key)
                for c, a, b in ((1, 0, TC), (0, TC, T)):
                    ins = dve.scalar_tensor_tensor(X[:, m, a:b], bk[:, a:b], mod[:, l, 8 * k + m, c:c + 1],
                                                   X[:, m, a:b], ALU.mult, ALU.add)
                ins.then_inc(dense.read(key), 1)

            def ffn(l):
                def low_u(f):
                    dve.wait_ge(S["uhi_ready"], FT * l + f + 1)
                    dve.tensor_tensor(u_lo[:, f, :], uf[:, f % 2, :], u_hi[:, f, :].bitcast(F32), ALU.subtract)\
                        .then_inc(S["u_ready"], 1)
                for f in range(FT):
                    dense.was_read(dve, ("gate", l, f))
                    bk = dense.filled(dve, ("up", l, f))
                    if f >= 2:
                        dve.wait_ge(S["u_ready"], FT * l + f - 1)
                    dve.tensor_tensor(uf[:, f % 2, :], sa[:, f % 2, :], bk[:, 0:T], ALU.mult)\
                        .then_inc(dense.read(("up", l, f)), 1)
                    if f:
                        low_u(f - 1)
                low_u(FT - 1)
                modulation(l, 20, 24)
                for m in range(DT):
                    residual(("down", l, m), l, m, 5)

            dve.memset(eps_col[:, :], EPS).then_inc(S["dve_own"], 1)
            own[0] += 1
            bk = misc.filled(dve, "vec")
            dve.tensor_copy(vec[:, :], bk[:, 0:NROWS]).then_inc(misc.read("vec"), 1)
            bk = misc.filled(dve, "ada_b")
            dve.tensor_copy(ada_b_col[:, :], bk[:, 0:96]).then_inc(misc.read("ada_b"), 1)
            bk = misc.filled(dve, "rowb")
            dve.tensor_copy(rowb[:, :], bk[:, 0:32]).then_inc(misc.read("rowb"), 1)
            misc.was_read(dve, "rowb")
            step(dve.tensor_scalar(neg_sink[:, :], rowb[:, 0:8], -1.0, None, ALU.mult))
            for c in range(NCH):
                for g in range(2):
                    bk = dense.filled(dve, ("x", c, g))
                    dve.tensor_copy(X[:, 4 * g:4 * g + 4, c * P:(c + 1) * P],
                                    bk[:, :].rearrange("p (j t) -> p j t", j=4)).then_inc(dense.read(("x", c, g)), 1)
            b0, b1 = col("hgrn_lower_bounds")[:, 0:8], col("hgrn_lower_bounds")[:, 8:16]
            step(dve.tensor_tensor(lbt[:, 2, :], b0, b1, ALU.max))
            dve.tensor_tensor(lbt[:, 0, :], b0, lbt[:, 2, :], ALU.subtract)
            dve.tensor_tensor(lbt[:, 1, :], b1, lbt[:, 2, :], ALU.subtract).then_inc(S["raw_f"], 1)
            dve.wait_ge(S["lb_exp"], 1)
            step(dve.tensor_tensor(lbt[:, 2, :], lbt[:, 0, :], lbt[:, 1, :], ALU.add))
            step(dve.reciprocal(lbt[:, 2, :], lbt[:, 2, :]))
            step(dve.tensor_tensor(lb[:, :], lbt[:, 0, :], lbt[:, 2, :], ALU.mult))
            step(dve.tensor_scalar(oml[:, :], lb[:, :], -1.0, 1.0, ALU.mult, ALU.add))
            modulation(0, 0, 8)
            norm(0, 0)

            for d, (f, k) in enumerate(((PF, kf), (SI, kb))):
                for h in range(H):
                    j = 4 * d + h
                    dense.was_read(dve, ("in0", 4 + j))
                    step(dve.tensor_scalar(f[:, h, :], f[:, h, :], oml[:, j:j + 1], lb[:, j:j + 1], ALU.mult, ALU.add))
                    step(dve.tensor_scalar(k[:, h, :], f[:, h, :], -1.0, 1.0, ALU.mult, ALU.add))
            dense.was_read(dve, ("in0", 3))
            dve.wait_ge(S["rest_in"], 16)

            lv = cst("levels")
            for i, L in enumerate(LEVELS):
                if i:
                    misc.filled(dve, ("level", i - 1, 2))
                if L == 0:
                    dve.tensor_copy(Qd[:], q[:])
                    dve.tensor_tensor(Kd[:], kf[:], kb[:], ALU.add).then_inc(S["level_ready"], 1)
                else:
                    halves = lambda t: flat(t).rearrange("p (n two l) -> p n two l", two=2, l=L)
                    (qv, fv, sv, kfv, kbv, sfv, pxv, qdv, kdv) = (halves(t) for t in
                                                                 (q, PF, SI, kf, kb, SF, PX, Qd, Kd))
                    A, B = 0, 1
                    mul = lambda o, a, b: dve.tensor_tensor(o, a, b, ALU.mult)
                    mul(qdv[:, :, B, :], qv[:, :, B, :], fv[:, :, B, :])
                    mul(qdv[:, :, A, :], qv[:, :, A, :], sv[:, :, A, :])
                    if L == 1:
                        dve.tensor_copy(kdv[:, :, A, :], kfv[:, :, A, :])
                        dve.tensor_copy(kdv[:, :, B, :], kbv[:, :, B, :]).then_inc(S["level_ready"], 1)
                        dve.tensor_copy(sfv[:, :, A, :], fv[:, :, B, :])
                        dve.memset(sfv[:, :, B, :], 1.0)
                        dve.tensor_copy(pxv[:, :, B, :], sv[:, :, A, :])
                        step(dve.memset(pxv[:, :, A, :], 1.0))
                    else:
                        mul(kdv[:, :, A, :], kfv[:, :, A, :], sfv[:, :, A, :])
                        mul(kdv[:, :, B, :], kbv[:, :, B, :], pxv[:, :, B, :]).then_inc(S["level_ready"], 1)
                        n = 1536 // (2 * L)
                        wide = lambda v: v.to_broadcast([P, n, L])
                        mul(sfv[:, :, A, :], sfv[:, :, A, :], wide(fv[:, :, B, L - 1:L]))
                        step(mul(pxv[:, :, B, :], pxv[:, :, B, :], wide(sv[:, :, A, 0:1])))
                    n = 1536 // (2 * L)
                    wide = lambda v: v.to_broadcast([P, n, L])
                    mul(fv[:, :, B, :], fv[:, :, B, :], wide(fv[:, :, A, L - 1:L]))
                    step(mul(sv[:, :, A, :], sv[:, :, A, :], wide(sv[:, :, B, 0:1])))
                for c in range(NCH):
                    bk = misc.filled(dve, ("level", i, c))
                    b3 = bk[:, :].rearrange("p (h t) -> p h t", h=H)
                    mask = lv[:, i * P:(i + 1) * P].unsqueeze(1).to_broadcast([P, H, P])
                    if i == 0:
                        dve.tensor_tensor(Am[:, c], b3, mask, ALU.mult).then_inc(misc.read(("level", i, c)), 1)
                        misc.was_read(dve, ("level", i, c))
                    else:
                        dve.copy_predicated(Am[:, c], mask.bitcast(I32), b3).then_inc(misc.read(("level", i, c)), 1)
            step(dve.tensor_tensor(SF[:, :, 0:2 * P], SF[:, :, 0:2 * P], kf[:, :, 0:2 * P], ALU.mult))
            dve.tensor_tensor(PX[:, :, 0:P], PX[:, :, 0:P], kb[:, :, 0:P], ALU.mult).then_inc(S["kfin_ready"], 1)
            dve.tensor_tensor(PX[:, :, 2 * P:T], PX[:, :, 2 * P:T], kb[:, :, 2 * P:T], ALU.mult)\
                .then_inc(S["kfin_ready"], 1)
            for o, f in ((Qd, PF), (Kd, SI)):
                dve.tensor_tensor(o[:, :, P:T], q[:, :, P:T], f[:, :, P:T], ALU.mult).then_inc(S["qi_ready"], 1)
            dve.wait_ge(S["qi_ready"], 2)
            modulation(0, 8, 20)
            dve.wait_ge(S["state_in"], 16)
            for d, tot in ((0, lambda h: PF[:, h, 2 * P - 1:2 * P]), (1, lambda h: SI[:, h, 2 * P:2 * P + 1])):
                bk = misc.filled(dve, ("kv", 2 + d))
                for h in range(H):
                    ins = dve.scalar_tensor_tensor(S1[:, d, h, :], S0[:, d, h, :], tot(h), bk[:, h * P:(h + 1) * P],
                                                   ALU.mult, ALU.add)
                ins.then_inc(misc.read(("kv", 2 + d)), 1)
            misc.was_read(dve, ("kv", 3))
            bk = dense.filled(dve, "gates")
            dve.tensor_tensor(G, bk[:, 0:48].rearrange("p (c j) -> p c j", c=NCH),
                              rowb[:, 8:24].unsqueeze(1).to_broadcast([P, NCH, 16]), ALU.add)\
                .then_inc(dense.read("gates"), 1)
            dense.was_read(dve, "gates")
            for c in range(NCH):
                bk = dense.filled(dve, ("hg_o", c))
                dve.tensor_copy(o_hg[:, :, c * P:(c + 1) * P], bk[:, :].rearrange("p (h t) -> p h t", h=H))\
                    .then_inc(dense.read(("hg_o", c)), 1)
                dense.was_read(dve, ("hg_o", c))

            def mixer_out(src, gate, g, n0, base):
                for h in range(H):
                    dve.wait_ge(S["mo_rstd"], n0 + h + 1)
                    dve.tensor_tensor(src[:, h, :], src[:, h, :], rstd[:, h % 2, :], ALU.mult).then_inc(S["mo_t"], 1)
                    dve.wait_ge(S["mo_t"], n0 + h + 1)
                    dve.scalar_tensor_tensor(ht[:, h % 2, :], src[:, h, :], g, gate[:, h, :], ALU.mult, ALU.mult)\
                        .then_inc(S["ht_ready"], 1)
                    dve.wait_ge(S["hhi_ready"], base + h + 1)
                    dve.tensor_tensor(h_lo[:, base - 8 + h, :], ht[:, h % 2, :],
                                      h_hi[:, base - 8 + h, :].bitcast(F32), ALU.subtract).then_inc(S["h_ready"], 1)

            mixer_out(o_hg, ga, col("hgrn_norm_g"), 0, 8)

            G5 = G.rearrange("p c (d k h) -> p c d k h", d=2, k=2)
            dve.engine_nop().then_inc(S["gates_ready"], 1)
            step(dve.tensor_scalar(LF, G5[:, :, :, 1, :], 0.0, None, ALU.min))
            dve.wait_ge(S["gates_abs"], 1)
            dve.tensor_tensor(LF, LF, LE, ALU.subtract).then_inc(S["gates_log"], 1)
            bk = misc.filled(dve, "B")
            B4 = bk[:, 0:24].rearrange("p (c d h) -> p c d h", c=NCH, d=2)
            dve.tensor_copy(GB[:, :, 2:4, :], B4)
            dve.tensor_tensor(GB[:, :, 0:2, :], G5[:, :, :, 0, :], B4, ALU.subtract).then_inc(misc.read("B"), 1)
            for c in range(NCH):
                bk = misc.filled(dve, ("rows", c))
                dve.tensor_copy(rows[:, :, c * P:(c + 1) * P], bk[0:4, :].rearrange("p (k t) -> p k t", k=4))\
                    .then_inc(misc.read(("rows", c)), 1)
                misc.was_read(dve, ("rows", c))
            sh = 1
            while sh < TL:
                f, g = rows[:, 0, :], rows[:, 1, :]
                step(dve.tensor_copy(row_copy, f))
                for lo, hi in ((0, P), (P, T)):
                    if sh < hi - lo:
                        dve.tensor_tensor(f[:, lo + sh:hi], f[:, lo + sh:hi], row_copy[:, lo:hi - sh], ALU.max)
                        last = dve.tensor_tensor(g[:, lo:hi - sh], g[:, lo:hi - sh], g[:, lo + sh:hi], ALU.max)
                step(last)
                sh *= 2
            dve.wait_ge(S["small_in"], 64)
            dve.tensor_scalar(rows[:, 0:2, 0:P], rows[:, 0:2, 0:P], 0.0, None, ALU.max)
            for d in range(2):
                ins = dve.tensor_scalar(rows[:, d, P:T], rows[:, d, P:T], m0_col[:, d:d + 1], None, ALU.max)
            step(ins)
            step(dve.tensor_tensor(rows[:, 2:4, :], rows[:, 2:4, :], rows[:, 0:2, :], ALU.add))
            for d, t in ((0, P - 1), (1, 0)):
                dve.tensor_copy(m_out[:, d:d + 1], rows[:, 2 + d, t:t + 1]).then_inc(S["rows_m"], 1)
            dve.wait_ge(S["s_out"], 16)
            for h in range(H):
                for d in range(2):
                    j = 2 * h + d
                    dense.was_read(dve, ("M", j))
                    dense.was_read(dve, ("qk10", h))
                    if j >= 2:
                        dense.filled(dve, ("den", j - 2))
                    if d == 0:
                        ins = dve.tensor_tensor(Aw[:, j % 2, :], Ew[:, j % 2, :], QK[:, 0:512], ALU.mult)
                    else:
                        dve.tensor_tensor(Aw[:, j % 2, 0:2 * P], Ew[:, j % 2, 0:2 * P], QK[:, 0:2 * P], ALU.mult)
                        ins = dve.tensor_tensor(Aw[:, j % 2, 2 * P:], Ew[:, j % 2, 2 * P:], QK[:, 3 * P:5 * P],
                                                ALU.mult)
                    ins.then_inc(S["A_ready"], 1)
                    bk = misc.filled(dve, ("ss", j))
                    if j:
                        dense.filled(dve, ("den", j - 1))
                    dve.tensor_tensor(qs, qm[:, h, P:T], bk[:, 0:TL], ALU.mult).then_inc(misc.read(("ss", j)), 1)
                    if j >= 2:
                        misc.filled(dve, ("C", j - 2))
                    if j == 0:
                        misc.was_read(dve, "k_tok")
                    at = 127 if d == 0 else 0
                    dve.tensor_scalar(k_in[:, j % 2, :], k_tok[:, h * P:(h + 1) * P], Ew[:, j % 2, at:at + 1], None,
                                      ALU.mult).then_inc(S["k_in_ready"], 1)
                    misc.was_read(dve, ("em", j))
                    dense.was_read(dve, ("den", j))
                    step(dve.tensor_tensor(den, den, em, ALU.max))
                    step(dve.reciprocal(den, den))
                    bk = misc.filled(dve, ("num", j))
                    dst = hm[:, h, :] if d == 0 else hf
                    dve.tensor_tensor(dst, bk[:, 0:T], den, ALU.mult).then_inc(misc.read(("num", j)), 1)
                    misc.was_read(dve, ("num", j))
                    if d == 0:
                        dve.engine_nop().then_inc(S["h_done"], 1)
                    else:
                        dve.tensor_tensor(hm[:, h, :], hm[:, h, :], hf, ALU.add).then_inc(S["h_done"], 1)
            dve.wait_ge(S["h_done"], 8)
            mixer_out(hm, ob, col("mlstm_norm_g"), 4, 12)
            for m in range(DT):
                residual(("out", 0, m), 0, m, 2)
            dense.was_read(dve, ("out", 0, 7))
            norm(1, 16)
            dve.wait_ge(S["s_out"], 16)
            dve.wait_ge(S["m_sent"], 16)
            dve.wait_ge(S["c_sent"], 32)
            ffn(0)
            modulation(1, 0, 8)
            norm(2, 24)

            for k in range(5):
                i = 0 if k < 3 else 1
                dve.wait_ge(S["cq_rstd"], i + 1)
                src = cqf[:, k, :] if i == 0 else ckvf[:, k - 3, :]
                g = col("mla_q_norm_g", k) if i == 0 else col("mla_kv_norm_g", k - 3)
                dve.scalar_tensor_tensor(src, src, g, rstd[:, i, :], ALU.mult, ALU.mult).then_inc(S["cq_t"], 1)
            for k in range(5):
                dve.wait_ge(S["cqhi"], k + 1)
                if k < 3:
                    dve.tensor_tensor(cq_lo[:, k, :], cqf[:, k, :], cq_hi[:, k, :].bitcast(F32), ALU.subtract)\
                        .then_inc(S["cq_ready"], 1)
                else:
                    dve.tensor_tensor(ckv_lo[:, k - 3, 0:T], ckvf[:, k - 3, :], ckv_hi[:, k - 3, 0:T].bitcast(F32),
                                      ALU.subtract).then_inc(S["ckv_ready"], 1)

            def rope(i):
                x = (qc[:, i, P:T] if i < 4 else kT[:, P:T] if i == 4 else kr4[:, P:T] if i == 5
                     else qr[:, i - 6, P:T])
                kind = "swa" if i < 5 else "mla"
                if i == 4:
                    dense.was_read(dve, ("kc",))
                bk = misc.filled(dve, ("rot", i))
                dve.tensor_tensor(rt[:, 0, :], x, cst(kind + "_cos"), ALU.mult)
                dve.tensor_tensor(rt[:, 1, :], bk[:, 0:TL], cst(kind + "_sin"), ALU.mult)\
                    .then_inc(misc.read(("rot", i)), 1)
                misc.was_read(dve, ("rot", i))
                dve.tensor_tensor(x, rt[:, 0, :], rt[:, 1, :], ALU.add).then_inc(S["roped"], 1)
                dve.wait_ge(S["roped"], i + 1)

            for i in range(6):
                rope(i)
            dve.wait_ge(S["cache_ready"], 1)
            bk = misc.filled(dve, ("cache",))
            dve.tensor_tensor(ckv_lo[:, :, T:TK], bk[:, 2 * P:512].rearrange("p (k t) -> p k t", k=2),
                              ckv_hi[:, :, T:TK].bitcast(F32), ALU.subtract).then_inc(misc.read(("cache",)), 1)
            rope(6)
            rope(7)

            for n in range(len(jobs) + 2):
                if n < len(jobs):
                    kind, heads, t, k0, nk = jobs[n]
                    scale = 64 ** -0.5 if kind == "swa" else 96 ** -0.5
                    nh = len(heads)
                    s_ = st[:, n % 2]
                    bk = dense.filled(dve, ("s", n))
                    step(dve.tensor_reduce(s_[:, 0, 0:nh], bk[:, 0:nh * nk].rearrange("p (h k) -> p h k", h=nh), AX.X,
                                           ALU.max))
                    if kind == "swa":
                        hs = slice(heads[0], heads[0] + nh)
                        step(dve.scalar_tensor_tensor(s_[:, 1, 0:nh], s_[:, 0, 0:nh], -scale, neg_sink[:, hs],
                                                      ALU.mult, ALU.min))
                        dve.tensor_tensor(s_[:, 3, 0:nh], rowb[:, hs], s_[:, 1, 0:nh], ALU.add)\
                            .then_inc(S["neg_max"], 1)
                    else:
                        dve.tensor_scalar(s_[:, 1, 0:nh], s_[:, 0, 0:nh], -scale, None, ALU.mult)\
                            .then_inc(S["neg_max"], 1)
                if 1 <= n <= len(jobs):
                    kind, heads, t, k0, nk = jobs[n - 1]
                    nh = len(heads)
                    s_ = st[:, (n - 1) % 2]
                    dense.was_read(dve, ("s", n - 1))
                    if kind == "swa":
                        step(dve.tensor_tensor(s_[:, 2, 0:nh], s_[:, 2, 0:nh], s_[:, 3, 0:nh], ALU.add))
                    step(dve.reciprocal(s_[:, 4, 0:nh], s_[:, 2, 0:nh]))
                    for i in range(nh):
                        p = pr[:, (n - 1) % 2, i * nk:(i + 1) * nk]
                        ins = dve.tensor_scalar(p, p, s_[:, 4, i:i + 1], None, ALU.mult)
                    ins.then_inc(S["p_ready"], 1)
                if n >= 2 and ends[n - 2][1]:
                    tile = job_tile[n - 2]
                    dve.wait_ge(S["pv_hi"], list(dict.fromkeys(job_tile)).index(tile) + 1)
                    bk = pvs.filled(dve, ("pv", tile))
                    dve.tensor_tensor(mix_part(h_lo, tile), mix_bank(bk, tile), mix_part(h_hi, tile).bitcast(F32),
                                      ALU.subtract).then_inc(pvs.read(("pv", tile)), 1)
            modulation(1, 8, 20)
            for m in range(DT):
                residual(("out", 1, m), 1, m, 2)
            dense.was_read(dve, ("out", 1, 7))
            norm(3, 32)
            dve.wait_ge(S["odd_sent"], 64)
            ffn(1)
            dense.was_read(dve, ("down", 1, 7))
            dve.wait_ge(S["rstd_ready"], 5)
            for m in range(DT):
                if m >= 2:
                    misc.filled(dve, ("y", m - 2))
                dve.scalar_tensor_tensor(ht[:, m % 2, :], X[:, m, :], col("final_norm_g", m), rstd[:, 0, :],
                                         ALU.mult, ALU.mult).then_inc(S["y_ready"], 1)


_INS = ["x_prompt", "x_sample", "state_hgrn", "state_mlstm_c", "state_mlstm_n", "state_mlstm_m",
        "cache_swa_k", "cache_swa_v", "cache_mla_ckv", "cache_mla_krope", "c", "c_ctx",
        "w_in_even", "hgrn_lower_bounds", "hgrn_norm_g", "mlstm_gate_bias", "mlstm_norm_g", "w_out_even",
        "w_in_odd", "swa_sink", "mla_q_norm_g", "mla_w_uq", "mla_kv_norm_g", "mla_w_uk", "mla_w_uv", "w_out_odd",
        "ada_w", "ada_b", "norm1_g", "norm2_g", "ffn_w1", "ffn_w3", "ffn_w2", "final_norm_g"]
_OUTS = [(1, TC, D), (1, TL, D), (1, 1, 2, H, P, P), (1, 1, 2, H, P, P), (1, 1, 2, H, P), (1, 1, 2, H),
         (1, 1, TC, 2, 64), (1, 1, TC, 2, 64), (1, 1, TC, 256), (1, 1, TC, 32)]


def kernel(**inputs):
    import concourse.bacc as _bacc
    from concourse.bass_utils import run_bass_kernel_spmd as _run

    nc = _bacc.Bacc("TRN2", target_bir_lowering=False, num_devices=1, dynamic_dma_scratch_size=4096)
    arrays, I, O = {}, {}, []
    for name in _INS + ["shape_constants"]:
        a = np.ascontiguousarray(inputs[name] if name in inputs else shape_constants())
        arrays[f"in_{name}"] = a
        I[name] = nc.dram_tensor(f"in_{name}", a.shape, mybir.dt.from_np(a.dtype), kind="ExternalInput").ap()
    for i, shape in enumerate(_OUTS):
        O.append(nc.dram_tensor(f"out_{i}", shape, F32, kind="ExternalOutput").ap())
    build(nc, I, O)
    r = _run(nc, [arrays], core_ids=[0])
    return tuple(r.results[0][f"out_{i}"] for i in range(len(_OUTS)))
```

```python
from contextlib import ExitStack

import numpy as np
import concourse.bass as bass
from concourse import mybir

F32 = mybir.dt.float32
F32R = mybir.dt.float32r
I32 = mybir.dt.int32
ALU = mybir.AluOpType
ACT = mybir.ActivationFunctionType
AX = mybir.AxisListType

P = 128
D = 1024
DT = D // P
TC = 128
TL = 256
T = TC + TL
NCH = T // P
H = 4
FF = 2816
FT = FF // P
WE = 4624
WO = 1440
EPS = 1e-6
HS = 8
TK = T + P
BIG = 1e30
TURN_LAG, VALUE_LAG = 2, 3
PR = TURN_LAG + 1
LEVELS = [0, 1, 2, 4, 8, 16, 32, 64]

ROWS = {}
_n = 0
for _name, _k in (("c", 8), ("c_ctx", 8), ("norm1_g", 16), ("norm2_g", 16), ("final_norm_g", 8),
                  ("hgrn_lower_bounds", 16), ("hgrn_norm_g", 1), ("mlstm_norm_g", 1),
                  ("mla_q_norm_g", 3), ("mla_kv_norm_g", 2), ("state_mlstm_n", 8)):
    ROWS[_name] = (_n, _k)
    _n += _k
NROWS = _n

CONSTS = {}
_n = 0
for _name, _k in (("ident", 128), ("ones", 128), ("swa_cos", 256), ("swa_sin", 256), ("mla_cos", 256),
                  ("mla_sin", 256), ("swa_turn", 128), ("mla_turn", 128), ("levels", 8 * 128),
                  ("tri_f", 128), ("tri_b", 128), ("big_f", 128), ("big_b", 128), ("band0", 128),
                  ("band1", 128), ("rep", 128)):
    CONSTS[_name] = (_n, _k)
    _n += _k
NCONST = _n


def shape_constants():
    out = np.zeros((P, NCONST), np.float32)

    def put(name, value):
        a, k = CONSTS[name]
        out[:value.shape[0], a:a + k] = value.reshape(value.shape[0], k)

    put("ident", np.eye(P, dtype=np.float32))
    put("ones", np.ones((P, P), np.float32))
    pos = np.arange(TL)
    rows, cols = (pos // 64).astype(np.float32), (pos % 64).astype(np.float32)
    for name, d, n in (("swa", 64, 2), ("mla", 32, 4)):
        ax, half = d // 2, d // 4
        inv = (10000.0 ** (-np.arange(0, ax, 2, dtype=np.float32) / ax)).astype(np.float32)
        cos, sin = np.zeros((d, TL), np.float32), np.zeros((d, TL), np.float32)
        turn = np.zeros((d, d), np.float32)
        for a, at in ((0, rows), (1, cols)):
            ang = (at[None, :] * inv[:, None]).astype(np.float32)
            for s in (0, 1):
                r = a * ax + s * half
                cos[r:r + half], sin[r:r + half] = np.cos(ang), np.sin(ang)
            for i in range(half):
                x1, x2 = a * ax + i, a * ax + half + i
                turn[x2, x1] = -1.0
                turn[x1, x2] = 1.0
        put(name + "_cos", np.tile(cos, (n, 1)))
        put(name + "_sin", np.tile(sin, (n, 1)))
        put(name + "_turn", np.kron(np.eye(n, dtype=np.float32), turn))
    s, t = np.arange(P)[:, None], np.arange(P)[None, :]
    lv = [(s == t)] + [(s // (2 * L) == t // (2 * L)) & (s // L != t // L) for L in LEVELS[1:]]
    put("levels", np.stack(lv, 1).astype(np.float32))
    put("tri_f", (s <= t).astype(np.float32))
    put("tri_b", (s >= t).astype(np.float32))
    put("big_f", np.where(s > t, BIG, 0).astype(np.float32))
    put("big_b", np.where(s < t, BIG, 0).astype(np.float32))
    put("band0", np.where(t > s, -BIG, 0).astype(np.float32))
    put("band1", np.where(t < s, -BIG, 0).astype(np.float32))
    rep = np.zeros((P, P), np.float32)
    rep[96:] = np.tile(np.eye(32, dtype=np.float32), (1, 4))
    put("rep", rep)
    return out


ADA_PLACES = {"start": 4, "norm0": 1, "hgrn_end": 2, "states": 2, "hgrn_norm": 2, "gates": 3, "mlstm": 3,
              "mlstm_norm": 1, "norm1": 1, "norm2": 1, "projections": 1, "attention": 2, "norm3": 1}
assert sum(ADA_PLACES.values()) == 24


def ada_pairs(place):
    at = 0
    for name, n in ADA_PLACES.items():
        if name == place:
            return range(at, at + n)
        at += n
    raise KeyError(place)


def plan_units():
    units = []
    add = lambda name, n, kt, cols, first=0: units.extend((name, first + i, kt, cols) for i in range(n))

    def ada(place):
        units.extend((f"ada{p // 12}", 2 * (p % 12) + i, DT, 256) for p in ada_pairs(place) for i in range(2))

    ada("start")
    ada("norm0")
    add("in0", 18, DT, 256)
    add("gates", 1, DT, 16)
    add("out0", 2, DT, 256)
    for place in ("hgrn_end", "states", "hgrn_norm", "gates", "mlstm", "mlstm_norm"):
        ada(place)
    add("out0", 2, DT, 256, 2)
    add("up0", 2, DT, 256)
    ada("norm1")
    add("up0", FT - 2, DT, 256, 2)
    add("down0", 16, 11, 128)
    add("in1", 2, DT, 256)
    ada("norm2")
    add("in1", 3, DT, 256, 2)
    add("in1", 1, DT, 160, 5)
    add("uq", 2, 3, 384)
    ada("projections")
    add("uk", 2, 2, 256)
    add("uv", 2, 2, 256)
    add("out1", 2, DT, 256)
    ada("attention")
    add("out1", 2, DT, 256, 2)
    add("up1", 2, DT, 256)
    ada("norm3")
    add("up1", FT - 2, DT, 256, 2)
    add("down1", 16, 11, 128)
    return units


def build(nc, I, O):
    units = plan_units()
    RAW, SPLIT = 3, 2
    number = {(n, i): u for u, (n, i, _, _) in enumerate(units)}
    native = [n.startswith("ada") for n, _, _, _ in units]
    split_units = [u for u in range(len(units)) if not native[u]]
    split_index = {u: s for s, u in enumerate(split_units)}
    native_index = {u: s for s, u in enumerate(u for u in range(len(units)) if native[u])}

    ctx = ExitStack()
    with ctx:
        def sb(name, shape, dt=F32):
            return ctx.enter_context(nc.sbuf_tensor(name, shape, dt))

        def sem(name):
            return ctx.enter_context(nc.semaphore(name))

        X = sb("X", [P, DT, T])
        h_hi = sb("h_hi", [P, DT, T], F32R)
        h_lo = sb("h_lo", [P, DT, T], F32R)
        raw = [sb(f"raw{i}", [P, 2048]) for i in range(RAW)]
        w_hi = [sb(f"w_hi{i}", [P, 2048], F32R) for i in range(SPLIT)]
        w_lo = [sb(f"w_lo{i}", [P, 2048], F32R) for i in range(SPLIT)]
        const = sb("const", [P, NCONST])
        vec = sb("vec", [P, NROWS])
        ada_b_col = sb("ada_b_col", [P, 96])
        cond = sb("cond", [P, DT, 2])
        ada_row = sb("ada_row", [2, 2, 512])
        mod = sb("mod", [P, 2, 48, 2])
        gain = sb("gain", [P, 4, DT, 2])
        lb = sb("lb", [P, 8])
        oml = sb("oml", [P, 8])
        lbt = sb("lbt", [P, 3, 8])
        row_in = sb("row_in", [1, 32])
        rowb = sb("rowb", [P, 32])
        m0_col = sb("m0_col", [4, 2])
        sq = sb("sq", [P, 2, T])
        rstd = sb("rstd", [P, 2, T])
        ht = sb("ht", [P, 2, T])
        eps_col = sb("eps_col", [P, 1])
        neg_sink = sb("neg_sink", [P, 8])

        def overlay(tensors):
            with ExitStack() as phase:
                return [phase.enter_context(nc.sbuf_tensor(n, s, dt)) for n, s, dt in tensors]

        xtok, vec_rows, ada_rows = overlay([
            ("xtok", [P, NCH, D], F32), ("vec_rows", [P, P], F32), ("ada_rows", [96, P], F32)])
        HB = [P, H, T]
        (q, PF, SI, kf, kb, SF, PX, Qd, Kd, Am, S0, C0, va, vb, ga, qm, km) = overlay(
            [(n, HB, F32) for n in ("q", "PF", "SI", "kf", "kb", "SF", "PX", "Qd", "Kd")]
            + [("Am", [P, NCH, H, P], F32), ("S0", [P, 2, H, P], F32), ("C0", [P, 2, H, P], F32), ("va", [P, NCH, 512], F32), ("vb", [P, NCH, 512], F32)]
            + [(n, HB, F32) for n in ("ga", "qm", "km")])
        (qc, kT, vt, cqf, ckvf, cq_hi, cq_lo, ckv_hi, ckv_lo, kr4, qn, qr, kn, vm, krr, rt, pr, pT,
         cin_k, cin_c, cin_r, out_k, out_c, out_r, st) = overlay([
            ("qc", [P, 4, T], F32), ("kT", [P, TK], F32), ("vt", [P, 4, P], F32), ("cqf", [P, 3, T], F32),
            ("ckvf", [P, 2, T], F32), ("cq_hi", [P, 3, T], F32R), ("cq_lo", [P, 3, T], F32R),
            ("ckv_hi", [P, 2, TK], F32R), ("ckv_lo", [P, 2, TK], F32R), ("kr4", [P, TK], F32),
            ("qn", [P, 4, T], F32), ("qr", [P, 2, T], F32), ("kn", [P, 4, TK], F32), ("vm", [P, 4, 512], F32),
            ("krr", [P, T], F32), ("rt", [P, 2, TL], F32), ("pr", [P, PR, 512], F32), ("pT", [P, 2, 512], F32),
            ("cin_k", [P, P], F32), ("cin_c", [P, 256], F32), ("cin_r", [P, 4, 32], F32),
            ("out_k", [P, P], F32), ("out_c", [P, 256], F32), ("out_r", [P, 32], F32), ("st", [P, PR, 5, 4], F32)])
        u_hi, u_lo, sa, uf = overlay([
            ("u_hi", [P, FT, T], F32R), ("u_lo", [P, FT, T], F32R), ("sa", [P, 2, T], F32), ("uf", [P, 2, T], F32)])

        def cst(name):
            a, k = CONSTS[name]
            return const[:, a:a + k]

        ident, ones = cst("ident"), cst("ones")

        flat = lambda t: t[:].rearrange("p a b -> p (a b)")
        kt4 = [flat(kf)[:, 0:512], flat(kf)[:, 512:1024], flat(kf)[:, 1024:1536], flat(q)[:, 1024:1536]]
        ob = kb
        S1 = flat(q)[:, 0:1024].rearrange("p (d h v) -> p d h v", d=2, h=H)
        Sout = flat(PX)[:, 0:1024].rearrange("p (d h v) -> p d h v", d=2, h=H)
        o_hg = SF
        hm = PX
        gate_rows = ht[0:16, 0, :]
        row_M, row_B = sq[0:4], rstd[0:4]
        ss_row = flat(PF)[0:4, 0:512].rearrange("p (d t) -> p d t", d=2)
        k_tok = flat(PF)[:, 512:1024]
        k_in = flat(PF)[:, 1024:1280].rearrange("p (b k) -> p b k", b=2)
        G = flat(SI)[:, 0:48].rearrange("p (c j) -> p c j", c=NCH)
        LF = flat(SI)[:, 64:88].rearrange("p (c d h) -> p c d h", c=NCH, d=2)
        LE = flat(SI)[:, 96:120].rearrange("p (c d h) -> p c d h", c=NCH, d=2)
        GB = flat(SI)[:, 128:176].rearrange("p (c k h) -> p c k h", c=NCH, k=4)
        m_out = flat(SI)[0:4, 192:194]
        n_out = flat(SI)[0:1, 512:1536].rearrange("p (d h k) -> p d h k", d=2, h=H)
        QK = flat(kf)[:, 0:1280].rearrange("p (b n) -> p b n", b=2)
        Ew = S0[:].rearrange("p d h v -> p (d h v)").rearrange("p (b n) -> p b n", b=2)
        Aw = flat(Qd)[:, 0:1024].rearrange("p (b n) -> p b n", b=2)
        em = flat(Kd)[:, 0:384]
        qs = [flat(Kd)[:, 384:640], flat(kf)[:, 1280:1536]]
        den = flat(Kd)[:, 640:1024]
        hf = flat(Kd)[:, 1024:1408]
        hg_sq, ml_sq = va[:].rearrange("p c e -> p (c e)").rearrange("p (h t) -> p h t", h=H), Kd
        Cout = Am[:].rearrange("p c h t -> p (c h t)")[:, 0:1024].rearrange("p (d h v) -> p d h v", d=2, h=H)

        bank = [ctx.enter_context(nc.psum_tensor(f"bank{i}", [P, 512], F32)) for i in range(8)]

        class Ring:

            def __init__(self, name, banks):
                self.name, self.banks, self.n, self.at = name, banks, len(banks), {}
                self.done = sem(name + "_filled")
                self.free = [sem(f"{name}{b}_read") for b in banks]

            def fill(self, pe, key):
                m = self.at[key] = len(self.at)
                if m >= self.n:
                    pe.wait_ge(self.free[m % self.n], m // self.n)
                return bank[self.banks[m % self.n]]

            def filled(self, eng, key):
                eng.wait_ge(self.done, self.at[key] + 1)
                return bank[self.banks[self.at[key] % self.n]]

            def read(self, key):
                return self.free[self.at[key] % self.n]

            def was_read(self, eng, key):
                eng.wait_ge(self.read(key), self.at[key] // self.n + 1)

        dense = Ring("dense", [0, 1, 2])
        adas = Ring("ada", [3])
        misc = Ring("misc", [5, 6, 7])
        pvs = Ring("pv", [4])
        STAT = bank[4]
        S = {}

        def signal(*names):
            for n in names:
                S[n] = sem(n)

        signal("raw_in0", "raw_in1", "raw_in2", "hi_ready", "lo_ready", "half_used")
        signal("const_in", "c_in", "rest_in", "rows_in", "adab_in", "small_in", "m0_in", "x_in", "state_in", "c0_in", "cache_in")
        signal("lb_exp")
        signal("sq_ready", "stat_done", "stat_read", "rstd_ready", "ht_ready", "hhi_ready", "h_ready")
        signal("uhi_ready", "u_ready")
        signal("pe_own", "dve_own", "act_own")
        signal("raw_f", "level_ready", "kfin_ready", "qi_ready",
               "s_out")
        signal("gates_log", "gates_ready", "gates_abs", "rows_m", "rows_done", "A_ready", "k_in_ready", "h_done", "m_sent", "c_sent")
        signal("mo_sq", "mo_rstd", "mo_t")
        signal("roped", "cq_sq", "cq_rstd", "cq_t", "cqhi", "cq_ready", "ckv_ready", "cache_ready", "odd_sent",
               "neg_max", "p_ready", "pv_hi")
        signal("y_ready", "y_sent")
        release = {}
        raw_need, seen = [], [0] * RAW
        pieces = {u: (2 if n.startswith("up") else 6 if n == "uq" else 4 if n == "in1" and i < 2 else 1)
                  for u, (n, i, _, _) in enumerate(units)}
        for u in range(len(units)):
            seen[u % RAW] += 16 * pieces[u]
            raw_need.append(seen[u % RAW])
        raw_in = [S["raw_in0"], S["raw_in1"], S["raw_in2"]]
        block = ctx.enter_context(nc.Block())

        def mix_part(h, tile):
            kind, part, j = tile
            base = 0 if kind == "swa" else 4
            return h[:, base + 2 * j:base + 2 * j + 2, 0:P] if part == "ctx" else h[:, base + j, P:T]

        def mix_bank(bk, tile):
            return bk[:, 0:2 * P].rearrange("p (j t) -> p j t", j=2) if tile[1] == "ctx" else bk[:, 0:2 * P]

        marks = {}

        def mark(mm, key):
            marks[key] = len(marks) + 1
            mm.then_inc(S["half_used"], 1)

        jobs, job_tile = [], []
        for kind, base in (("swa", 0), ("mla", 4)):
            for g in range(2):
                jobs.append((kind, [4 * g + i for i in range(4)], 0, 0, P))
                job_tile.append((kind, "ctx", g))
            for j in range(4):
                for h in (2 * j, 2 * j + 1):
                    for t in (1, 2):
                        jobs.append((kind, [h], t, P, T))
                        job_tile.append((kind, "lat", j))
        ends = [(n == 0 or job_tile[n - 1] != job_tile[n], n == len(jobs) - 1 or job_tile[n + 1] != job_tile[n])
                for n in range(len(jobs))]

        def pv_at(n, h):
            kind, heads, t, _, _ = jobs[n]
            return (h - heads[0]) // 2 * P if t == 0 else (t - 1) * P

        at_jobs = [4 * (i + 1) for i in range(len(ada_pairs("attention")))]
        fill_after = {n: [p] for n, p in zip(at_jobs, ada_pairs("attention"))}

        starts = []
        for n, (kind, heads, t, _, _) in enumerate(jobs):
            starts.append({(i, 0) for i in range(2)} if t == 0 else ({(0, 0)} if t == 1 else set()))

        @block.tensor
        def _(pe):
            def raw_unit(u):
                pe.wait_ge(raw_in[u % RAW], raw_need[u])
                return raw[u % RAW][:, 0:2048].rearrange("p (k n) -> p k n", k=DT)

            def weight(u, kt, k, c, n=P):
                at = units[u][3] * k + c
                return w_hi[split_index[u] % SPLIT][:, at:at + n], w_lo[split_index[u] % SPLIT][:, at:at + n]

            def three(out, terms, first=True, last=True):
                for j, (s_hi, s_lo, m_hi, m_lo) in enumerate(terms):
                    pe.matmul(out, s_hi, m_hi, start=first and j == 0, stop=False)
                    pe.matmul(out, s_hi, m_lo, start=False, stop=False)
                    mm = pe.matmul(out, s_lo, m_hi, start=False, stop=last and j == len(terms) - 1)
                return mm

            def unit_ready(u):
                pe.wait_ge(S["lo_ready"], split_index[u] + 1)

            def features(key, u, c, k_tiles=DT, x=(h_hi, h_lo), n=T, ready=None):
                out = dense.fill(pe, key)[:, 0:n]
                unit_ready(u)
                if ready is not None:
                    for k in range(k_tiles):
                        pe.wait_ge(S["h_ready"], ready + k + 1)
                        w1, w2 = weight(u, k_tiles, k, c)
                        mm = three(out, [(w1, w2, x[0][:, k, :], x[1][:, k, :])], k == 0, k == k_tiles - 1)
                else:
                    mm = three(out, [(*weight(u, k_tiles, k, c), x[0][:, k, 0:n], x[1][:, k, 0:n])
                                     for k in range(k_tiles)])
                mm.then_inc(dense.done, 1)
                release[u] = (dense.done, dense.at[key] + 1)

            def tokens(key, u, c, n, chunk, k_tiles=DT, x=(h_hi, h_lo), out=None, more=False, last=True):
                bk = dense.fill(pe, key) if out is None else out[0]
                at = 0 if out is None else out[1]
                unit_ready(u)
                terms = []
                for k in range(k_tiles):
                    w1, w2 = weight(u, k_tiles, k, c, n)
                    s = slice(chunk * P, chunk * P + P)
                    terms.append((x[0][:, k, s], x[1][:, k, s], w1, w2))
                for j, (s_hi, s_lo, m_hi, m_lo) in enumerate(terms):
                    pe.matmul(bk[:, at:at + n], s_hi, m_hi, start=j == 0, stop=False)
                    pe.matmul(bk[:, at:at + n], s_hi, m_lo, start=False, stop=False)
                    mm = pe.matmul(bk[:, at:at + n], s_lo, m_hi, start=False, stop=j == k_tiles - 1)
                if last:
                    mm.then_inc(dense.done, 1)
                    release[u] = (dense.done, dense.at[key] + 1)
                return bk

            def turn(ring, key, parts):
                bk = ring.fill(pe, key)
                for at, src in parts:
                    rows, cols = src.shape
                    tr = pe.transpose(bk[0:cols, at:at + rows], src, const[0:rows, 0:rows])
                tr.then_inc(ring.done, 1)

            def modulation(place, pairs=None):
                for p in (ada_pairs(place) if pairs is None else pairs):
                    out = adas.fill(pe, ("ada", p))
                    for i in range(2):
                        u = number[(f"ada{p // 12}", 2 * (p % 12) + i)]
                        w = raw_unit(u)
                        for k in range(DT):
                            mm = pe.matmul(out[0:2, 256 * i:256 * i + 256], cond[:, k, :], w[:, k, :],
                                           start=i == 0 and k == 0, stop=k == DT - 1, skip_group_check=True)
                        if i == 0:
                            mark(mm, ("ada", p))
                            release[u] = (S["half_used"], marks[("ada", p)])
                    mm.then_inc(adas.done, 1)
                    release[u] = (adas.done, adas.at[("ada", p)] + 1)
                    if p % 2:
                        out = adas.fill(pe, ("mod", p // 2))
                        for j in range(8):
                            tr = pe.transpose(out[:, 2 * j:2 * j + 2],
                                              ada_row[:, j // 4, j % 4 * P:j % 4 * P + P], const[0:2, 0:2])
                        tr.then_inc(adas.done, 1)

            def stat(n):
                pe.wait_ge(S["sq_ready"], n + 1)
                pe.matmul(bank[4][:, 0:T], ones, sq[:, 0, :], start=True, stop=True).then_inc(S["stat_done"], 1)

            def out_projection(l, ready, n):
                for m in range(DT):
                    features(("out", l, m), number[(f"out{l}", m // 2)], m % 2 * P, ready=None if m else ready)
                stat(n)

            def ffn(l, ready, n):
                for f in range(FT):
                    u = number[(f"up{l}", f)]
                    features(("gate", l, f), u, 0, ready=ready if f == 0 else None)
                    features(("up", l, f), u, P)
                for m in range(DT):
                    out = dense.fill(pe, ("down", l, m))[:, 0:T]
                    for half in range(2):
                        u = number[(f"down{l}", 2 * m + half)]
                        unit_ready(u)
                        for k in range(11):
                            f = 11 * half + k
                            if m == 0:
                                pe.wait_ge(S["u_ready"], FT * l + f + 1)
                            mm = three(out, [(*weight(u, 11, k, 0), u_hi[:, f, :], u_lo[:, f, :])],
                                       f == 0, f == FT - 1)
                        if half == 0:
                            mark(mm, ("half", l, m))
                            release[u] = (S["half_used"], marks[("half", l, m)])
                    mm.then_inc(dense.done, 1)
                    release[u] = (dense.done, dense.at[("down", l, m)] + 1)
                stat(n)

            pe.wait_ge(S["const_in"], 16)
            pe.wait_ge(S["c_in"], 32)
            turn(misc, "cond", [(0, vec_rows[0:2 * DT, :])])
            misc.was_read(pe, "cond")
            modulation("start", range(0, 1))
            pe.wait_ge(S["x_in"], 32)
            for c in range(NCH):
                for g in range(2):
                    turn(dense, ("x", c, g), [(j * P, xtok[:, c, (4 * g + j) * P:(4 * g + j + 1) * P])
                                              for j in range(4)])
            pe.wait_ge(S["rows_in"], 16 * (len(ROWS) - 2))
            turn(misc, "vec", [(0, vec_rows[0:NROWS, :])])
            pe.wait_ge(S["adab_in"], 16)
            turn(misc, "ada_b", [(0, ada_rows[:, :])])
            pe.wait_ge(S["small_in"], 48)
            out = misc.fill(pe, "rowb")
            pe.matmul(out[:, 0:32], ones[0:1, :], row_in[:, :], start=True, stop=True).then_inc(misc.done, 1)
            modulation("start", range(1, 2))
            stat(0)
            modulation("start", range(2, 4))
            modulation("norm0")

            in0 = lambda c: (number[("in0", c // 256)], c % 256)
            for j in range(12):
                features(("in0", j), *in0(j * P), ready=0 if j == 0 else None)

            def level(i):
                pe.wait_ge(S["level_ready"], i + 1)
                for c in range(NCH):
                    out = misc.fill(pe, ("level", i, c))
                    for h in range(H):
                        mm = pe.matmul(out[:, h * P:(h + 1) * P], Kd[:, h, c * P:(c + 1) * P],
                                       Qd[:, h, c * P:(c + 1) * P], start=h == 0, stop=h == H - 1,
                                       skip_group_check=True)
                    mm.then_inc(misc.done, 1)

            for j in range(6, 18):
                if j in (6, 7, 14, 15):
                    for c in range(NCH):
                        tokens(("in0v", j, c), number[("in0", j)], 0, 256, c)
                else:
                    features(("in0", 2 * j), number[("in0", j)], 0)
                    features(("in0", 2 * j + 1), number[("in0", j)], P)
                if j < 14:
                    level(j - 6)
            u = number[("gates", 0)]
            out = dense.fill(pe, "gate_rows")
            unit_ready(u)
            mm = three(out[0:16, 0:T], [(*weight(u, DT, k, 0, 16), h_hi[:, k, :], h_lo[:, k, :]) for k in range(DT)])
            mm.then_inc(dense.done, 1)
            release[u] = (dense.done, dense.at["gate_rows"] + 1)

            tri_f, tri_b = cst("tri_f"), cst("tri_b")
            pairs = ada_pairs("hgrn_end")
            dense.was_read(pe, "gate_rows")
            turn(dense, "gates", [(16 * c, gate_rows[:, c * P:(c + 1) * P]) for c in range(NCH)])
            modulation("hgrn_end", pairs[0:1])
            pe.wait_ge(S["gates_log"], 1)
            out = misc.fill(pe, "B")
            for d, tri, order in ((0, tri_f, (0, 1, 2)), (1, tri_b, (0, 2, 1))):
                for i, c in enumerate(order):
                    o = out[:, (c * 2 + d) * 4:(c * 2 + d) * 4 + 4]
                    start = d == 0 and c == 0
                    if i == 2:
                        pe.matmul(o, ones, LF[:, order[1], d, :], start=False, stop=False, skip_group_check=True)
                    mm = pe.matmul(o, tri, LF[:, c, d, :], start=start, stop=True, skip_group_check=True)
            mm.then_inc(misc.done, 1)

            pe.wait_ge(S["kfin_ready"], 2)
            for i, (src, c) in enumerate(((SF, 0), (PX, 0), (SF, 1), (PX, 2))):
                turn(misc, ("kfin", i), [(h * P, src[:, h, c * P:(c + 1) * P]) for h in range(H)])
            modulation("hgrn_end", pairs[1:])
            misc.was_read(pe, "B")
            for c in range(NCH):
                turn(misc, ("rows", c), [(k * P, GB[:, c, k, :]) for k in range(4)])
            for i, c in enumerate((0, 0, 1, 2)):
                misc.was_read(pe, ("kfin", i))
                out = misc.fill(pe, ("kv", i))
                for h in range(H):
                    mm = pe.matmul(out[:, h * P:(h + 1) * P], kt4[i][:, h * P:(h + 1) * P],
                                   va[:, c, h * P:(h + 1) * P], start=h == 0, stop=h == H - 1,
                                   skip_group_check=True)
                mm.then_inc(misc.done, 1)
            modulation("states")
            for c in range(NCH):
                misc.was_read(pe, ("level", len(LEVELS) - 1, c))
            for c in range(NCH):
                if c == 1:
                    misc.was_read(pe, ("kv", 2))
                    misc.was_read(pe, ("kv", 3))
                    pe.wait_ge(S["qi_ready"], 2)
                out = dense.fill(pe, ("hg_o", c))
                for h in range(H):
                    o = out[:, h * P:(h + 1) * P]
                    t = slice(c * P, (c + 1) * P)
                    terms = [(va[:, c, h * P:(h + 1) * P], Am[:, c, h, :])]
                    if c:
                        terms.append(((S0 if c == 1 else S1)[:, 0, h, :], Qd[:, h, t]))
                        terms.append(((S1 if c == 1 else S0)[:, 1, h, :], Kd[:, h, t]))
                    for a, (s, m) in enumerate(terms):
                        mm = pe.matmul(o, s, m, start=h == 0 and a == 0, stop=h == H - 1 and a == len(terms) - 1,
                                       skip_group_check=True)
                mm.then_inc(dense.done, 1)
            turn(misc, "k_tok", [(h * P, km[:, h, 0:P]) for h in range(H)])

            def mix_norm(kind, n0, place, squares):
                pairs = ada_pairs(place)
                for h in range(H):
                    if h % 2 == 0:
                        modulation(place, pairs[h // 2:h // 2 + 1])
                    pe.wait_ge(S["mo_sq"], n0 + h + 1)
                    out = misc.fill(pe, (kind, h))
                    pe.matmul(out[:, 0:T], ones, squares[:, h, :], start=True, stop=True).then_inc(misc.done, 1)

            mix_norm("hg_norm", 0, "hgrn_norm", hg_sq)

            def qk(h):
                bk = dense.fill(pe, ("qk", h))
                blocks = [(0, 0), (1, 1), (1, 2), (2, 2)]
                for i, (s, t) in enumerate(blocks):
                    mm = pe.matmul(bk[:, i * P:(i + 1) * P], km[:, h, s * P:(s + 1) * P], qm[:, h, t * P:(t + 1) * P],
                                   start=i == 0, stop=i == 3, skip_group_check=True)
                mm.then_inc(dense.done, 1)
                bk = dense.fill(pe, ("qk10", h))
                pe.matmul(bk[:, 0:P], km[:, h, 2 * P:3 * P], qm[:, h, P:2 * P], start=True, stop=True)\
                    .then_inc(dense.done, 1)

            def decays(j):
                h, d = j // 2, j % 2
                sel = ident[0:4, h:h + 1].to_broadcast([4, P])
                big = cst("big_f" if d == 0 else "big_b")
                bk = dense.fill(pe, ("M", j))
                M = row_M[:, d, :]
                other, masked = (M[:, 2 * P:T], (0, 1, 3)) if d == 0 else (M[:, P:2 * P], (0, 1, 2))
                pe.matmul(bk[:, 0:T], sel, M, start=True, stop=False, skip_group_check=True)
                pe.matmul(bk[:, T:512], sel, other, start=False, stop=False, skip_group_check=True)
                for i in masked:
                    mm = pe.matmul(bk[:, i * P:(i + 1) * P], ident, big, start=False, stop=i == masked[-1],
                                   skip_group_check=True)
                mm.then_inc(dense.done, 1)
                bk = misc.fill(pe, ("ss", j))
                pe.matmul(bk[:, 0:TL], sel, ss_row[:, d, :], start=True, stop=True).then_inc(misc.done, 1)

            def sums(j):
                h, d = j // 2, j % 2
                sel = ident[0:4, h:h + 1].to_broadcast([4, P])
                pe.wait_ge(S["A_ready"], j + 1)
                misc.was_read(pe, ("ss", j))
                a = Aw[:, j % 2, :]
                for key, lhs, st in ((("den", j), lambda c: ones,
                                      vec[:, ROWS["state_mlstm_n"][0] + 4 * d + h:][:, 0:1].to_broadcast([P, P])),
                                     (("num", j), lambda c: vb[:, c, h * P:(h + 1) * P], C0[:, d, h, :])):
                    bk = misc.fill(pe, key) if key[0] == "num" else dense.fill(pe, key)
                    pe.matmul(bk[:, 0:P], lhs(0), a[:, 0:P], start=True, stop=False, skip_group_check=True)
                    pe.matmul(bk[:, P:T], st, qs[j % 2], start=False, stop=False, skip_group_check=True)
                    if d == 0:
                        pe.matmul(bk[:, P:T], lhs(1), a[:, P:T], start=False, stop=False, skip_group_check=True)
                        mm = pe.matmul(bk[:, 2 * P:T], lhs(2), a[:, T:512], start=False, stop=True,
                                       skip_group_check=True)
                    else:
                        pe.matmul(bk[:, P:2 * P], lhs(1), a[:, P:2 * P], start=False, stop=False,
                                  skip_group_check=True)
                        pe.matmul(bk[:, 2 * P:T], lhs(2), a[:, 2 * P:T], start=False, stop=False,
                                  skip_group_check=True)
                        mm = pe.matmul(bk[:, P:2 * P], lhs(2), a[:, T:512], start=False, stop=True,
                                       skip_group_check=True)
                    mm.then_inc(misc.done if key[0] == "num" else dense.done, 1)
                    if key[0] == "den":
                        bk = misc.fill(pe, ("em", j))
                        pe.matmul(bk[:, 0:T], sel, row_B[:, d, :], start=True, stop=True).then_inc(misc.done, 1)
                pe.wait_ge(S["k_in_ready"], j + 1)
                bk = misc.fill(pe, ("C", j))
                pe.matmul(bk[:, 0:P], k_in[:, j % 2, :], vb[:, 0, h * P:(h + 1) * P], start=True, stop=True,
                          skip_group_check=True)
                at = 127 if d == 0 else 0
                pe.matmul(bk[0:1, P:2 * P], Ew[:, j % 2, at:at + 1], k_tok[:, h * P:(h + 1) * P],
                          start=False, stop=True, skip_group_check=True).then_inc(misc.done, 1)

            qk(0)
            modulation("gates")
            pe.wait_ge(S["rows_done"], 2)
            pe.wait_ge(S["c0_in"], 16)
            decays(0)
            for j in range(2 * H):
                if j % 2 and j < 2 * H - 1:
                    qk(j // 2 + 1)
                if j < 2 * H - 1:
                    decays(j + 1)
                sums(j)
                if j % 2:
                    modulation("mlstm", ada_pairs("mlstm")[j // 2:j // 2 + 1])
            mix_norm("ml_norm", 4, "mlstm_norm", ml_sq)
            out_projection(0, 8, 1)
            modulation("norm1")
            ffn(0, 16, 2)

            modulation("norm2")
            in1 = lambda i: number[("in1", i)]
            for j in range(4):
                features(("qc", j), in1(j // 2), j % 2 * P, ready=24 if j == 0 else None)
            features(("kc",), in1(2), 0)
            bk = None
            for c in range(NCH):
                bk = tokens(("vc",), in1(2), P, P, c, out=None if c == 0 else (bk, P * c), last=c == 2)
            turn_s, turn_m = cst("swa_turn"), cst("mla_turn")

            def rotate(key, matrix, src):
                out = misc.fill(pe, key)
                pe.matmul(out[:, 0:TL], matrix, src, start=True, stop=True).then_inc(misc.done, 1)

            for j in range(3):
                features(("cq", j), in1(3 + j // 2), j % 2 * P)
                dense.was_read(pe, ("qc", j))
                rotate(("rot", j), turn_s, qc[:, j, P:T])
            features(("ckv", 0), in1(4), P)
            dense.was_read(pe, ("qc", 3))
            rotate(("rot", 3), turn_s, qc[:, 3, P:T])
            features(("ckv", 1), in1(5), 0)
            dense.was_read(pe, ("kc",))
            rotate(("rot", 4), turn_s, kT[:, P:T])
            features(("kr",), in1(5), 32)

            def norm_of(key, k_tiles, n0):
                out = misc.fill(pe, key)
                for k in range(k_tiles):
                    pe.wait_ge(S["cq_sq"], n0 + k + 1)
                    mm = pe.matmul(out[:, 0:T], ones, sq[:, k % 2, :], start=k == 0, stop=k == k_tiles - 1)
                    if k < k_tiles - 1:
                        mark(mm, (key, k))
                mm.then_inc(misc.done, 1)

            norm_of("cq_norm", 3, 0)
            norm_of("ckv_norm", 2, 3)
            modulation("projections")
            dense.was_read(pe, ("kr",))
            out = misc.fill(pe, ("rep",))
            pe.matmul(out[:, 0:T], cst("rep")[96:128, :], krr[96:128, :], start=True, stop=True).then_inc(misc.done, 1)
            misc.was_read(pe, ("rep",))
            rotate(("rot", 5), turn_m, kr4[:, P:T])
            pe.wait_ge(S["cache_in"], 16 * 7)
            turn(misc, ("cache",), [(0, cin_k[:]), (P, cin_r[:].rearrange("p a b -> p (a b)")),
                                    (2 * P, cin_c[:, 0:P]), (3 * P, cin_c[:, P:2 * P])])
            pe.wait_ge(S["cq_ready"], 3)
            for i in range(2):
                u = number[("uq", i)]
                for j in range(2):
                    features(("qn", 2 * i + j), u, j * P, 3, (cq_hi, cq_lo))
                features(("qr", i), u, 2 * P, 3, (cq_hi, cq_lo))
            for i in range(2):
                dense.was_read(pe, ("qr", i))
                rotate(("rot", 6 + i), turn_m, qr[:, i, P:T])
            pe.wait_ge(S["ckv_ready"], 2)
            misc.was_read(pe, ("cache",))
            for j in range(4):
                features(("kn", j), number[("uk", j // 2)], j % 2 * P, 2, (ckv_hi, ckv_lo), n=TK)
            for c in range(4):
                for i in range(2):
                    if i == 0:
                        bk = tokens(("vm", c), number[("uv", 0)], 0, 256, c, 2, (ckv_hi, ckv_lo), last=False)
                    else:
                        tokens(("vm", c), number[("uv", 1)], 0, 256, c, 2, (ckv_hi, ckv_lo), out=(bk, 256))
            release[number[("uv", 0)]] = release[number[("uv", 1)]]
            pe.wait_ge(S["cq_t"], 5)
            turn(misc, ("ctx_cache",), [(0, kT[:, 0:P]), (P, ckvf[:, 0, 0:P]), (2 * P, ckvf[:, 1, 0:P]),
                                        (3 * P, kr4[0:32, 0:P])])

            band = {1: cst("band0"), 2: cst("band1")}

            def scores(n, job):
                kind, heads, t, k0, nk = job
                if n == 0:
                    pe.wait_ge(S["roped"], 8)
                    dense.was_read(pe, ("vm", 3))
                    misc.was_read(pe, ("cache",))
                bk = dense.fill(pe, ("s", n))
                for i, h in enumerate(heads):
                    o = bk[:, i * nk:(i + 1) * nk]
                    tq = slice(t * P, (t + 1) * P)
                    if kind == "swa":
                        b = h // 4 * 64
                        mm = pe.matmul(o, qc[b:b + 64, h % 4, tq], kT[b:b + 64, k0:k0 + nk],
                                       start=i == 0, stop=t == 0, skip_group_check=True)
                        if t:
                            at = P if t == 1 else 0
                            mm = pe.matmul(bk[:, at:at + P], ident, band[t], start=False, stop=True,
                                           skip_group_check=True)
                    else:
                        b, r = h % 2 * 64, h % 4 * 32
                        if i:
                            pe_own[0] += 1
                            mm.then_inc(S["pe_own"], 1)
                            pe.wait_ge(S["pe_own"], pe_own[0])
                        pe.matmul(o, qn[b:b + 64, h // 2, tq], kn[b:b + 64, h // 2, k0:k0 + nk],
                                  start=i == 0, stop=False, skip_group_check=True)
                        mm = pe.matmul(o, qr[r:r + 32, h // 4, tq], kr4[r:r + 32, k0:k0 + nk],
                                       start=False, stop=True, skip_group_check=True,
                                       tile_position=(r, 0))
                mm.then_inc(dense.done, 1)

            def turned(n, job):
                kind, heads, t, k0, nk = job
                pe.wait_ge(S["p_ready"], n + 1)
                w = len(heads) * nk
                turn(misc, ("pT", n), [(i * P, pr[:, n % PR, i * P:(i + 1) * P]) for i in range(w // P)])

            def values(n, job):
                kind, heads, t, k0, nk = job
                misc.was_read(pe, ("pT", n))
                first, last = ends[n]
                if first:
                    pv_bank[0] = pvs.fill(pe, ("pv", job_tile[n]))
                for i, h in enumerate(heads):
                    b = h % 2 * 64
                    at = pv_at(n, h)
                    for k in range(nk // P):
                        chunk = k0 // P + k
                        v = (vt[:, chunk, h // 4 * 64:h // 4 * 64 + 64] if kind == "swa"
                             else vm[:, chunk, h * 64:h * 64 + 64])
                        mm = pe.matmul(pv_bank[0][b:b + 64, at:at + P], v,
                                       pT[:, n % 2, (i * nk + k * P):(i * nk + (k + 1) * P)],
                                       start=k == 0 and (i, at) in starts[n], stop=k == nk // P - 1,
                                       skip_group_check=True)
                if last:
                    mm.then_inc(pvs.done, 1)
                else:
                    mark(mm, ("pv", n))

            pv_bank = [None]
            pe_own = [0]
            for n in range(len(jobs) + VALUE_LAG):
                if n < len(jobs):
                    scores(n, jobs[n])
                if 0 <= n - TURN_LAG < len(jobs):
                    turned(n - TURN_LAG, jobs[n - TURN_LAG])
                if n >= VALUE_LAG:
                    values(n - VALUE_LAG, jobs[n - VALUE_LAG])
                if n in fill_after:
                    modulation("attention", fill_after[n])
            for tile in dict.fromkeys(job_tile):
                pvs.was_read(pe, ("pv", tile))
            out_projection(1, None, 3)
            modulation("norm3")
            ffn(1, 32, 4)
            for m in range(DT):
                pe.wait_ge(S["y_ready"], m + 1)
                turn(misc, ("y", m), [(c * P, ht[:, m % 2, c * P:(c + 1) * P]) for c in range(NCH)])

        @block.sync
        def _(sp):
            w = {"in0": I["w_in_even"][0], "in1": I["w_in_odd"][0], "out0": I["w_out_even"][0],
                 "out1": I["w_out_odd"][0], "uk": I["mla_w_uk"][0], "uv": I["mla_w_uv"][0],
                 "ada0": I["ada_w"][0], "ada1": I["ada_w"][1]}
            k_first = lambda a: a.rearrange("(k p) n -> p k n", p=P)
            sp.dma_start(const[:, 0:256], I["shape_constants"][:, 0:256]).then_inc(S["const_in"], 16)
            sp.wait_ge(S["c_in"], 32)
            for u, (name, i, kt, cols) in enumerate(units):
                if u == 2:
                    sp.dma_start(xtok[:, 0, :], I["x_prompt"][0]).then_inc(S["x_in"], 16)
                    sp.dma_start(xtok[:, 1:3, :], I["x_sample"][0].rearrange("(c p) d -> p c d", p=P))\
                        .then_inc(S["x_in"], 16)
                if u >= RAW:
                    last = u - RAW
                    if native[last]:
                        sp.wait_ge(*release[last])
                    else:
                        sp.wait_ge(S["lo_ready"], split_index[last] + 1)
                dst = raw[u % RAW][:, 0:kt * cols].rearrange("p (k n) -> p k n", k=kt)
                if name[:2] == "up":
                    l = int(name[2])
                    pieces_of = [(dst[:, :, 0:P], k_first(I["ffn_w1"][l])[:, :, i * P:(i + 1) * P]),
                                 (dst[:, :, P:2 * P], k_first(I["ffn_w3"][l])[:, :, i * P:(i + 1) * P])]
                elif name[:4] == "down":
                    rows = slice(i % 2 * 11 * P, (i % 2 + 1) * 11 * P)
                    pieces_of = [(dst, k_first(I["ffn_w2"][int(name[4])][rows, i // 2 * P:(i // 2 + 1) * P]))]
                elif name == "gates":
                    pieces_of = [(dst, k_first(I["w_in_even"][0])[:, :, WE - 16:WE])]
                elif name == "in1" and i < 2:
                    src = k_first(w["in1"])[:, :, 0:512].rearrange("p k (g j e) -> p k g j e", g=2, j=4)
                    to = dst.rearrange("p k (j g e) -> p k g j e", j=2, g=2)
                    pieces_of = [(to[:, :, g, j], src[:, :, g, 2 * i + j]) for g in range(2) for j in range(2)]
                elif name == "uq":
                    src = k_first(I["mla_w_uq"][0])[:, :, i * 384:(i + 1) * 384].rearrange("p k (h e) -> p k h e", h=4)
                    heads = lambda a: a.rearrange("p (h e) -> p h e", h=4)
                    pieces_of = [(heads(dst[:, k, 0:256]), src[:, k, :, 0:64]) for k in range(3)]
                    pieces_of += [(heads(dst[:, k, 256:384]), src[:, k, :, 64:96]) for k in range(3)]
                else:
                    pieces_of = [(dst, k_first(w[name])[:, :, i * 256:i * 256 + cols])]
                assert len(pieces_of) == pieces[u]
                for to, src in pieces_of:
                    if name == "uq" or (name == "in1" and i < 2):
                        with nc.allow_non_contiguous_dma(reason="short runs of heads"):
                            sp.dma_start(to, src).then_inc(raw_in[u % RAW], 16)
                    else:
                        sp.dma_start(to, src).then_inc(raw_in[u % RAW], 16)

        @block.gpsimd
        def _(pool):
            for s, u in enumerate(split_units):
                n = units[u][2] * units[u][3]
                pool.wait_ge(S["hi_ready"], s + 1)
                pool.tensor_tensor(w_lo[s % SPLIT][:, 0:n], raw[u % RAW][:, 0:n],
                                   w_hi[s % SPLIT][:, 0:n].bitcast(F32), ALU.subtract).then_inc(S["lo_ready"], 1)

        @block.scalar
        def _(act):
            own = [0]
            split_at = [0]

            def step(ins):
                own[0] += 1
                ins.then_inc(S["act_own"], 1)
                act.wait_ge(S["act_own"], own[0])

            def split_to(end):
                while split_at[0] < min(end, len(split_units)):
                    s = split_at[0]
                    u = split_units[s]
                    n = units[u][2] * units[u][3]
                    act.wait_ge(raw_in[u % RAW], raw_need[u])
                    if s >= SPLIT:
                        act.wait_ge(*release[split_units[s - SPLIT]])
                    act.activation(w_hi[s % SPLIT][:, 0:n], raw[u % RAW][:, 0:n], ACT.Copy)\
                        .then_inc(S["hi_ready"], 1)
                    split_at[0] += 1

            def ahead(name, i, last=None):
                s = split_index[number[(name, i)]]
                split_to(min(s + SPLIT, last if last is not None else s + SPLIT))

            def end_of(name, n):
                return split_index[number[(name, n - 1)]] + 1

            def evacuate(ring, key, dst, src, func=ACT.Copy, **kw):
                bk = ring.filled(act, key)
                act.activation(dst, src(bk), func, **kw).then_inc(ring.read(key), 1)

            def square(src, i):
                act.activation(sq[:, i % 2, :], src, ACT.Square).then_inc(S["cq_sq"], 1)

            def norm(n, base, high=True):
                act.wait_ge(S["stat_done"], n + 1)
                act.activation(rstd[:, 0, :], bank[4][:, 0:T], ACT.Ln, bias=eps_col[:, :], scale=1.0 / D)\
                    .then_inc(S["stat_read"], 1)
                act.wait_ge(S["stat_read"], n + 1)
                act.activation(rstd[:, 0, :], rstd[:, 0, :], ACT.Exp, scale=-0.5).then_inc(S["rstd_ready"], 1)
                if n == 0:
                    split_to(SPLIT)
                if high:
                    l, k = n // 2, 3 * (n % 2)
                    for m in range(DT):
                        act.wait_ge(S["ht_ready"], base + m + 1)
                        for c, a, b in ((1, 0, TC), (0, TC, T)):
                            ins = act.activation(h_hi[:, m, a:b], ht[:, m % 2, a:b], ACT.Identity,
                                                 bias=mod[:, l, 8 * k + m, c:c + 1])
                        ins.then_inc(S["hhi_ready"], 1)

            def out_projection(l, n):
                for m in range(DT):
                    ahead(f"out{l}", m // 2, end_of(f"up{l}", FT))
                split_to(split_index[number[(f"up{l}", 0)]] + SPLIT)

            def ffn(l, n):
                end = end_of(f"up{l}", FT)
                for f in range(FT):
                    ahead(f"up{l}", f)
                    bk = dense.filled(act, ("gate", l, f))
                    if f >= 2:
                        dense.was_read(act, ("up", l, f - 2))
                    act.activation(sa[:, f % 2, :], bk[:, 0:T], ACT.Silu).then_inc(dense.read(("gate", l, f)), 1)
                    dense.was_read(act, ("up", l, f))
                    act.activation(u_hi[:, f, :], uf[:, f % 2, :], ACT.Copy).then_inc(S["uhi_ready"], 1)
                for m in range(DT):
                    split_to(split_index[number[(f"down{l}", 2 * m + 1)]] + SPLIT)

            def load_rows(name):
                at, k = ROWS[name]
                a = I[name]
                src = {1: lambda: a.rearrange("(r e) -> r e", e=P),
                       2: lambda: a.rearrange("n (r e) -> (n r) e", e=P),
                       3: lambda: a.rearrange("n d (r e) -> (n d r) e", e=P),
                       5: lambda: a.rearrange("b n d h e -> (b n d h) e")}[len(a.shape)]()
                act.dma_start(vec_rows[at:at + k, :], src)\
                    .then_inc(S["c_in" if name in ("c", "c_ctx") else "rows_in"], 16)

            load_rows("c")
            load_rows("c_ctx")
            bk = misc.filled(act, "cond")
            act.activation(cond[:, :, :], bk[:, 0:2 * DT].rearrange("p (c k) -> p k c", c=2), ACT.Silu)\
                .then_inc(misc.read("cond"), 1)
            for name in list(ROWS)[2:]:
                load_rows(name)
            act.dma_start(ada_rows[:, :], I["ada_b"].rearrange("l (r e) -> (l r) e", e=P)).then_inc(S["adab_in"], 16)
            act.dma_start(row_in[:, 0:8], I["swa_sink"]).then_inc(S["small_in"], 16)
            act.dma_start(row_in[:, 8:24], I["mlstm_gate_bias"].rearrange("n k h -> n (k h)"))\
                .then_inc(S["small_in"], 16)
            act.dma_start(row_in[:, 24:32], I["state_mlstm_m"].rearrange("b n d h -> (b n) (d h)"))\
                .then_inc(S["small_in"], 16)

            for c in range(NCH):
                for g in range(2):
                    dense.was_read(act, ("x", c, g))
            act.wait_ge(S["raw_f"], 1)
            act.activation(lbt[:, 0:2, :], lbt[:, 0:2, :], ACT.Exp).then_inc(S["lb_exp"], 1)
            norm(0, 0)

            act.dma_start(const[:, 256:NCONST], I["shape_constants"][:, 256:NCONST]).then_inc(S["rest_in"], 16)
            act.dma_start(S0[:], I["state_hgrn"].rearrange("b n d h k v -> k (b n d) h v")).then_inc(S["state_in"], 16)
            act.dma_start(C0[:], I["state_mlstm_c"].rearrange("b n d h k v -> k (b n d) h v"))\
                .then_inc(S["c0_in"], 16)
            with nc.allow_non_contiguous_dma(reason="eight values"):
                act.dma_start(m0_col[:, :], I["state_mlstm_m"].rearrange("b n d h -> h (b n d)"))\
                    .then_inc(S["m0_in"], 16)

            end = end_of("gates", 1)
            for j in range(12):
                ahead("in0", j // 2, end)
                bk = dense.filled(act, ("in0", j))
                h = j % 4
                dst, f = ((q, ACT.Silu), (PF, ACT.Sigmoid), (SI, ACT.Sigmoid))[j // 4]
                act.activation(dst[:, h, :], bk[:, 0:T], f).then_inc(dense.read(("in0", j)), 1)
            for j in range(6, 18):
                ahead("in0", j, end)
                if j == 16:
                    act.wait_ge(S["kfin_ready"], 2)
                if j in (6, 7, 14, 15):
                    dst = va if j < 8 else vb
                    for c in range(NCH):
                        evacuate(dense, ("in0v", j, c), dst[:, c, j % 2 * 256:j % 2 * 256 + 256], lambda b: b[:, 0:256])
                else:
                    for i in (2 * j, 2 * j + 1):
                        dst, f, sc = {4: (ga, ACT.Silu, 1.0), 5: (qm, ACT.Copy, P ** -0.5), 6: (km, ACT.Copy, 1.0),
                                      8: (ob, ACT.Sigmoid, 1.0)}[i // 4]
                        evacuate(dense, ("in0", i), dst[:, i % 4, :], lambda b: b[:, 0:T], f, scale=sc)

            evacuate(dense, "gate_rows", gate_rows, lambda b: b[0:16, 0:T])
            split_to(split_index[number[("out0", 0)]] + SPLIT)
            G5 = G.rearrange("p c (d k h) -> p c d k h", d=2, k=2)
            act.wait_ge(S["gates_ready"], 1)
            step(act.activation(LE, G5[:, :, :, 1, :], ACT.Abs))
            step(act.activation(LE, LE, ACT.Exp, scale=-1.0))
            act.activation(LE, LE, ACT.Ln, bias=1.0).then_inc(S["gates_abs"], 1)

            act.wait_ge(S["qi_ready"], 2)
            for i in range(4):
                evacuate(misc, ("kfin", i), kt4[i], lambda b: b[:, :])
            for i in range(2):
                bk = misc.filled(act, ("kv", i))
                act.activation(Sout[:, i, :, :], bk[:, :].rearrange("p (h v) -> p h v", h=H), ACT.Copy)\
                    .then_inc(misc.read(("kv", i)), 1)
            misc.was_read(act, ("kv", 1))
            act.dma_start(O[2].rearrange("b n d h k v -> k (b n d) h v"), Sout).then_inc(S["s_out"], 16)

            def head_rms(kind, src, squares):
                for h in range(H):
                    act.activation(squares[:, h, :], src[:, h, :], ACT.Square).then_inc(S["mo_sq"], 1)
                for h in range(H):
                    bk = misc.filled(act, (kind, h))
                    act.activation(squares[:, h, :], bk[:, 0:T], ACT.Ln, bias=eps_col[:, :], scale=1.0 / P)\
                        .then_inc(misc.read((kind, h)), 1)
                for h in range(H):
                    misc.was_read(act, (kind, h))
                    act.activation(squares[:, h, :], squares[:, h, :], ACT.Exp, scale=-0.5)\
                        .then_inc(S["mo_rstd"], 1)

            def head_high(h, base):
                act.wait_ge(S["ht_ready"], base + h + 1)
                act.activation(h_hi[:, base - 8 + h, :], ht[:, h % 2, :], ACT.Copy).then_inc(S["hhi_ready"], 1)

            evacuate(misc, "k_tok", k_tok, lambda b: b[:, :])
            for c in range(NCH):
                dense.was_read(act, ("hg_o", c))
            head_rms("hg_norm", o_hg, hg_sq)
            act.wait_ge(S["rows_m"], 2)
            with nc.allow_non_contiguous_dma(reason="eight values"):
                act.dma_start(O[5].rearrange("b n d h -> h (b n d)"), m_out).then_inc(S["m_sent"], 16)
            step(act.activation(row_B, row_B, ACT.Exp, scale=-1.0))
            for d in range(2):
                act.activation(ss_row[:, d, :], row_M[:, d, P:T], ACT.Exp, scale=-1.0, bias=m0_col[:, d:d + 1])\
                    .then_inc(S["rows_done"], 1)

            def take_qk(h):
                if h >= 2:
                    act.wait_ge(S["A_ready"], 2 * (h - 1))
                evacuate(dense, ("qk", h), QK[:, h % 2, 0:512], lambda b: b[:, :])
                evacuate(dense, ("qk10", h), QK[:, h % 2, 512:640], lambda b: b[:, 0:P])

            def decays(j):
                h, d = j // 2, j % 2
                bk = dense.filled(act, ("M", j))
                if j >= 2:
                    act.wait_ge(S["k_in_ready"], j - 1)
                    misc.filled(act, ("C", j - 2))
                cuts = (0, P, T, 512) if d == 0 else (0, P, 2 * P, 512)
                for c in range(NCH):
                    e = act.activation(Ew[:, j % 2, cuts[c]:cuts[c + 1]], bk[:, cuts[c]:cuts[c + 1]], ACT.Exp,
                                       scale=-1.0, bias=GB[:, c, d, h:h + 1])
                e.then_inc(dense.read(("M", j)), 1)

            take_qk(0)
            decays(0)
            for j in range(2 * H):
                h, d = j // 2, j % 2
                if j % 2 and j < 2 * H - 1:
                    take_qk(h + 1)
                if j < 2 * H - 1:
                    decays(j + 1)
                if j:
                    act.wait_ge(S["h_done"], j)
                evacuate(dense, ("den", j), den, lambda b: b[:, 0:T], ACT.Abs)
                evacuate(misc, ("em", j), em, lambda b: b[:, 0:T])
                bk = misc.filled(act, ("C", j))
                act.activation(Cout[:, d, h, :], bk[:, 0:P], ACT.Copy)
                act.activation(n_out[:, d, h, :], bk[0:1, P:2 * P], ACT.Copy).then_inc(misc.read(("C", j)), 1)
                if d:
                    head_high(h, 8)
            misc.was_read(act, ("C", 7))
            act.dma_start(O[3].rearrange("b n d h k v -> k (b n d) h v"), Cout).then_inc(S["c_sent"], 16)
            act.dma_start(O[4].rearrange("b n d h k -> (b n) d h k"), n_out).then_inc(S["c_sent"], 16)
            act.wait_ge(S["h_done"], 8)
            head_rms("ml_norm", hm, ml_sq)
            for h in range(H):
                head_high(h, 12)
            out_projection(0, 1)
            norm(1, 16)
            act.wait_ge(S["s_out"], 16)
            act.wait_ge(S["m_sent"], 16)
            act.wait_ge(S["c_sent"], 32)
            ffn(0, 2)

            cache = [(cin_k[:], I["cache_swa_k"].rearrange("b n t h e -> (b n t) (h e)")),
                     (vt[:, 3, :], I["cache_swa_v"].rearrange("b n t h e -> (b n t) (h e)")),
                     (cin_c[:], I["cache_mla_ckv"].rearrange("b n t e -> (b n t) e"))]
            cache += [(cin_r[:, i, :], I["cache_mla_krope"].rearrange("b n t e -> (b n t) e")) for i in range(4)]
            for dst, src in cache:
                act.dma_start(dst, src).then_inc(S["cache_in"], 16)
            norm(2, 24)
            end = end_of("uv", 2)
            for j in range(4):
                ahead("in1", j // 2, end)
                evacuate(dense, ("qc", j), qc[:, j, :], lambda b: b[:, 0:T])
            ahead("in1", 2, end)
            evacuate(dense, ("kc",), kT[:, 0:T], lambda b: b[:, 0:T])
            evacuate(dense, ("vc",), vt[:, 0:3, :], lambda b: b[:, 0:T].rearrange("p (c e) -> p c e", c=3))
            for j in range(3):
                ahead("in1", 3 + j // 2, end)
                evacuate(dense, ("cq", j), cqf[:, j, :], lambda b: b[:, 0:T])
            evacuate(dense, ("ckv", 0), ckvf[:, 0, :], lambda b: b[:, 0:T])
            ahead("in1", 5, end)
            evacuate(dense, ("ckv", 1), ckvf[:, 1, :], lambda b: b[:, 0:T])
            evacuate(dense, ("kr",), krr[96:128, :], lambda b: b[96:128, 0:T])
            low_rank = (("cq_norm", cqf, 3), ("ckv_norm", ckvf, 2))
            for i, (key, src, k_tiles) in enumerate(low_rank):
                for k in range(k_tiles):
                    if k == 2:
                        act.wait_ge(S["half_used"], marks[(key, 0)])
                    dense.was_read(act, (("cq", "ckv")[i], k))
                    if i == 1 and k == 0:
                        misc.filled(act, "cq_norm")
                    square(src[:, k, :], k)
            for i, (key, src, k_tiles) in enumerate(low_rank):
                bk = misc.filled(act, key)
                act.activation(rstd[:, i, :], bk[:, 0:T], ACT.Ln, bias=eps_col[:, :], scale=1.0 / (k_tiles * P))\
                    .then_inc(misc.read(key), 1)
            for i, (key, src, k_tiles) in enumerate(low_rank):
                misc.was_read(act, key)
                act.activation(rstd[:, i, :], rstd[:, i, :], ACT.Exp, scale=-0.5).then_inc(S["cq_rstd"], 1)
            evacuate(misc, ("rep",), kr4[:, 0:T], lambda b: b[:, 0:T])
            for k in range(5):
                act.wait_ge(S["cq_t"], k + 1)
                dst, src = (cq_hi[:, k, :], cqf[:, k, :]) if k < 3 else (ckv_hi[:, k - 3, 0:T], ckvf[:, k - 3, :])
                act.activation(dst, src, ACT.Copy).then_inc(S["cqhi"], 1)
            bk = misc.filled(act, ("cache",))
            act.activation(kT[:, T:TK], bk[:, 0:P], ACT.Copy)
            act.activation(kr4[:, T:TK], bk[:, P:2 * P], ACT.Copy)
            act.activation(ckv_hi[:, :, T:TK], bk[:, 2 * P:512].rearrange("p (k t) -> p k t", k=2), ACT.Copy)\
                .then_inc(S["cache_ready"], 1)
            for i in range(2):
                ahead("uq", i, end)
                for j in range(2):
                    evacuate(dense, ("qn", 2 * i + j), qn[:, 2 * i + j, :], lambda b: b[:, 0:T])
                evacuate(dense, ("qr", i), qr[:, i, :], lambda b: b[:, 0:T])
            for j in range(4):
                ahead("uk", j // 2, end)
                evacuate(dense, ("kn", j), kn[:, j, :], lambda b: b[:, :])
            split_to(end)
            for c in range(4):
                evacuate(dense, ("vm", c), vm[:, c, :], lambda b: b[:, :])
            bk = misc.filled(act, ("ctx_cache",))
            act.activation(out_k[:], bk[:, 0:P], ACT.Copy)
            act.activation(out_c[:], bk[:, P:3 * P], ACT.Copy)
            act.activation(out_r[:], bk[:, 3 * P:3 * P + 32], ACT.Copy).then_inc(misc.read(("ctx_cache",)), 1)
            misc.was_read(act, ("ctx_cache",))
            act.dma_start(O[6].rearrange("b n t h e -> (b n t) (h e)"), out_k[:]).then_inc(S["odd_sent"], 16)
            act.dma_start(O[7].rearrange("b n t h e -> (b n t) (h e)"), vt[:, 0, :]).then_inc(S["odd_sent"], 16)
            act.dma_start(O[8].rearrange("b n t e -> (b n t) e"), out_c[:]).then_inc(S["odd_sent"], 16)
            act.dma_start(O[9].rearrange("b n t e -> (b n t) e"), out_r[:]).then_inc(S["odd_sent"], 16)

            for n in range(len(jobs) + VALUE_LAG):
                if n in (3, 5):
                    split_to(split_index[number[("out1", 0)]] + (n - 1) // 2)
                if n < len(jobs):
                    kind, heads, t, k0, nk = jobs[n]
                    scale = 64 ** -0.5 if kind == "swa" else 96 ** -0.5
                    s_, pr_ = st[:, n % PR], pr[:, n % PR]
                    act.wait_ge(S["neg_max"], n + 1)
                    if n >= PR:
                        misc.filled(act, ("pT", n - PR))
                    bk = dense.filled(act, ("s", n))
                    for i in range(len(heads)):
                        e = act.activation(pr_[:, i * nk:(i + 1) * nk], bk[:, i * nk:(i + 1) * nk], ACT.Exp,
                                           scale=scale, bias=s_[:, 1, i:i + 1], accum_out=s_[:, 2, i:i + 1])
                    if kind == "swa":
                        e = act.activation(s_[:, 3, 0:len(heads)], s_[:, 3, 0:len(heads)], ACT.Exp)
                    e.then_inc(dense.read(("s", n)), 1)
                m = n - TURN_LAG
                if 0 <= m < len(jobs):
                    w = len(jobs[m][1]) * jobs[m][4]
                    if m >= 2:
                        if ("pv", m - 2) in marks:
                            act.wait_ge(S["half_used"], marks[("pv", m - 2)])
                        else:
                            pvs.filled(act, ("pv", job_tile[m - 2]))
                    evacuate(misc, ("pT", m), pT[:, m % 2, 0:w], lambda b: b[:, 0:w])
                m = n - VALUE_LAG
                if m >= 0 and ends[m][1]:
                    bk = pvs.filled(act, ("pv", job_tile[m]))
                    act.activation(mix_part(h_hi, job_tile[m]), mix_bank(bk, job_tile[m]), ACT.Copy)\
                        .then_inc(S["pv_hi"], 1)
            out_projection(1, 3)
            norm(3, 32)
            act.wait_ge(S["odd_sent"], 64)
            ffn(1, 4)
            norm(4, 0, high=False)
            for m in range(DT):
                evacuate(misc, ("y", m), xtok[:, :, m * P:(m + 1) * P],
                         lambda b: b[:, 0:T].rearrange("p (c e) -> p c e", c=NCH))
                if m % 4 == 3:
                    for i in range(m - 3, m + 1):
                        misc.was_read(act, ("y", i))
                    f = slice((m - 3) * P, (m + 1) * P)
                    act.dma_start(O[0][0][:, f], xtok[:, 0, f]).then_inc(S["y_sent"], 16)
                    act.dma_start(O[1][0].rearrange("(c p) d -> p c d", p=P)[:, :, f], xtok[:, 1:3, f])\
                        .then_inc(S["y_sent"], 16)
            act.wait_ge(S["y_sent"], 64)

        @block.vector
        def _(dve):
            own = [0]
            col = lambda name, i=None: (vec[:, ROWS[name][0]:ROWS[name][0] + ROWS[name][1]] if i is None
                                        else vec[:, ROWS[name][0] + i:ROWS[name][0] + i + 1])

            def step(ins):
                own[0] += 1
                ins.then_inc(S["dve_own"], 1)
                dve.wait_ge(S["dve_own"], own[0])

            def modulation(place, pairs=None):
                for p in (ada_pairs(place) if pairs is None else pairs):
                    bk = adas.filled(dve, ("ada", p))
                    dve.tensor_copy(ada_row[:, p % 2, :], bk[0:2, :]).then_inc(adas.read(("ada", p)), 1)
                    if p % 2:
                        l, g = p // 12, p % 12 // 2
                        bk = adas.filled(dve, ("mod", p // 2))
                        dve.tensor_tensor(mod[:, l, 8 * g:8 * g + 8, :], bk[:, 0:16].rearrange("p (j c) -> p j c", c=2),
                                          ada_b_col[:, 48 * l + 8 * g:48 * l + 8 * g + 8].unsqueeze(2)
                                          .to_broadcast([P, 8, 2]), ALU.add).then_inc(adas.read(("mod", p // 2)), 1)
                        adas.was_read(dve, ("mod", p // 2))

            def gains(n):
                l, k = n // 2, 1 + 3 * (n % 2)
                step(dve.tensor_scalar(gain[:, n], mod[:, l, 8 * k:8 * k + 8, :], 1.0, None, ALU.add))
                g = vec[:, ROWS[f"norm{n % 2 + 1}_g"][0] + 8 * l:][:, 0:8]
                step(dve.tensor_tensor(gain[:, n], gain[:, n], g.unsqueeze(2).to_broadcast([P, 8, 2]), ALU.mult))

            def norm(n, base, place):
                l, k = n // 2, 3 * (n % 2)

                def low(m):
                    dve.wait_ge(S["hhi_ready"], base + m + 1)
                    for c, a, b in ((1, 0, TC), (0, TC, T)):
                        ins = dve.scalar_tensor_tensor(h_lo[:, m, a:b], ht[:, m % 2, a:b], mod[:, l, 8 * k + m, c:c + 1],
                                                       h_hi[:, m, a:b].bitcast(F32), ALU.add, ALU.subtract)
                    ins.then_inc(S["h_ready"], 1)

                gains(n)
                dve.wait_ge(S["rstd_ready"], n + 1)
                for m in range(DT):
                    if m >= 2:
                        dve.wait_ge(S["h_ready"], base + m - 1)
                    for c, a, b in ((1, 0, TC), (0, TC, T)):
                        ins = dve.scalar_tensor_tensor(ht[:, m % 2, a:b], X[:, m, a:b], gain[:, n, m, c:c + 1],
                                                       rstd[:, 0, a:b], ALU.mult, ALU.mult)
                    ins.then_inc(S["ht_ready"], 1)
                    if m:
                        low(m - 1)
                    modulation(place, ada_pairs(place)[m:m + 1])
                low(DT - 1)

            def add_squares(n, m):
                if m == 0:
                    step(dve.tensor_tensor(sq[:, 0, :], X[:, 0, :], X[:, 0, :], ALU.mult))
                else:
                    step(dve.tensor_tensor(sq[:, 1, :], X[:, m, :], X[:, m, :], ALU.mult))
                    ins = dve.tensor_tensor(sq[:, 0, :], sq[:, 0, :], sq[:, 1, :], ALU.add)
                    if m < DT - 1:
                        step(ins)
                    else:
                        ins.then_inc(S["sq_ready"], 1)

            def residual(key, n, l, m, k):
                bk = dense.filled(dve, key)
                for c, a, b in ((1, 0, TC), (0, TC, T)):
                    ins = dve.scalar_tensor_tensor(X[:, m, a:b], bk[:, a:b], mod[:, l, 8 * k + m, c:c + 1],
                                                   X[:, m, a:b], ALU.mult, ALU.add)
                ins.then_inc(dense.read(key), 1)
                dense.was_read(dve, key)
                add_squares(n, m)

            def ffn(l):
                def low_u(f):
                    dve.wait_ge(S["uhi_ready"], FT * l + f + 1)
                    dve.tensor_tensor(u_lo[:, f, :], uf[:, f % 2, :], u_hi[:, f, :].bitcast(F32), ALU.subtract)\
                        .then_inc(S["u_ready"], 1)
                for f in range(FT):
                    dense.was_read(dve, ("gate", l, f))
                    bk = dense.filled(dve, ("up", l, f))
                    if f >= 2:
                        dve.wait_ge(S["u_ready"], FT * l + f - 1)
                    dve.tensor_tensor(uf[:, f % 2, :], sa[:, f % 2, :], bk[:, 0:T], ALU.mult)\
                        .then_inc(dense.read(("up", l, f)), 1)
                    if f:
                        low_u(f - 1)
                low_u(FT - 1)
                for m in range(DT):
                    residual(("down", l, m), 2 * l + 2, l, m, 5)

            dve.memset(eps_col[:, :], EPS).then_inc(S["dve_own"], 1)
            own[0] += 1
            modulation("start", range(0, 1))
            for c in range(NCH):
                for g in range(2):
                    bk = dense.filled(dve, ("x", c, g))
                    dve.tensor_copy(X[:, 4 * g:4 * g + 4, c * P:(c + 1) * P],
                                    bk[:, :].rearrange("p (j t) -> p j t", j=4)).then_inc(dense.read(("x", c, g)), 1)
            dense.was_read(dve, ("x", NCH - 1, 1))
            for m in range(DT):
                add_squares(0, m)
            bk = misc.filled(dve, "vec")
            dve.tensor_copy(vec[:, :], bk[:, 0:NROWS]).then_inc(misc.read("vec"), 1)
            bk = misc.filled(dve, "ada_b")
            dve.tensor_copy(ada_b_col[:, :], bk[:, 0:96]).then_inc(misc.read("ada_b"), 1)
            bk = misc.filled(dve, "rowb")
            dve.tensor_copy(rowb[:, :], bk[:, 0:32]).then_inc(misc.read("rowb"), 1)
            misc.was_read(dve, "rowb")
            step(dve.tensor_scalar(neg_sink[:, :], rowb[:, 0:8], -1.0, None, ALU.mult))
            modulation("start", range(1, 2))
            b0, b1 = col("hgrn_lower_bounds")[:, 0:8], col("hgrn_lower_bounds")[:, 8:16]
            step(dve.tensor_tensor(lbt[:, 2, :], b0, b1, ALU.max))
            dve.tensor_tensor(lbt[:, 0, :], b0, lbt[:, 2, :], ALU.subtract)
            dve.tensor_tensor(lbt[:, 1, :], b1, lbt[:, 2, :], ALU.subtract).then_inc(S["raw_f"], 1)
            dve.wait_ge(S["lb_exp"], 1)
            step(dve.tensor_tensor(lbt[:, 2, :], lbt[:, 0, :], lbt[:, 1, :], ALU.add))
            step(dve.reciprocal(lbt[:, 2, :], lbt[:, 2, :]))
            step(dve.tensor_tensor(lb[:, :], lbt[:, 0, :], lbt[:, 2, :], ALU.mult))
            step(dve.tensor_scalar(oml[:, :], lb[:, :], -1.0, 1.0, ALU.mult, ALU.add))
            modulation("start", range(2, 4))
            norm(0, 0, "norm0")

            for d, (f, k) in enumerate(((PF, kf), (SI, kb))):
                for h in range(H):
                    j = 4 * d + h
                    dense.was_read(dve, ("in0", 4 + j))
                    step(dve.tensor_scalar(f[:, h, :], f[:, h, :], oml[:, j:j + 1], lb[:, j:j + 1], ALU.mult, ALU.add))
                    step(dve.tensor_scalar(k[:, h, :], f[:, h, :], -1.0, 1.0, ALU.mult, ALU.add))
            dense.was_read(dve, ("in0", 3))
            dve.wait_ge(S["rest_in"], 16)

            lv = cst("levels")
            for i, L in enumerate(LEVELS):
                if i:
                    misc.filled(dve, ("level", i - 1, 2))
                if L == 0:
                    dve.tensor_copy(Qd[:], q[:])
                    dve.tensor_tensor(Kd[:], kf[:], kb[:], ALU.add).then_inc(S["level_ready"], 1)
                else:
                    halves = lambda t: flat(t).rearrange("p (n two l) -> p n two l", two=2, l=L)
                    (qv, fv, sv, kfv, kbv, sfv, pxv, qdv, kdv) = (halves(t) for t in
                                                                 (q, PF, SI, kf, kb, SF, PX, Qd, Kd))
                    A, B = 0, 1
                    mul = lambda o, a, b: dve.tensor_tensor(o, a, b, ALU.mult)
                    mul(qdv[:, :, B, :], qv[:, :, B, :], fv[:, :, B, :])
                    mul(qdv[:, :, A, :], qv[:, :, A, :], sv[:, :, A, :])
                    if L == 1:
                        dve.tensor_copy(kdv[:, :, A, :], kfv[:, :, A, :])
                        dve.tensor_copy(kdv[:, :, B, :], kbv[:, :, B, :]).then_inc(S["level_ready"], 1)
                        dve.tensor_copy(sfv[:, :, A, :], fv[:, :, B, :])
                        dve.memset(sfv[:, :, B, :], 1.0)
                        dve.tensor_copy(pxv[:, :, B, :], sv[:, :, A, :])
                        step(dve.memset(pxv[:, :, A, :], 1.0))
                    else:
                        mul(kdv[:, :, A, :], kfv[:, :, A, :], sfv[:, :, A, :])
                        mul(kdv[:, :, B, :], kbv[:, :, B, :], pxv[:, :, B, :]).then_inc(S["level_ready"], 1)
                        n = 1536 // (2 * L)
                        wide = lambda v: v.to_broadcast([P, n, L])
                        mul(sfv[:, :, A, :], sfv[:, :, A, :], wide(fv[:, :, B, L - 1:L]))
                        step(mul(pxv[:, :, B, :], pxv[:, :, B, :], wide(sv[:, :, A, 0:1])))
                    n = 1536 // (2 * L)
                    wide = lambda v: v.to_broadcast([P, n, L])
                    mul(fv[:, :, B, :], fv[:, :, B, :], wide(fv[:, :, A, L - 1:L]))
                    step(mul(sv[:, :, A, :], sv[:, :, A, :], wide(sv[:, :, B, 0:1])))
                for c in range(NCH):
                    bk = misc.filled(dve, ("level", i, c))
                    b3 = bk[:, :].rearrange("p (h t) -> p h t", h=H)
                    mask = lv[:, i * P:(i + 1) * P].unsqueeze(1).to_broadcast([P, H, P])
                    if i == 0:
                        dve.tensor_tensor(Am[:, c], b3, mask, ALU.mult).then_inc(misc.read(("level", i, c)), 1)
                        misc.was_read(dve, ("level", i, c))
                    else:
                        dve.copy_predicated(Am[:, c], mask.bitcast(I32), b3).then_inc(misc.read(("level", i, c)), 1)
            step(dve.tensor_tensor(SF[:, :, 0:2 * P], SF[:, :, 0:2 * P], kf[:, :, 0:2 * P], ALU.mult))
            dve.tensor_tensor(PX[:, :, 0:P], PX[:, :, 0:P], kb[:, :, 0:P], ALU.mult).then_inc(S["kfin_ready"], 1)
            dve.tensor_tensor(PX[:, :, 2 * P:T], PX[:, :, 2 * P:T], kb[:, :, 2 * P:T], ALU.mult)\
                .then_inc(S["kfin_ready"], 1)
            for o, f in ((Qd, PF), (Kd, SI)):
                dve.tensor_tensor(o[:, :, P:T], q[:, :, P:T], f[:, :, P:T], ALU.mult).then_inc(S["qi_ready"], 1)
            dve.wait_ge(S["qi_ready"], 2)
            bk = dense.filled(dve, "gates")
            dve.tensor_tensor(G, bk[:, 0:48].rearrange("p (c j) -> p c j", c=NCH),
                              rowb[:, 8:24].unsqueeze(1).to_broadcast([P, NCH, 16]), ALU.add)\
                .then_inc(dense.read("gates"), 1)
            dense.was_read(dve, "gates")
            dve.engine_nop().then_inc(S["gates_ready"], 1)
            G5 = G.rearrange("p c (d k h) -> p c d k h", d=2, k=2)
            step(dve.tensor_scalar(LF, G5[:, :, :, 1, :], 0.0, None, ALU.min))
            dve.wait_ge(S["gates_abs"], 1)
            dve.tensor_tensor(LF, LF, LE, ALU.subtract).then_inc(S["gates_log"], 1)
            pairs = ada_pairs("hgrn_end")
            modulation("hgrn_end", pairs[0:1])
            bk = misc.filled(dve, "B")
            B4 = bk[:, 0:24].rearrange("p (c d h) -> p c d h", c=NCH, d=2)
            dve.tensor_copy(GB[:, :, 2:4, :], B4)
            dve.tensor_tensor(GB[:, :, 0:2, :], G5[:, :, :, 0, :], B4, ALU.subtract).then_inc(misc.read("B"), 1)
            modulation("hgrn_end", pairs[1:])
            for c in range(NCH):
                bk = misc.filled(dve, ("rows", c))
                b4 = bk[0:4, :].rearrange("p (k t) -> p k t", k=4)
                dve.tensor_copy(row_M[:, :, c * P:(c + 1) * P], b4[:, 0:2])
                dve.tensor_copy(row_B[:, :, c * P:(c + 1) * P], b4[:, 2:4]).then_inc(misc.read(("rows", c)), 1)
            misc.was_read(dve, ("rows", 2))
            dve.wait_ge(S["m0_in"], 16)
            for d in range(2):
                for lo, hi, m0 in ((0, P, 0.0), (P, T, m0_col[:, d:d + 1])):
                    r = row_M[:, d, lo:hi]
                    if d:
                        r = r[:, ::-1]
                    ins = dve.tensor_tensor_scan(r, r, r, m0, ALU.max, ALU.max)
            step(ins)
            step(dve.tensor_tensor(row_B, row_B, row_M, ALU.add))
            for d, t in ((0, P - 1), (1, 0)):
                dve.tensor_copy(m_out[:, d:d + 1], row_B[:, d, t:t + 1]).then_inc(S["rows_m"], 1)
            dve.wait_ge(S["state_in"], 16)
            for d, tot in ((0, lambda h: PF[:, h, 2 * P - 1:2 * P]), (1, lambda h: SI[:, h, 2 * P:2 * P + 1])):
                bk = misc.filled(dve, ("kv", 2 + d))
                for h in range(H):
                    ins = dve.scalar_tensor_tensor(S1[:, d, h, :], S0[:, d, h, :], tot(h), bk[:, h * P:(h + 1) * P],
                                                   ALU.mult, ALU.add)
                ins.then_inc(misc.read(("kv", 2 + d)), 1)
            modulation("states")
            for c in range(NCH):
                bk = dense.filled(dve, ("hg_o", c))
                dve.tensor_copy(o_hg[:, :, c * P:(c + 1) * P], bk[:, :].rearrange("p (h t) -> p h t", h=H))\
                    .then_inc(dense.read(("hg_o", c)), 1)
            modulation("hgrn_norm")

            def head_out(h, src, gate, g, squares, n0, base):
                dve.wait_ge(S["mo_rstd"], n0 + h + 1)
                dve.tensor_tensor(src[:, h, :], src[:, h, :], squares[:, h, :], ALU.mult).then_inc(S["mo_t"], 1)
                dve.wait_ge(S["mo_t"], n0 + h + 1)
                if h >= 2:
                    dve.wait_ge(S["h_ready"], base + h - 1)
                dve.scalar_tensor_tensor(ht[:, h % 2, :], src[:, h, :], g, gate[:, h, :], ALU.mult, ALU.mult)\
                    .then_inc(S["ht_ready"], 1)

            def head_low(h, base):
                dve.wait_ge(S["hhi_ready"], base + h + 1)
                dve.tensor_tensor(h_lo[:, base - 8 + h, :], ht[:, h % 2, :],
                                  h_hi[:, base - 8 + h, :].bitcast(F32), ALU.subtract).then_inc(S["h_ready"], 1)

            modulation("gates")
            dve.wait_ge(S["s_out"], 16)

            def weights(j):
                h, d = j // 2, j % 2
                qk, A, E = QK[:, h % 2, :], Aw[:, j % 2, :], Ew[:, j % 2, :]
                dense.was_read(dve, ("M", j))
                dense.was_read(dve, ("qk10", h))
                if j >= 2:
                    misc.filled(dve, ("num", j - 2))
                if d == 0:
                    ins = dve.tensor_tensor(A, E, qk[:, 0:512], ALU.mult)
                else:
                    dve.tensor_tensor(A[:, 0:2 * P], E[:, 0:2 * P], qk[:, 0:2 * P], ALU.mult)
                    ins = dve.tensor_tensor(A[:, 2 * P:], E[:, 2 * P:], qk[:, 3 * P:5 * P], ALU.mult)
                ins.then_inc(S["A_ready"], 1)
                bk = misc.filled(dve, ("ss", j))
                dve.tensor_tensor(qs[j % 2], qm[:, h, P:T], bk[:, 0:TL], ALU.mult).then_inc(misc.read(("ss", j)), 1)
                if j >= 2:
                    misc.filled(dve, ("C", j - 2))
                if j == 0:
                    misc.was_read(dve, "k_tok")
                at = 127 if d == 0 else 0
                dve.tensor_scalar(k_in[:, j % 2, :], k_tok[:, h * P:(h + 1) * P], E[:, at:at + 1], None,
                                  ALU.mult).then_inc(S["k_in_ready"], 1)

            weights(0)
            for j in range(2 * H):
                h, d = j // 2, j % 2
                if j < 2 * H - 1:
                    weights(j + 1)
                misc.was_read(dve, ("em", j))
                dense.was_read(dve, ("den", j))
                step(dve.tensor_tensor(den, den, em, ALU.max))
                step(dve.reciprocal(den, den))
                bk = misc.filled(dve, ("num", j))
                dst = hm[:, h, :] if d == 0 else hf
                dve.tensor_tensor(dst, bk[:, 0:T], den, ALU.mult).then_inc(misc.read(("num", j)), 1)
                misc.was_read(dve, ("num", j))
                if d == 0:
                    dve.engine_nop().then_inc(S["h_done"], 1)
                else:
                    dve.tensor_tensor(hm[:, h, :], hm[:, h, :], hf, ALU.add).then_inc(S["h_done"], 1)
                    modulation("mlstm", ada_pairs("mlstm")[h:h + 1])
                    if h:
                        head_low(h - 1, 8)
                    head_out(h, o_hg, ga, col("hgrn_norm_g"), hg_sq, 0, 8)
            dve.wait_ge(S["h_done"], 8)
            head_low(H - 1, 8)
            modulation("mlstm_norm")
            for h in range(H):
                head_out(h, hm, ob, col("mlstm_norm_g"), ml_sq, 4, 12)
                if h:
                    head_low(h - 1, 12)
            head_low(H - 1, 12)
            for m in range(DT):
                residual(("out", 0, m), 1, 0, m, 2)
            dense.was_read(dve, ("out", 0, 7))
            norm(1, 16, "norm1")
            dve.wait_ge(S["s_out"], 16)
            dve.wait_ge(S["m_sent"], 16)
            dve.wait_ge(S["c_sent"], 32)
            ffn(0)
            norm(2, 24, "norm2")

            def rope(i):
                x = (qc[:, i, P:T] if i < 4 else kT[:, P:T] if i == 4 else kr4[:, P:T] if i == 5
                     else qr[:, i - 6, P:T])
                kind = "swa" if i < 5 else "mla"
                if i == 4:
                    dense.was_read(dve, ("kc",))
                bk = misc.filled(dve, ("rot", i))
                dve.tensor_tensor(rt[:, 0, :], x, cst(kind + "_cos"), ALU.mult)
                dve.tensor_tensor(rt[:, 1, :], bk[:, 0:TL], cst(kind + "_sin"), ALU.mult)\
                    .then_inc(misc.read(("rot", i)), 1)
                misc.was_read(dve, ("rot", i))
                dve.tensor_tensor(x, rt[:, 0, :], rt[:, 1, :], ALU.add).then_inc(S["roped"], 1)
                dve.wait_ge(S["roped"], i + 1)

            for i in range(5):
                rope(i)
            modulation("projections")
            for k in range(5):
                i = 0 if k < 3 else 1
                dve.wait_ge(S["cq_rstd"], i + 1)
                src = cqf[:, k, :] if i == 0 else ckvf[:, k - 3, :]
                g = col("mla_q_norm_g", k) if i == 0 else col("mla_kv_norm_g", k - 3)
                dve.scalar_tensor_tensor(src, src, g, rstd[:, i, :], ALU.mult, ALU.mult).then_inc(S["cq_t"], 1)
            for k in range(5):
                dve.wait_ge(S["cqhi"], k + 1)
                if k < 3:
                    dve.tensor_tensor(cq_lo[:, k, :], cqf[:, k, :], cq_hi[:, k, :].bitcast(F32), ALU.subtract)\
                        .then_inc(S["cq_ready"], 1)
                else:
                    dve.tensor_tensor(ckv_lo[:, k - 3, 0:T], ckvf[:, k - 3, :], ckv_hi[:, k - 3, 0:T].bitcast(F32),
                                      ALU.subtract).then_inc(S["ckv_ready"], 1)

            rope(5)
            dve.wait_ge(S["cache_ready"], 1)
            bk = misc.filled(dve, ("cache",))
            dve.tensor_tensor(ckv_lo[:, :, T:TK], bk[:, 2 * P:512].rearrange("p (k t) -> p k t", k=2),
                              ckv_hi[:, :, T:TK].bitcast(F32), ALU.subtract).then_inc(misc.read(("cache",)), 1)
            rope(6)
            rope(7)

            for n in range(len(jobs) + VALUE_LAG):
                if n < len(jobs):
                    kind, heads, t, k0, nk = jobs[n]
                    scale = 64 ** -0.5 if kind == "swa" else 96 ** -0.5
                    nh = len(heads)
                    s_ = st[:, n % PR]
                    bk = dense.filled(dve, ("s", n))
                    step(dve.tensor_reduce(s_[:, 0, 0:nh], bk[:, 0:nh * nk].rearrange("p (h k) -> p h k", h=nh), AX.X,
                                           ALU.max))
                    if kind == "swa":
                        hs = slice(heads[0], heads[0] + nh)
                        step(dve.scalar_tensor_tensor(s_[:, 1, 0:nh], s_[:, 0, 0:nh], -scale, neg_sink[:, hs],
                                                      ALU.mult, ALU.min))
                        dve.tensor_tensor(s_[:, 3, 0:nh], rowb[:, hs], s_[:, 1, 0:nh], ALU.add)\
                            .then_inc(S["neg_max"], 1)
                    else:
                        dve.tensor_scalar(s_[:, 1, 0:nh], s_[:, 0, 0:nh], -scale, None, ALU.mult)\
                            .then_inc(S["neg_max"], 1)
                if 1 <= n <= len(jobs):
                    kind, heads, t, k0, nk = jobs[n - 1]
                    nh = len(heads)
                    s_ = st[:, (n - 1) % PR]
                    dense.was_read(dve, ("s", n - 1))
                    if kind == "swa":
                        step(dve.tensor_tensor(s_[:, 2, 0:nh], s_[:, 2, 0:nh], s_[:, 3, 0:nh], ALU.add))
                    step(dve.reciprocal(s_[:, 4, 0:nh], s_[:, 2, 0:nh]))
                    for i in range(nh):
                        p = pr[:, (n - 1) % PR, i * nk:(i + 1) * nk]
                        ins = dve.tensor_scalar(p, p, s_[:, 4, i:i + 1], None, ALU.mult)
                    ins.then_inc(S["p_ready"], 1)
                if n >= VALUE_LAG and ends[n - VALUE_LAG][1]:
                    tile = job_tile[n - VALUE_LAG]
                    dve.wait_ge(S["pv_hi"], list(dict.fromkeys(job_tile)).index(tile) + 1)
                    bk = pvs.filled(dve, ("pv", tile))
                    dve.tensor_tensor(mix_part(h_lo, tile), mix_bank(bk, tile), mix_part(h_hi, tile).bitcast(F32),
                                      ALU.subtract).then_inc(pvs.read(("pv", tile)), 1)
                if n in fill_after:
                    modulation("attention", fill_after[n])
            for m in range(DT):
                residual(("out", 1, m), 3, 1, m, 2)
            dense.was_read(dve, ("out", 1, 7))
            norm(3, 32, "norm3")
            dve.wait_ge(S["odd_sent"], 64)
            ffn(1)
            dense.was_read(dve, ("down", 1, 7))
            dve.wait_ge(S["rstd_ready"], 5)
            for m in range(DT):
                if m >= 2:
                    misc.filled(dve, ("y", m - 2))
                dve.scalar_tensor_tensor(ht[:, m % 2, :], X[:, m, :], col("final_norm_g", m), rstd[:, 0, :],
                                         ALU.mult, ALU.mult).then_inc(S["y_ready"], 1)


_INS = ["x_prompt", "x_sample", "state_hgrn", "state_mlstm_c", "state_mlstm_n", "state_mlstm_m",
        "cache_swa_k", "cache_swa_v", "cache_mla_ckv", "cache_mla_krope", "c", "c_ctx",
        "w_in_even", "hgrn_lower_bounds", "hgrn_norm_g", "mlstm_gate_bias", "mlstm_norm_g", "w_out_even",
        "w_in_odd", "swa_sink", "mla_q_norm_g", "mla_w_uq", "mla_kv_norm_g", "mla_w_uk", "mla_w_uv", "w_out_odd",
        "ada_w", "ada_b", "norm1_g", "norm2_g", "ffn_w1", "ffn_w3", "ffn_w2", "final_norm_g"]
_OUTS = [(1, TC, D), (1, TL, D), (1, 1, 2, H, P, P), (1, 1, 2, H, P, P), (1, 1, 2, H, P), (1, 1, 2, H),
         (1, 1, TC, 2, 64), (1, 1, TC, 2, 64), (1, 1, TC, 256), (1, 1, TC, 32)]


def kernel(**inputs):
    import concourse.bacc as _bacc
    from concourse.bass_utils import run_bass_kernel_spmd as _run

    nc = _bacc.Bacc("TRN2", target_bir_lowering=False, num_devices=1, dynamic_dma_scratch_size=4096)
    arrays, I, O = {}, {}, []
    for name in _INS + ["shape_constants"]:
        a = np.ascontiguousarray(inputs[name] if name in inputs else shape_constants())
        arrays[f"in_{name}"] = a
        I[name] = nc.dram_tensor(f"in_{name}", a.shape, mybir.dt.from_np(a.dtype), kind="ExternalInput").ap()
    for i, shape in enumerate(_OUTS):
        O.append(nc.dram_tensor(f"out_{i}", shape, F32, kind="ExternalOutput").ap())
    build(nc, I, O)
    r = _run(nc, [arrays], core_ids=[0])
    return tuple(r.results[0][f"out_{i}"] for i in range(len(_OUTS)))
```

```python
from contextlib import ExitStack

import numpy as np
import concourse.bass as bass
from concourse import mybir

F32 = mybir.dt.float32
F32R = mybir.dt.float32r
I32 = mybir.dt.int32
ALU = mybir.AluOpType
ACT = mybir.ActivationFunctionType
AX = mybir.AxisListType

P = 128
D = 1024
DT = D // P
TC = 128
TL = 256
T = TC + TL
NCH = T // P
H = 4
FF = 2816
FT = FF // P
WE = 4624
WO = 1440
EPS = 1e-6
HS = 8
TK = T + P
BIG = 1e30
TURN_LAG, VALUE_LAG = 3, 4
PR = TURN_LAG + 1
LEVELS = [0, 1, 2, 4, 8, 16, 32, 64]

ROWS = {}
_n = 0
for _name, _k in (("c", 8), ("c_ctx", 8), ("norm1_g", 16), ("norm2_g", 16), ("final_norm_g", 8),
                  ("hgrn_lower_bounds", 16), ("hgrn_norm_g", 1), ("mlstm_norm_g", 1),
                  ("mla_q_norm_g", 3), ("mla_kv_norm_g", 2), ("state_mlstm_n", 8)):
    ROWS[_name] = (_n, _k)
    _n += _k
NROWS = _n

CONSTS = {}
_n = 0
for _name, _k in (("ident", 128), ("ones", 128), ("swa_cos", 256), ("swa_sin", 256), ("mla_cos", 256),
                  ("mla_sin", 256), ("swa_turn", 128), ("mla_turn", 128), ("levels", 8 * 128),
                  ("tri_f", 128), ("tri_b", 128), ("big_f", 128), ("big_b", 128), ("band0", 128),
                  ("band1", 128), ("rep", 128)):
    CONSTS[_name] = (_n, _k)
    _n += _k
NCONST = _n


def shape_constants():
    out = np.zeros((P, NCONST), np.float32)

    def put(name, value):
        a, k = CONSTS[name]
        out[:value.shape[0], a:a + k] = value.reshape(value.shape[0], k)

    put("ident", np.eye(P, dtype=np.float32))
    put("ones", np.ones((P, P), np.float32))
    pos = np.arange(TL)
    rows, cols = (pos // 64).astype(np.float32), (pos % 64).astype(np.float32)
    for name, d, n in (("swa", 64, 2), ("mla", 32, 4)):
        ax, half = d // 2, d // 4
        inv = (10000.0 ** (-np.arange(0, ax, 2, dtype=np.float32) / ax)).astype(np.float32)
        cos, sin = np.zeros((d, TL), np.float32), np.zeros((d, TL), np.float32)
        turn = np.zeros((d, d), np.float32)
        for a, at in ((0, rows), (1, cols)):
            ang = (at[None, :] * inv[:, None]).astype(np.float32)
            for s in (0, 1):
                r = a * ax + s * half
                cos[r:r + half], sin[r:r + half] = np.cos(ang), np.sin(ang)
            for i in range(half):
                x1, x2 = a * ax + i, a * ax + half + i
                turn[x2, x1] = -1.0
                turn[x1, x2] = 1.0
        put(name + "_cos", np.tile(cos, (n, 1)))
        put(name + "_sin", np.tile(sin, (n, 1)))
        put(name + "_turn", np.kron(np.eye(n, dtype=np.float32), turn))
    s, t = np.arange(P)[:, None], np.arange(P)[None, :]
    lv = [(s == t)] + [(s // (2 * L) == t // (2 * L)) & (s // L != t // L) for L in LEVELS[1:]]
    put("levels", np.stack(lv, 1).astype(np.float32))
    put("tri_f", (s <= t).astype(np.float32))
    put("tri_b", (s >= t).astype(np.float32))
    put("big_f", np.where(s > t, BIG, 0).astype(np.float32))
    put("big_b", np.where(s < t, BIG, 0).astype(np.float32))
    put("band0", np.where(t > s, -BIG, 0).astype(np.float32))
    put("band1", np.where(t < s, -BIG, 0).astype(np.float32))
    rep = np.zeros((P, P), np.float32)
    rep[96:] = np.tile(np.eye(32, dtype=np.float32), (1, 4))
    put("rep", rep)
    return out


ADA_PLACES = {"start": 4, "norm0": 1, "hgrn_norm": 1, "mlstm": 4, "mlstm_norm": 1, "norm1": 1, "ffn0": 10,
              "norm2": 1, "norm3": 1}
assert sum(ADA_PLACES.values()) == 24
VADA, VADA_UP = 2 * ADA_PLACES["ffn0"], 12
VADA_AT_UP = {3 + 3 * n // 2: n for n in range(VADA_UP)}
VADA_AT_DOWN = {n: VADA_UP + n for n in range(VADA - VADA_UP)}


def ada_pairs(place):
    at = 0
    for name, n in ADA_PLACES.items():
        if name == place:
            return range(at, at + n)
        at += n
    raise KeyError(place)


def plan_units():
    units = []
    add = lambda name, n, kt, cols, first=0: units.extend((name, first + i, kt, cols) for i in range(n))

    def ada(place):
        units.extend((f"ada{p // 12}", 2 * (p % 12) + i, DT, 256) for p in ada_pairs(place) for i in range(2))

    ada("start")
    add("in0", 1, DT, 256)
    ada("norm0")
    add("in0", 6, DT, 256, 1)
    add("gates", 1, DT, 16)
    add("in0", 11, DT, 256, 7)
    add("out0", 2, DT, 256)
    for place in ("hgrn_norm", "mlstm", "mlstm_norm"):
        ada(place)
    add("out0", 2, DT, 256, 2)
    add("up0", 2, DT, 256)
    ada("norm1")
    add("up0", FT - 2, DT, 256, 2)
    add("down0", 16, 11, 128)
    add("in1", 2, DT, 256)
    ada("norm2")
    add("in1", 3, DT, 256, 2)
    add("in1", 1, DT, 160, 5)
    add("uq", 2, 3, 384)
    add("uk", 2, 2, 256)
    add("uv", 2, 2, 256)
    add("out1", 4, DT, 256)
    add("up1", 2, DT, 256)
    ada("norm3")
    add("up1", FT - 2, DT, 256, 2)
    add("down1", 16, 11, 128)
    return units


def build(nc, I, O):
    units = plan_units()
    RAW, SPLIT = 3, 2
    number = {(n, i): u for u, (n, i, _, _) in enumerate(units)}
    native = [n.startswith("ada") for n, _, _, _ in units]
    split_units = [u for u in range(len(units)) if not native[u]]
    split_index = {u: s for s, u in enumerate(split_units)}
    native_index = {u: s for s, u in enumerate(u for u in range(len(units)) if native[u])}

    ctx = ExitStack()
    with ctx:
        def sb(name, shape, dt=F32):
            return ctx.enter_context(nc.sbuf_tensor(name, shape, dt))

        def sem(name):
            return ctx.enter_context(nc.semaphore(name))

        X = sb("X", [P, DT, T])
        h_hi = sb("h_hi", [P, DT, T], F32R)
        h_lo = sb("h_lo", [P, DT, T], F32R)
        raw = [sb(f"raw{i}", [P, 2048]) for i in range(RAW)]
        w_hi = [sb(f"w_hi{i}", [P, 2048], F32R) for i in range(SPLIT)]
        w_lo = [sb(f"w_lo{i}", [P, 2048], F32R) for i in range(SPLIT)]
        const = sb("const", [P, NCONST])
        vec = sb("vec", [P, NROWS])
        ada_b_col = sb("ada_b_col", [P, 96])
        cond = sb("cond", [P, DT, 2])
        ada_row = sb("ada_row", [2, 2, 512])
        mod = sb("mod", [P, 2, 48, 2])
        gain = sb("gain", [P, 4, DT, 2])
        lb = sb("lb", [P, 8])
        oml = sb("oml", [P, 8])
        bound_exp = sb("bound_exp", [P, 3, 8])
        row_in = sb("row_in", [1, 32])
        rowb = sb("rowb", [P, 32])
        m0_col = sb("m0_col", [4, 2])
        sq = sb("sq", [P, 2, T])
        rstd = sb("rstd", [P, 2, T])
        ht = sb("ht", [P, 2, T])
        eps_col = sb("eps_col", [P, 1])
        table_col = sb("table_col", [P, 1])
        neg_sink = sb("neg_sink", [P, 8])
        gates = sb("gates", [P, 178])

        def overlay(tensors):
            with ExitStack() as phase:
                return [phase.enter_context(nc.sbuf_tensor(n, s, dt)) for n, s, dt in tensors]

        xtok, vec_rows, ada_rows = overlay([
            ("xtok", [P, NCH, D], F32), ("vec_rows", [P, P], F32), ("ada_rows", [96, P], F32)])
        HB = [P, H, T]
        (q, PF, SI, kf, kb, SF, PX, Qd, Kd, Am, S0, C0, va, vb, ga, qm, km) = overlay(
            [(n, HB, F32) for n in ("q", "PF", "SI", "kf", "kb", "SF", "PX", "Qd", "Kd")]
            + [("Am", [P, NCH, H, P], F32), ("S0", [P, 2, H, P], F32), ("C0", [P, 2, H, P], F32), ("va", [P, NCH, 512], F32), ("vb", [P, NCH, 512], F32)]
            + [(n, HB, F32) for n in ("ga", "qm", "km")])
        (qc, kT, vt, cqf, ckvf, cq_hi, cq_lo, ckv_hi, ckv_lo, kr4, qn, qr, kn, vm, krr, rt, pr, pT,
         cin_k, cin_c, cin_r, out_k, out_c, out_r, st) = overlay([
            ("qc", [P, 4, T], F32), ("kT", [P, TK], F32), ("vt", [P, 4, P], F32), ("cqf", [P, 3, T], F32),
            ("ckvf", [P, 2, T], F32), ("cq_hi", [P, 3, T], F32R), ("cq_lo", [P, 3, T], F32R),
            ("ckv_hi", [P, 2, TK], F32R), ("ckv_lo", [P, 2, TK], F32R), ("kr4", [P, TK], F32),
            ("qn", [P, 4, T], F32), ("qr", [P, 2, T], F32), ("kn", [P, 4, TK], F32), ("vm", [P, 4, 512], F32),
            ("krr", [P, T], F32), ("rt", [P, 2, TL], F32), ("pr", [P, PR, 512], F32), ("pT", [P, 2, 512], F32),
            ("cin_k", [P, P], F32), ("cin_c", [P, 256], F32), ("cin_r", [P, 4, 32], F32),
            ("out_k", [P, P], F32), ("out_c", [P, 256], F32), ("out_r", [P, 32], F32), ("st", [P, PR, 5, 4], F32)])
        u_hi, u_lo, sa, uf, vada_sum, vada_raw = overlay([
            ("u_hi", [P, FT, T], F32R), ("u_lo", [P, FT, T], F32R), ("sa", [P, 2, T], F32), ("uf", [P, 2, T], F32),
            ("vada_sum", [P, 4, 2, 256], F32), ("vada_raw", [P, 2, 2048], F32)])

        def cst(name):
            a, k = CONSTS[name]
            return const[:, a:a + k]

        ident, ones = cst("ident"), cst("ones")

        flat = lambda t: t[:].rearrange("p a b -> p (a b)")
        kt4 = [flat(kf)[:, 0:512], flat(kf)[:, 512:1024], flat(kf)[:, 1024:1536], flat(q)[:, 1024:1536]]
        ob = kb
        S1 = flat(q)[:, 0:1024].rearrange("p (d h v) -> p d h v", d=2, h=H)
        Sout = flat(PX)[:, 0:1024].rearrange("p (d h v) -> p d h v", d=2, h=H)
        o_hg = SF
        hm = PX
        gate_rows = ht[0:16, 0, :]
        row_M, row_B = sq[0:4], rstd[0:4]
        ss_row = flat(PF)[0:4, 0:512].rearrange("p (d t) -> p d t", d=2)
        k_tok = flat(PF)[:, 512:1024]
        k_in = flat(PF)[:, 1024:1280].rearrange("p (b k) -> p b k", b=2)
        G = gates[:, 0:48].rearrange("p (c j) -> p c j", c=NCH)
        LF = gates[:, 64:88].rearrange("p (c d h) -> p c d h", c=NCH, d=2)
        LE = gates[:, 96:120].rearrange("p (c d h) -> p c d h", c=NCH, d=2)
        GB = gates[:, 128:176].rearrange("p (c k h) -> p c k h", c=NCH, k=4)
        m_out = gates[0:4, 176:178]
        n_out = flat(SI)[0:1, 512:1536].rearrange("p (d h k) -> p d h k", d=2, h=H)
        QK = flat(kf)[:, 0:1280].rearrange("p (b n) -> p b n", b=2)
        Ew = S0[:].rearrange("p d h v -> p (d h v)").rearrange("p (b n) -> p b n", b=2)
        Aw = flat(Qd)[:, 0:1024].rearrange("p (b n) -> p b n", b=2)
        em = flat(Kd)[:, 0:384]
        qs = [flat(Kd)[:, 384:640], flat(kf)[:, 1280:1536]]
        den = flat(Kd)[:, 640:1024]
        hf = flat(Kd)[:, 1024:1408]
        hg_sq, ml_sq = va[:].rearrange("p c e -> p (c e)").rearrange("p (h t) -> p h t", h=H), Kd
        Cout = Am[:].rearrange("p c h t -> p (c h t)")[:, 0:1024].rearrange("p (d h v) -> p d h v", d=2, h=H)

        bank = [ctx.enter_context(nc.psum_tensor(f"bank{i}", [P, 512], F32)) for i in range(8)]

        class Ring:

            def __init__(self, name, banks):
                self.name, self.banks, self.n, self.at = name, banks, len(banks), {}
                self.done = sem(name + "_filled")
                self.free = [sem(f"{name}{b}_read") for b in banks]

            def fill(self, pe, key):
                m = self.at[key] = len(self.at)
                if m >= self.n:
                    pe.wait_ge(self.free[m % self.n], m // self.n)
                return bank[self.banks[m % self.n]]

            def filled(self, eng, key):
                eng.wait_ge(self.done, self.at[key] + 1)
                return bank[self.banks[self.at[key] % self.n]]

            def read(self, key):
                return self.free[self.at[key] % self.n]

            def was_read(self, eng, key):
                eng.wait_ge(self.read(key), self.at[key] // self.n + 1)

        dense = Ring("dense", [0, 1, 2])
        adas = Ring("ada", [3])
        misc = Ring("misc", [5, 6, 7])
        pvs = Ring("pv", [4])
        S = {}

        def signal(*names):
            for n in names:
                S[n] = sem(n)

        signal("raw_in0", "raw_in1", "raw_in2", "hi_ready", "lo_ready", "half_used")
        signal("const_in", "c_in", "rest_in", "rows_in", "adab_in", "small_in", "m0_in", "x_in", "state_in", "c0_in", "cache_in")
        signal("bounds_exp", "vada_part", "vada_ready")
        signal("sq_ready", "stat_done", "stat_read", "rstd_ready", "ht_ready", "hhi_ready", "h_ready")
        signal("uhi_ready", "u_ready")
        signal("pe_own", "dve_own", "act_own")
        signal("bounds_ready", "level_ready", "kfin_ready", "qi_ready",
               "s_out")
        signal("gates_log", "gates_ready", "gates_abs", "rows_m", "rows_done", "A_ready", "k_in_ready", "h_done", "m_sent", "c_sent")
        signal("mo_sq", "mo_rstd", "mo_t")
        signal("roped", "cq_sq", "cq_rstd", "cq_t", "cqhi", "cq_ready", "ckv_ready", "cache_ready", "odd_sent",
               "neg_max", "p_ready", "pv_hi")
        signal("y_ready", "y_sent")
        release = {}
        raw_need, seen = [], [0] * RAW
        pieces = {u: (2 if n.startswith("up") else 6 if n == "uq" else 4 if n == "in1" and i < 2 else 1)
                  for u, (n, i, _, _) in enumerate(units)}
        for u in range(len(units)):
            seen[u % RAW] += 16 * pieces[u]
            raw_need.append(seen[u % RAW])
        vada_in = [sem("vada_in0"), sem("vada_in1")]
        raw_in = [S["raw_in0"], S["raw_in1"], S["raw_in2"]]
        first_vada = ada_pairs("ffn0")[0]

        fetch_at = {("up", f - 1): n for f, n in VADA_AT_UP.items()}
        fetch_at.update({("down", m - 1) if m else ("up", FT - 1): n for m, n in VADA_AT_DOWN.items()})
        block = ctx.enter_context(nc.Block())

        def mix_part(h, tile):
            kind, part, j = tile
            base = 0 if kind == "swa" else 4
            return h[:, base + 2 * j:base + 2 * j + 2, 0:P] if part == "ctx" else h[:, base + j, P:T]

        def mix_bank(bk, tile):
            return bk[:, 0:2 * P].rearrange("p (j t) -> p j t", j=2) if tile[1] == "ctx" else bk[:, 0:2 * P]

        marks = {}

        def mark(mm, key):
            marks[key] = len(marks) + 1
            mm.then_inc(S["half_used"], 1)

        jobs, job_tile = [], []
        for kind, base in (("swa", 0), ("mla", 4)):
            for g in range(2):
                jobs.append((kind, [4 * g + i for i in range(4)], 0, 0, P))
                job_tile.append((kind, "ctx", g))
            for j in range(4):
                for h in (2 * j, 2 * j + 1):
                    for t in (1, 2):
                        jobs.append((kind, [h], t, P, T))
                        job_tile.append((kind, "lat", j))
        ends = [(n == 0 or job_tile[n - 1] != job_tile[n], n == len(jobs) - 1 or job_tile[n + 1] != job_tile[n])
                for n in range(len(jobs))]

        def pv_at(n, h):
            kind, heads, t, _, _ = jobs[n]
            return (h - heads[0]) // 2 * P if t == 0 else (t - 1) * P

        vada_at_up = {3 * q + 6: q for q in range(VADA_UP // 2)}
        vada_at_down = {min(2 * q + 2, DT - 1): VADA_UP // 2 + q for q in range((VADA - VADA_UP) // 2)}
        starts = []
        for n, (kind, heads, t, _, _) in enumerate(jobs):
            starts.append({(i, 0) for i in range(2)} if t == 0 else ({(0, 0)} if t == 1 else set()))

        @block.tensor
        def _(pe):
            def raw_unit(u):
                pe.wait_ge(raw_in[u % RAW], raw_need[u])
                return raw[u % RAW][:, 0:2048].rearrange("p (k n) -> p k n", k=DT)

            def weight(u, kt, k, c, n=P):
                at = units[u][3] * k + c
                return w_hi[split_index[u] % SPLIT][:, at:at + n], w_lo[split_index[u] % SPLIT][:, at:at + n]

            def three(out, terms, first=True, last=True):
                for j, (s_hi, s_lo, m_hi, m_lo) in enumerate(terms):
                    pe.matmul(out, s_hi, m_hi, start=first and j == 0, stop=False)
                    pe.matmul(out, s_hi, m_lo, start=False, stop=False)
                    mm = pe.matmul(out, s_lo, m_hi, start=False, stop=last and j == len(terms) - 1)
                return mm

            def unit_ready(u):
                pe.wait_ge(S["lo_ready"], split_index[u] + 1)

            def features(key, u, c, k_tiles=DT, x=(h_hi, h_lo), n=T):
                out = dense.fill(pe, key)[:, 0:n]
                unit_ready(u)
                three(out, [(*weight(u, k_tiles, k, c), x[0][:, k, 0:n], x[1][:, k, 0:n]) for k in range(k_tiles)])\
                    .then_inc(dense.done, 1)
                release[u] = (dense.done, dense.at[key] + 1)

            def first_features(keys, u, ready):
                outs = [dense.fill(pe, key)[:, 0:T] for key in keys]
                unit_ready(u)
                for k in range(DT):
                    pe.wait_ge(S["h_ready"], ready + k + 1)
                    for i, out in enumerate(outs):
                        mm = three(out, [(*weight(u, DT, k, i * P), h_hi[:, k, :], h_lo[:, k, :])], k == 0, k == DT - 1)
                        if k == DT - 1:
                            mm.then_inc(dense.done, 1)
                release[u] = (dense.done, dense.at[keys[1]] + 1)

            def tokens(key, u, c, n, chunk, k_tiles=DT, x=(h_hi, h_lo), out=None, more=False, last=True):
                bk = dense.fill(pe, key) if out is None else out[0]
                at = 0 if out is None else out[1]
                unit_ready(u)
                terms = []
                for k in range(k_tiles):
                    w1, w2 = weight(u, k_tiles, k, c, n)
                    s = slice(chunk * P, chunk * P + P)
                    terms.append((x[0][:, k, s], x[1][:, k, s], w1, w2))
                for j, (s_hi, s_lo, m_hi, m_lo) in enumerate(terms):
                    pe.matmul(bk[:, at:at + n], s_hi, m_hi, start=j == 0, stop=False)
                    pe.matmul(bk[:, at:at + n], s_hi, m_lo, start=False, stop=False)
                    mm = pe.matmul(bk[:, at:at + n], s_lo, m_hi, start=False, stop=j == k_tiles - 1)
                if last:
                    mm.then_inc(dense.done, 1)
                    release[u] = (dense.done, dense.at[key] + 1)
                return bk

            def turn(ring, key, parts):
                bk = ring.fill(pe, key)
                for at, src in parts:
                    rows, cols = src.shape
                    tr = pe.transpose(bk[0:cols, at:at + rows], src, const[0:rows, 0:rows])
                tr.then_inc(ring.done, 1)

            def vada_columns(q):
                out = adas.fill(pe, ("vada", q))
                pe.wait_ge(S["vada_ready"], 2 * q + 2)
                for j in range(4):
                    for c in range(2):
                        part = vada_sum[:, (2 * q + j // 2) % 4, c, j % 2 * P:j % 2 * P + P]
                        mm = pe.matmul(out[:, 2 * j + c:2 * j + c + 1], part, ones[:, 0:1],
                                       start=j == 0 and c == 0, stop=True, skip_group_check=True)
                mm.then_inc(adas.done, 1)

            def modulation(place, pairs=None, between=None):
                for p in (ada_pairs(place) if pairs is None else pairs):
                    out = adas.fill(pe, ("ada", p))
                    for i in range(2):
                        u = number[(f"ada{p // 12}", 2 * (p % 12) + i)]
                        w = raw_unit(u)
                        for k in range(DT):
                            mm = pe.matmul(out[0:2, 256 * i:256 * i + 256], cond[:, k, :], w[:, k, :],
                                           start=i == 0 and k == 0, stop=k == DT - 1, skip_group_check=True)
                        if i == 0:
                            mark(mm, ("ada", p))
                            release[u] = (S["half_used"], marks[("ada", p)])
                            if between is not None:
                                between()
                                between = None
                    mm.then_inc(adas.done, 1)
                    release[u] = (adas.done, adas.at[("ada", p)] + 1)
                    if p % 2:
                        out = adas.fill(pe, ("mod", p // 2))
                        for j in range(8):
                            tr = pe.transpose(out[:, 2 * j:2 * j + 2],
                                              ada_row[:, j // 4, j % 4 * P:j % 4 * P + P], const[0:2, 0:2])
                        tr.then_inc(adas.done, 1)

            def stat(n):
                for i in range(2):
                    pe.wait_ge(S["sq_ready"], 2 * n + i + 1)
                    mm = pe.matmul(bank[4][:, 0:T], ones, sq[:, i, :], start=i == 0, stop=i == 1)
                mm.then_inc(S["stat_done"], 1)

            def out_projection(l, ready):
                first_features([("out", l, m) for m in range(2)], number[(f"out{l}", 0)], ready)
                for m in range(2, DT):
                    features(("out", l, m), number[(f"out{l}", m // 2)], m % 2 * P)

            def ffn(l, ready):
                first_features([("gate", l, 0), ("up", l, 0)], number[(f"up{l}", 0)], ready)
                for f in range(1, FT):
                    u = number[(f"up{l}", f)]
                    features(("gate", l, f), u, 0)
                    features(("up", l, f), u, P)
                    if l == 0 and f in vada_at_up:
                        vada_columns(vada_at_up[f])
                for m in range(DT):
                    out = dense.fill(pe, ("down", l, m))[:, 0:T]
                    for half in range(2):
                        u = number[(f"down{l}", 2 * m + half)]
                        unit_ready(u)
                        for k in range(11):
                            f = 11 * half + k
                            if m == 0:
                                pe.wait_ge(S["u_ready"], FT * l + f + 1)
                            mm = three(out, [(*weight(u, 11, k, 0), u_hi[:, f, :], u_lo[:, f, :])],
                                       f == 0, f == FT - 1)
                        if half == 0:
                            mark(mm, ("half", l, m))
                            release[u] = (S["half_used"], marks[("half", l, m)])
                    mm.then_inc(dense.done, 1)
                    release[u] = (dense.done, dense.at[("down", l, m)] + 1)
                    if l == 0 and m in vada_at_down:
                        vada_columns(vada_at_down[m])

            pe.wait_ge(S["const_in"], 16)
            pe.wait_ge(S["c_in"], 32)
            turn(misc, "cond", [(0, vec_rows[0:2 * DT, :])])
            misc.was_read(pe, "cond")
            modulation("start", range(0, 1))
            pe.wait_ge(S["x_in"], 32)
            for c in range(NCH):
                for g in range(2):
                    turn(dense, ("x", c, g), [(j * P, xtok[:, c, (4 * g + j) * P:(4 * g + j + 1) * P])
                                              for j in range(4)])
            pe.wait_ge(S["rows_in"], 16 * (len(ROWS) - 2))
            turn(misc, "vec", [(0, vec_rows[0:NROWS, :])])
            pe.wait_ge(S["adab_in"], 16)
            turn(misc, "ada_b", [(0, ada_rows[:, :])])
            pe.wait_ge(S["small_in"], 48)
            out = misc.fill(pe, "rowb")
            pe.matmul(out[:, 0:32], ones[0:1, :], row_in[:, :], start=True, stop=True).then_inc(misc.done, 1)
            modulation("start", range(1, 3))
            stat(0)
            modulation("start", range(3, 4))
            modulation("norm0")

            in0 = lambda c: (number[("in0", c // 256)], c % 256)
            first_features([("in0", 0), ("in0", 1)], number[("in0", 0)], 0)
            for j in range(2, 12):
                features(("in0", j), *in0(j * P))

            def level(i):
                pe.wait_ge(S["level_ready"], i + 1)
                for c in range(NCH):
                    out = misc.fill(pe, ("level", i, c))
                    for h in range(H):
                        mm = pe.matmul(out[:, h * P:(h + 1) * P], Kd[:, h, c * P:(c + 1) * P],
                                       Qd[:, h, c * P:(c + 1) * P], start=h == 0, stop=h == H - 1,
                                       skip_group_check=True)
                    mm.then_inc(misc.done, 1)

            def gate_step(j):
                if j == 6:
                    u = number[("gates", 0)]
                    out = dense.fill(pe, "gate_rows")
                    unit_ready(u)
                    mm = three(out[0:16, 0:T], [(*weight(u, DT, k, 0, 16), h_hi[:, k, :], h_lo[:, k, :])
                                                for k in range(DT)])
                    mm.then_inc(dense.done, 1)
                    release[u] = (dense.done, dense.at["gate_rows"] + 1)
                elif j == 7:
                    dense.was_read(pe, "gate_rows")
                    turn(dense, "gates", [(16 * c, gate_rows[:, c * P:(c + 1) * P]) for c in range(NCH)])
                elif j == 9:
                    tri_f, tri_b = cst("tri_f"), cst("tri_b")
                    pe.wait_ge(S["gates_log"], 1)
                    out = dense.fill(pe, "B")
                    for d, tri, order in ((0, tri_f, (0, 1, 2)), (1, tri_b, (0, 2, 1))):
                        for i, c in enumerate(order):
                            o = out[:, (c * 2 + d) * 4:(c * 2 + d) * 4 + 4]
                            if i == 2:
                                pe.matmul(o, ones, LF[:, order[1], d, :], start=False, stop=False,
                                          skip_group_check=True)
                            mm = pe.matmul(o, tri, LF[:, c, d, :], start=d == 0 and c == 0, stop=True,
                                           skip_group_check=True)
                    mm.then_inc(dense.done, 1)
                elif 10 <= j < 13:
                    c = j - 10
                    dense.was_read(pe, "B")
                    turn(dense, ("rows", c), [(k * P, GB[:, c, k, :]) for k in range(4)])
                elif j == 17:
                    turn(misc, "k_tok", [(h * P, km[:, h, 0:P]) for h in range(H)])

            def hgrn_end(j):
                if j == 15:
                    pe.wait_ge(S["kfin_ready"], 2)
                    for i, (src, c) in enumerate(((SF, 0), (PX, 0), (SF, 1), (PX, 2))):
                        turn(misc, ("kfin", i), [(h * P, src[:, h, c * P:(c + 1) * P]) for h in range(H)])
                elif j == 16:
                    for i, c in enumerate((0, 0, 1, 2)):
                        misc.was_read(pe, ("kfin", i))
                        out = misc.fill(pe, ("kv", i))
                        for h in range(H):
                            mm = pe.matmul(out[:, h * P:(h + 1) * P], kt4[i][:, h * P:(h + 1) * P],
                                           va[:, c, h * P:(h + 1) * P], start=h == 0, stop=h == H - 1,
                                           skip_group_check=True)
                        mm.then_inc(misc.done, 1)
                elif j == 17:
                    for c in range(NCH):
                        misc.was_read(pe, ("level", len(LEVELS) - 1, c))
                    for c in range(NCH):
                        if c == 1:
                            misc.was_read(pe, ("kv", 2))
                            misc.was_read(pe, ("kv", 3))
                            pe.wait_ge(S["qi_ready"], 2)
                        out = dense.fill(pe, ("hg_o", c))
                        for h in range(H):
                            o = out[:, h * P:(h + 1) * P]
                            t = slice(c * P, (c + 1) * P)
                            terms = [(va[:, c, h * P:(h + 1) * P], Am[:, c, h, :])]
                            if c:
                                terms.append(((S0 if c == 1 else S1)[:, 0, h, :], Qd[:, h, t]))
                                terms.append(((S1 if c == 1 else S0)[:, 1, h, :], Kd[:, h, t]))
                            for a, (s, m) in enumerate(terms):
                                mm = pe.matmul(o, s, m, start=h == 0 and a == 0,
                                               stop=h == H - 1 and a == len(terms) - 1, skip_group_check=True)
                        mm.then_inc(dense.done, 1)

            for j in range(6, 18):
                if j in (6, 7, 14, 15):
                    for c in range(NCH):
                        tokens(("in0v", j, c), number[("in0", j)], 0, 256, c)
                else:
                    features(("in0", 2 * j), number[("in0", j)], 0)
                    features(("in0", 2 * j + 1), number[("in0", j)], P)
                if j < 14:
                    level(j - 6)
                gate_step(j)
                hgrn_end(j)

            def mix_norm(kind, n0, place, squares):
                pairs = ada_pairs(place)
                for h in range(H):
                    modulation(place, pairs[h:h + 1])
                    pe.wait_ge(S["mo_sq"], n0 + h + 1)
                    out = misc.fill(pe, (kind, h))
                    pe.matmul(out[:, 0:T], ones, squares[:, h, :], start=True, stop=True).then_inc(misc.done, 1)

            mix_norm("hg_norm", 0, "hgrn_norm", hg_sq)

            def qk(h):
                bk = dense.fill(pe, ("qk", h))
                blocks = [(0, 0), (1, 1), (1, 2), (2, 2)]
                for i, (s, t) in enumerate(blocks):
                    mm = pe.matmul(bk[:, i * P:(i + 1) * P], km[:, h, s * P:(s + 1) * P], qm[:, h, t * P:(t + 1) * P],
                                   start=i == 0, stop=i == 3, skip_group_check=True)
                mm.then_inc(dense.done, 1)
                bk = dense.fill(pe, ("qk10", h))
                pe.matmul(bk[:, 0:P], km[:, h, 2 * P:3 * P], qm[:, h, P:2 * P], start=True, stop=True)\
                    .then_inc(dense.done, 1)

            def decays(j):
                h, d = j // 2, j % 2
                sel = ident[0:4, h:h + 1].to_broadcast([4, P])
                big = cst("big_f" if d == 0 else "big_b")
                bk = dense.fill(pe, ("M", j))
                M = row_M[:, d, :]
                other, masked = (M[:, 2 * P:T], (0, 1, 3)) if d == 0 else (M[:, P:2 * P], (0, 1, 2))
                pe.matmul(bk[:, 0:T], sel, M, start=True, stop=False, skip_group_check=True)
                pe.matmul(bk[:, T:512], sel, other, start=False, stop=False, skip_group_check=True)
                for i in masked:
                    mm = pe.matmul(bk[:, i * P:(i + 1) * P], ident, big, start=False, stop=i == masked[-1],
                                   skip_group_check=True)
                mm.then_inc(dense.done, 1)
                bk = misc.fill(pe, ("ss", j))
                pe.matmul(bk[:, 0:TL], sel, ss_row[:, d, :], start=True, stop=True).then_inc(misc.done, 1)

            def sums(j):
                h, d = j // 2, j % 2
                sel = ident[0:4, h:h + 1].to_broadcast([4, P])
                pe.wait_ge(S["A_ready"], j + 1)
                misc.was_read(pe, ("ss", j))
                a = Aw[:, j % 2, :]
                for key, lhs, st in ((("den", j), lambda c: ones,
                                      vec[:, ROWS["state_mlstm_n"][0] + 4 * d + h:][:, 0:1].to_broadcast([P, P])),
                                     (("num", j), lambda c: vb[:, c, h * P:(h + 1) * P], C0[:, d, h, :])):
                    bk = misc.fill(pe, key) if key[0] == "num" else dense.fill(pe, key)
                    pe.matmul(bk[:, 0:P], lhs(0), a[:, 0:P], start=True, stop=False, skip_group_check=True)
                    pe.matmul(bk[:, P:T], st, qs[j % 2], start=False, stop=False, skip_group_check=True)
                    if d == 0:
                        pe.matmul(bk[:, P:T], lhs(1), a[:, P:T], start=False, stop=False, skip_group_check=True)
                        mm = pe.matmul(bk[:, 2 * P:T], lhs(2), a[:, T:512], start=False, stop=True,
                                       skip_group_check=True)
                    else:
                        pe.matmul(bk[:, P:2 * P], lhs(1), a[:, P:2 * P], start=False, stop=False,
                                  skip_group_check=True)
                        pe.matmul(bk[:, 2 * P:T], lhs(2), a[:, 2 * P:T], start=False, stop=False,
                                  skip_group_check=True)
                        mm = pe.matmul(bk[:, P:2 * P], lhs(2), a[:, T:512], start=False, stop=True,
                                       skip_group_check=True)
                    mm.then_inc(misc.done if key[0] == "num" else dense.done, 1)
                    if key[0] == "den":
                        bk = misc.fill(pe, ("em", j))
                        pe.matmul(bk[:, 0:T], sel, row_B[:, d, :], start=True, stop=True).then_inc(misc.done, 1)
                pe.wait_ge(S["k_in_ready"], j + 1)
                bk = misc.fill(pe, ("C", j))
                pe.matmul(bk[:, 0:P], k_in[:, j % 2, :], vb[:, 0, h * P:(h + 1) * P], start=True, stop=True,
                          skip_group_check=True)
                at = 127 if d == 0 else 0
                pe.matmul(bk[0:1, P:2 * P], Ew[:, j % 2, at:at + 1], k_tok[:, h * P:(h + 1) * P],
                          start=False, stop=True, skip_group_check=True).then_inc(misc.done, 1)

            qk(0)
            pe.wait_ge(S["rows_done"], 2)
            pe.wait_ge(S["c0_in"], 16)
            decays(0)
            for j in range(2 * H):
                if j % 2 and j < 2 * H - 1:
                    qk(j // 2 + 1)
                if j < 2 * H - 1:
                    decays(j + 1)
                sums(j)
                modulation("mlstm", ada_pairs("mlstm")[j:j + 1])
            mix_norm("ml_norm", 4, "mlstm_norm", ml_sq)
            out_projection(0, 8)
            modulation("norm1", between=lambda: stat(1))
            ffn(0, 16)

            modulation("norm2", between=lambda: stat(2))
            in1 = lambda i: number[("in1", i)]
            first_features([("qc", 0), ("qc", 1)], in1(0), 24)
            for j in range(2, 4):
                features(("qc", j), in1(1), j % 2 * P)
            features(("kc",), in1(2), 0)
            bk = None
            for c in range(NCH):
                bk = tokens(("vc",), in1(2), P, P, c, out=None if c == 0 else (bk, P * c), last=c == 2)
            turn_s, turn_m = cst("swa_turn"), cst("mla_turn")

            def rotate(key, matrix, src):
                out = misc.fill(pe, key)
                pe.matmul(out[:, 0:TL], matrix, src, start=True, stop=True).then_inc(misc.done, 1)

            for j in range(3):
                features(("cq", j), in1(3 + j // 2), j % 2 * P)
            features(("ckv", 0), in1(4), P)
            features(("ckv", 1), in1(5), 0)
            features(("kr",), in1(5), 32)

            def norm_of(key, k_tiles, n0):
                out = misc.fill(pe, key)
                for k in range(k_tiles):
                    pe.wait_ge(S["cq_sq"], n0 + k + 1)
                    mm = pe.matmul(out[:, 0:T], ones, sq[:, k % 2, :], start=k == 0, stop=k == k_tiles - 1)
                    if k < k_tiles - 1:
                        mark(mm, (key, k))
                mm.then_inc(misc.done, 1)

            norm_of("cq_norm", 3, 0)
            norm_of("ckv_norm", 2, 3)
            for j in range(4):
                dense.was_read(pe, ("qc", j))
                rotate(("rot", j), turn_s, qc[:, j, P:T])
            dense.was_read(pe, ("kc",))
            rotate(("rot", 4), turn_s, kT[:, P:T])
            dense.was_read(pe, ("kr",))
            out = misc.fill(pe, ("rep",))
            pe.matmul(out[:, 0:T], cst("rep")[96:128, :], krr[96:128, :], start=True, stop=True).then_inc(misc.done, 1)
            misc.was_read(pe, ("rep",))
            rotate(("rot", 5), turn_m, kr4[:, P:T])
            pe.wait_ge(S["cache_in"], 16 * 7)
            turn(misc, ("cache",), [(0, cin_k[:]), (P, cin_r[:].rearrange("p a b -> p (a b)")),
                                    (2 * P, cin_c[:, 0:P]), (3 * P, cin_c[:, P:2 * P])])
            pe.wait_ge(S["cq_ready"], 3)
            for i in range(2):
                u = number[("uq", i)]
                for j in range(2):
                    features(("qn", 2 * i + j), u, j * P, 3, (cq_hi, cq_lo))
                features(("qr", i), u, 2 * P, 3, (cq_hi, cq_lo))
            for i in range(2):
                dense.was_read(pe, ("qr", i))
                rotate(("rot", 6 + i), turn_m, qr[:, i, P:T])
            pe.wait_ge(S["ckv_ready"], 2)
            misc.was_read(pe, ("cache",))
            for j in range(4):
                features(("kn", j), number[("uk", j // 2)], j % 2 * P, 2, (ckv_hi, ckv_lo), n=TK)
            for c in range(4):
                for i in range(2):
                    if i == 0:
                        bk = tokens(("vm", c), number[("uv", 0)], 0, 256, c, 2, (ckv_hi, ckv_lo), last=False)
                    else:
                        tokens(("vm", c), number[("uv", 1)], 0, 256, c, 2, (ckv_hi, ckv_lo), out=(bk, 256))
            release[number[("uv", 0)]] = release[number[("uv", 1)]]
            pe.wait_ge(S["cq_t"], 5)
            turn(misc, ("ctx_cache",), [(0, kT[:, 0:P]), (P, ckvf[:, 0, 0:P]), (2 * P, ckvf[:, 1, 0:P]),
                                        (3 * P, kr4[0:32, 0:P])])

            band = {1: cst("band0"), 2: cst("band1")}

            def scores(n, job):
                kind, heads, t, k0, nk = job
                if n == 0:
                    pe.wait_ge(S["roped"], 8)
                    dense.was_read(pe, ("vm", 3))
                    misc.was_read(pe, ("cache",))
                bk = dense.fill(pe, ("s", n))
                for i, h in enumerate(heads):
                    o = bk[:, i * nk:(i + 1) * nk]
                    tq = slice(t * P, (t + 1) * P)
                    if kind == "swa":
                        b = h // 4 * 64
                        mm = pe.matmul(o, qc[b:b + 64, h % 4, tq], kT[b:b + 64, k0:k0 + nk],
                                       start=i == 0, stop=t == 0, skip_group_check=True)
                        if t:
                            at = P if t == 1 else 0
                            mm = pe.matmul(bk[:, at:at + P], ident, band[t], start=False, stop=True,
                                           skip_group_check=True)
                    else:
                        b, r = h % 2 * 64, h % 4 * 32
                        if i:
                            pe_own[0] += 1
                            mm.then_inc(S["pe_own"], 1)
                            pe.wait_ge(S["pe_own"], pe_own[0])
                        pe.matmul(o, qn[b:b + 64, h // 2, tq], kn[b:b + 64, h // 2, k0:k0 + nk],
                                  start=i == 0, stop=False, skip_group_check=True)
                        mm = pe.matmul(o, qr[r:r + 32, h // 4, tq], kr4[r:r + 32, k0:k0 + nk],
                                       start=False, stop=True, skip_group_check=True,
                                       tile_position=(r, 0))
                mm.then_inc(dense.done, 1)

            def turned(n, job):
                kind, heads, t, k0, nk = job
                pe.wait_ge(S["p_ready"], n + 1)
                w = len(heads) * nk
                turn(misc, ("pT", n), [(i * P, pr[:, n % PR, i * P:(i + 1) * P]) for i in range(w // P)])

            def values(n, job):
                kind, heads, t, k0, nk = job
                misc.was_read(pe, ("pT", n))
                first, last = ends[n]
                if first:
                    pv_bank[0] = pvs.fill(pe, ("pv", job_tile[n]))
                for i, h in enumerate(heads):
                    b = h % 2 * 64
                    at = pv_at(n, h)
                    for k in range(nk // P):
                        chunk = k0 // P + k
                        v = (vt[:, chunk, h // 4 * 64:h // 4 * 64 + 64] if kind == "swa"
                             else vm[:, chunk, h * 64:h * 64 + 64])
                        mm = pe.matmul(pv_bank[0][b:b + 64, at:at + P], v,
                                       pT[:, n % 2, (i * nk + k * P):(i * nk + (k + 1) * P)],
                                       start=k == 0 and (i, at) in starts[n], stop=k == nk // P - 1,
                                       skip_group_check=True)
                if last:
                    mm.then_inc(pvs.done, 1)
                else:
                    mark(mm, ("pv", n))

            pv_bank = [None]
            pe_own = [0]
            for n in range(len(jobs) + VALUE_LAG):
                if n < len(jobs):
                    scores(n, jobs[n])
                if 0 <= n - TURN_LAG < len(jobs):
                    turned(n - TURN_LAG, jobs[n - TURN_LAG])
                if n >= VALUE_LAG:
                    values(n - VALUE_LAG, jobs[n - VALUE_LAG])
            for tile in dict.fromkeys(job_tile):
                pvs.was_read(pe, ("pv", tile))
            out_projection(1, 16)
            modulation("norm3", between=lambda: stat(3))
            ffn(1, 32)
            stat(4)
            for m in range(DT):
                pe.wait_ge(S["y_ready"], m + 1)
                turn(misc, ("y", m), [(c * P, ht[:, m % 2, c * P:(c + 1) * P]) for c in range(NCH)])

        @block.sync
        def _(sp):
            w = {"in0": I["w_in_even"][0], "in1": I["w_in_odd"][0], "out0": I["w_out_even"][0],
                 "out1": I["w_out_odd"][0], "uk": I["mla_w_uk"][0], "uv": I["mla_w_uv"][0],
                 "ada0": I["ada_w"][0], "ada1": I["ada_w"][1]}
            k_first = lambda a: a.rearrange("(k p) n -> p k n", p=P)
            sp.dma_start(const[:, 0:256], I["shape_constants"][:, 0:256]).then_inc(S["const_in"], 16)
            sp.wait_ge(S["c_in"], 32)
            for u, (name, i, kt, cols) in enumerate(units):
                if u == 2:
                    sp.dma_start(xtok[:, 0, :], I["x_prompt"][0]).then_inc(S["x_in"], 16)
                    sp.dma_start(xtok[:, 1:3, :], I["x_sample"][0].rearrange("(c p) d -> p c d", p=P))\
                        .then_inc(S["x_in"], 16)
                if u >= RAW:
                    last = u - RAW
                    if native[last]:
                        sp.wait_ge(*release[last])
                    else:
                        sp.wait_ge(S["lo_ready"], split_index[last] + 1)
                dst = raw[u % RAW][:, 0:kt * cols].rearrange("p (k n) -> p k n", k=kt)
                if name[:2] == "up":
                    l = int(name[2])
                    pieces_of = [(dst[:, :, 0:P], k_first(I["ffn_w1"][l])[:, :, i * P:(i + 1) * P]),
                                 (dst[:, :, P:2 * P], k_first(I["ffn_w3"][l])[:, :, i * P:(i + 1) * P])]
                elif name[:4] == "down":
                    rows = slice(i % 2 * 11 * P, (i % 2 + 1) * 11 * P)
                    pieces_of = [(dst, k_first(I["ffn_w2"][int(name[4])][rows, i // 2 * P:(i // 2 + 1) * P]))]
                elif name == "gates":
                    pieces_of = [(dst, k_first(I["w_in_even"][0])[:, :, WE - 16:WE])]
                elif name == "in1" and i < 2:
                    src = k_first(w["in1"])[:, :, 0:512].rearrange("p k (g j e) -> p k g j e", g=2, j=4)
                    to = dst.rearrange("p k (j g e) -> p k g j e", j=2, g=2)
                    pieces_of = [(to[:, :, g, j], src[:, :, g, 2 * i + j]) for g in range(2) for j in range(2)]
                elif name == "uq":
                    src = k_first(I["mla_w_uq"][0])[:, :, i * 384:(i + 1) * 384].rearrange("p k (h e) -> p k h e", h=4)
                    heads = lambda a: a.rearrange("p (h e) -> p h e", h=4)
                    pieces_of = [(heads(dst[:, k, 0:256]), src[:, k, :, 0:64]) for k in range(3)]
                    pieces_of += [(heads(dst[:, k, 256:384]), src[:, k, :, 64:96]) for k in range(3)]
                else:
                    pieces_of = [(dst, k_first(w[name])[:, :, i * 256:i * 256 + cols])]
                assert len(pieces_of) == pieces[u]
                for to, src in pieces_of:
                    if name == "uq" or (name == "in1" and i < 2):
                        with nc.allow_non_contiguous_dma(reason="short runs of heads"):
                            sp.dma_start(to, src).then_inc(raw_in[u % RAW], 16)
                    else:
                        sp.dma_start(to, src).then_inc(raw_in[u % RAW], 16)

        @block.gpsimd
        def _(pool):
            for s, u in enumerate(split_units):
                n = units[u][2] * units[u][3]
                pool.wait_ge(S["hi_ready"], s + 1)
                pool.tensor_tensor(w_lo[s % SPLIT][:, 0:n], raw[u % RAW][:, 0:n],
                                   w_hi[s % SPLIT][:, 0:n].bitcast(F32), ALU.subtract).then_inc(S["lo_ready"], 1)

        @block.scalar
        def _(act):
            own = [0]
            split_at = [0]

            def step(ins):
                own[0] += 1
                ins.then_inc(S["act_own"], 1)
                act.wait_ge(S["act_own"], own[0])

            def split_to(end):
                while split_at[0] < min(end, len(split_units)):
                    s = split_at[0]
                    u = split_units[s]
                    n = units[u][2] * units[u][3]
                    act.wait_ge(raw_in[u % RAW], raw_need[u])
                    if s >= SPLIT:
                        act.wait_ge(*release[split_units[s - SPLIT]])
                    act.activation(w_hi[s % SPLIT][:, 0:n], raw[u % RAW][:, 0:n], ACT.Copy)\
                        .then_inc(S["hi_ready"], 1)
                    split_at[0] += 1

            def ahead(name, i, last=None):
                s = split_index[number[(name, i)]]
                split_to(min(s + SPLIT, last if last is not None else s + SPLIT))

            def end_of(name, n):
                return split_index[number[(name, n - 1)]] + 1

            def evacuate(ring, key, dst, src, func=ACT.Copy, **kw):
                bk = ring.filled(act, key)
                act.activation(dst, src(bk), func, **kw).then_inc(ring.read(key), 1)

            def square(src, i):
                act.activation(sq[:, i % 2, :], src, ACT.Square).then_inc(S["cq_sq"], 1)

            def norm(n, base):
                act.activation(table_col[:, :], eps_col[:, :], ACT.Ln)
                act.wait_ge(S["stat_done"], n + 1)
                act.activation(rstd[:, 0, :], bank[4][:, 0:T], ACT.Ln, bias=eps_col[:, :], scale=1.0 / D)\
                    .then_inc(S["stat_read"], 1)
                act.wait_ge(S["stat_read"], n + 1)
                act.activation(rstd[:, 0, :], rstd[:, 0, :], ACT.Exp, scale=-0.5).then_inc(S["rstd_ready"], 1)
                if n == 0:
                    split_to(SPLIT)
                if n < 4:
                    l, k = n // 2, 3 * (n % 2)
                    for m in range(DT):
                        act.wait_ge(S["ht_ready"], base + m + 1)
                        for c, a, b in ((1, 0, TC), (0, TC, T)):
                            ins = act.activation(h_hi[:, m, a:b], ht[:, m % 2, a:b], ACT.Identity,
                                                 bias=mod[:, l, 8 * k + m, c:c + 1])
                        ins.then_inc(S["hhi_ready"], 1)

            def out_projection(l, n):
                for m in range(DT):
                    ahead(f"out{l}", m // 2, end_of(f"up{l}", FT))
                split_to(split_index[number[(f"up{l}", 0)]] + SPLIT)

            def fetch_vada(step_key):
                if step_key in fetch_at:
                    n = fetch_at[step_key]
                    if n >= 2:
                        act.wait_ge(S["vada_ready"], n - 1)
                    p = first_vada + n // 2
                    at = 256 * (2 * (p % 12) + n % 2)
                    act.dma_start(vada_raw[:, n % 2, :].rearrange("p (k n) -> p k n", k=DT),
                                  I["ada_w"][p // 12].rearrange("(k p) n -> p k n", p=P)[:, :, at:at + 256])\
                        .then_inc(vada_in[n % 2], 16)

            def ffn(l, n):
                end = end_of(f"up{l}", FT)
                for f in range(FT):
                    ahead(f"up{l}", f)
                    if l == 0:
                        fetch_vada(("up", f))
                    bk = dense.filled(act, ("gate", l, f))
                    if f >= 2:
                        dense.was_read(act, ("up", l, f - 2))
                    act.activation(sa[:, f % 2, :], bk[:, 0:T], ACT.Silu).then_inc(dense.read(("gate", l, f)), 1)
                    dense.was_read(act, ("up", l, f))
                    act.activation(u_hi[:, f, :], uf[:, f % 2, :], ACT.Copy).then_inc(S["uhi_ready"], 1)
                for m in range(DT):
                    if l == 0:
                        fetch_vada(("down", m))
                    split_to(split_index[number[(f"down{l}", 2 * m + 1)]] + SPLIT)
                split_to(end_of(f"down{l}", 16) + SPLIT)

            def load_rows(name):
                at, k = ROWS[name]
                a = I[name]
                src = {1: lambda: a.rearrange("(r e) -> r e", e=P),
                       2: lambda: a.rearrange("n (r e) -> (n r) e", e=P),
                       3: lambda: a.rearrange("n d (r e) -> (n d r) e", e=P),
                       5: lambda: a.rearrange("b n d h e -> (b n d h) e")}[len(a.shape)]()
                act.dma_start(vec_rows[at:at + k, :], src)\
                    .then_inc(S["c_in" if name in ("c", "c_ctx") else "rows_in"], 16)

            load_rows("c")
            load_rows("c_ctx")
            bk = misc.filled(act, "cond")
            act.activation(cond[:, :, :], bk[:, 0:2 * DT].rearrange("p (c k) -> p k c", c=2), ACT.Silu)\
                .then_inc(misc.read("cond"), 1)
            for name in list(ROWS)[2:]:
                load_rows(name)
            act.dma_start(ada_rows[:, :], I["ada_b"].rearrange("l (r e) -> (l r) e", e=P)).then_inc(S["adab_in"], 16)
            act.dma_start(row_in[:, 0:8], I["swa_sink"]).then_inc(S["small_in"], 16)
            act.dma_start(row_in[:, 8:24], I["mlstm_gate_bias"].rearrange("n k h -> n (k h)"))\
                .then_inc(S["small_in"], 16)
            act.dma_start(row_in[:, 24:32], I["state_mlstm_m"].rearrange("b n d h -> (b n) (d h)"))\
                .then_inc(S["small_in"], 16)

            for c in range(NCH):
                for g in range(2):
                    dense.was_read(act, ("x", c, g))
            act.wait_ge(S["bounds_ready"], 1)
            act.activation(bound_exp[:, 0:2, :], bound_exp[:, 0:2, :], ACT.Exp).then_inc(S["bounds_exp"], 1)
            split_to(1)
            norm(0, 0)

            act.dma_start(const[:, 256:NCONST], I["shape_constants"][:, 256:NCONST]).then_inc(S["rest_in"], 16)
            act.dma_start(S0[:], I["state_hgrn"].rearrange("b n d h k v -> k (b n d) h v")).then_inc(S["state_in"], 16)
            act.dma_start(C0[:], I["state_mlstm_c"].rearrange("b n d h k v -> k (b n d) h v"))\
                .then_inc(S["c0_in"], 16)
            with nc.allow_non_contiguous_dma(reason="eight values"):
                act.dma_start(m0_col[:, :], I["state_mlstm_m"].rearrange("b n d h -> h (b n d)"))\
                    .then_inc(S["m0_in"], 16)

            for j in range(12):
                ahead("in0", j // 2)
                bk = dense.filled(act, ("in0", j))
                h = j % 4
                dst, f = ((q, ACT.Silu), (PF, ACT.Sigmoid), (SI, ACT.Sigmoid))[j // 4]
                act.activation(dst[:, h, :], bk[:, 0:T], f).then_inc(dense.read(("in0", j)), 1)
            for j in range(6, 18):
                ahead("in0", j)
                if j == 7:
                    evacuate(dense, "gate_rows", gate_rows, lambda b: b[0:16, 0:T])
                if j == 16:
                    act.wait_ge(S["kfin_ready"], 2)
                if j in (6, 7, 14, 15):
                    dst = va if j < 8 else vb
                    for c in range(NCH):
                        evacuate(dense, ("in0v", j, c), dst[:, c, j % 2 * 256:j % 2 * 256 + 256], lambda b: b[:, 0:256])
                else:
                    for i in (2 * j, 2 * j + 1):
                        dst, f, sc = {4: (ga, ACT.Silu, 1.0), 5: (qm, ACT.Copy, P ** -0.5), 6: (km, ACT.Copy, 1.0),
                                      8: (ob, ACT.Sigmoid, 1.0)}[i // 4]
                        evacuate(dense, ("in0", i), dst[:, i % 4, :], lambda b: b[:, 0:T], f, scale=sc)
                if j == 8:
                    G5 = G.rearrange("p c (d k h) -> p c d k h", d=2, k=2)
                    act.wait_ge(S["gates_ready"], 1)
                    step(act.activation(LE, G5[:, :, :, 1, :], ACT.Abs))
                    step(act.activation(LE, LE, ACT.Exp, scale=-1.0))
                    act.activation(LE, LE, ACT.Ln, bias=1.0).then_inc(S["gates_abs"], 1)
                elif j == 15:
                    act.wait_ge(S["qi_ready"], 2)
                    for i in range(4):
                        evacuate(misc, ("kfin", i), kt4[i], lambda b: b[:, :])
                elif j == 16:
                    for i in range(2):
                        bk = misc.filled(act, ("kv", i))
                        act.activation(Sout[:, i, :, :], bk[:, :].rearrange("p (h v) -> p h v", h=H), ACT.Copy)\
                            .then_inc(misc.read(("kv", i)), 1)
                    misc.was_read(act, ("kv", 1))
                    act.dma_start(O[2].rearrange("b n d h k v -> k (b n d) h v"), Sout).then_inc(S["s_out"], 16)
            split_to(split_index[number[("out0", 0)]] + SPLIT)
            misc.was_read(act, ("kv", 3))
            evacuate(misc, "k_tok", k_tok, lambda b: b[:, :])

            def head_rms(kind, src, squares):
                for h in range(H):
                    act.activation(squares[:, h, :], src[:, h, :], ACT.Square).then_inc(S["mo_sq"], 1)
                for h in range(H):
                    bk = misc.filled(act, (kind, h))
                    act.activation(squares[:, h, :], bk[:, 0:T], ACT.Ln, bias=eps_col[:, :], scale=1.0 / P)\
                        .then_inc(misc.read((kind, h)), 1)
                for h in range(H):
                    misc.was_read(act, (kind, h))
                    act.activation(squares[:, h, :], squares[:, h, :], ACT.Exp, scale=-0.5)\
                        .then_inc(S["mo_rstd"], 1)

            def head_high(h, base):
                act.wait_ge(S["ht_ready"], base + h + 1)
                act.activation(h_hi[:, base - 8 + h, :], ht[:, h % 2, :], ACT.Copy).then_inc(S["hhi_ready"], 1)

            act.wait_ge(S["rows_m"], 2)
            with nc.allow_non_contiguous_dma(reason="eight values"):
                act.dma_start(O[5].rearrange("b n d h -> h (b n d)"), m_out).then_inc(S["m_sent"], 16)
            step(act.activation(row_B, row_B, ACT.Exp, scale=-1.0))
            for d in range(2):
                act.activation(ss_row[:, d, :], row_M[:, d, P:T], ACT.Exp, scale=-1.0, bias=m0_col[:, d:d + 1])\
                    .then_inc(S["rows_done"], 1)
            for c in range(NCH):
                dense.was_read(act, ("hg_o", c))
            head_rms("hg_norm", o_hg, hg_sq)

            def take_qk(h):
                if h >= 2:
                    act.wait_ge(S["A_ready"], 2 * (h - 1))
                evacuate(dense, ("qk", h), QK[:, h % 2, 0:512], lambda b: b[:, :])
                evacuate(dense, ("qk10", h), QK[:, h % 2, 512:640], lambda b: b[:, 0:P])

            def decays(j):
                h, d = j // 2, j % 2
                bk = dense.filled(act, ("M", j))
                if j >= 2:
                    act.wait_ge(S["k_in_ready"], j - 1)
                    misc.filled(act, ("C", j - 2))
                cuts = (0, P, T, 512) if d == 0 else (0, P, 2 * P, 512)
                for c in range(NCH):
                    e = act.activation(Ew[:, j % 2, cuts[c]:cuts[c + 1]], bk[:, cuts[c]:cuts[c + 1]], ACT.Exp,
                                       scale=-1.0, bias=GB[:, c, d, h:h + 1])
                e.then_inc(dense.read(("M", j)), 1)

            take_qk(0)
            decays(0)
            for j in range(2 * H):
                h, d = j // 2, j % 2
                if j % 2 and j < 2 * H - 1:
                    take_qk(h + 1)
                if j < 2 * H - 1:
                    decays(j + 1)
                if j:
                    act.wait_ge(S["h_done"], j)
                evacuate(dense, ("den", j), den, lambda b: b[:, 0:T], ACT.Abs)
                evacuate(misc, ("em", j), em, lambda b: b[:, 0:T])
                bk = misc.filled(act, ("C", j))
                act.activation(Cout[:, d, h, :], bk[:, 0:P], ACT.Copy)
                act.activation(n_out[:, d, h, :], bk[0:1, P:2 * P], ACT.Copy).then_inc(misc.read(("C", j)), 1)
                if d:
                    head_high(h, 8)
            misc.was_read(act, ("C", 7))
            act.dma_start(O[3].rearrange("b n d h k v -> k (b n d) h v"), Cout).then_inc(S["c_sent"], 16)
            act.dma_start(O[4].rearrange("b n d h k -> (b n) d h k"), n_out).then_inc(S["c_sent"], 16)
            act.wait_ge(S["h_done"], 8)
            head_rms("ml_norm", hm, ml_sq)
            for h in range(H):
                head_high(h, 12)
            out_projection(0, 1)
            norm(1, 16)
            act.wait_ge(S["s_out"], 16)
            act.wait_ge(S["m_sent"], 16)
            act.wait_ge(S["c_sent"], 32)
            ffn(0, 2)

            cache = [(cin_k[:], I["cache_swa_k"].rearrange("b n t h e -> (b n t) (h e)")),
                     (vt[:, 3, :], I["cache_swa_v"].rearrange("b n t h e -> (b n t) (h e)")),
                     (cin_c[:], I["cache_mla_ckv"].rearrange("b n t e -> (b n t) e"))]
            cache += [(cin_r[:, i, :], I["cache_mla_krope"].rearrange("b n t e -> (b n t) e")) for i in range(4)]
            adas.filled(act, ("vada", VADA // 2 - 1))
            for dst, src in cache:
                act.dma_start(dst, src).then_inc(S["cache_in"], 16)
            norm(2, 24)
            end = end_of("uv", 2)
            for j in range(4):
                ahead("in1", j // 2, end)
                evacuate(dense, ("qc", j), qc[:, j, :], lambda b: b[:, 0:T])
            ahead("in1", 2, end)
            evacuate(dense, ("kc",), kT[:, 0:T], lambda b: b[:, 0:T])
            evacuate(dense, ("vc",), vt[:, 0:3, :], lambda b: b[:, 0:T].rearrange("p (c e) -> p c e", c=3))
            for j in range(3):
                ahead("in1", 3 + j // 2, end)
                evacuate(dense, ("cq", j), cqf[:, j, :], lambda b: b[:, 0:T])
            evacuate(dense, ("ckv", 0), ckvf[:, 0, :], lambda b: b[:, 0:T])
            ahead("in1", 5, end)
            evacuate(dense, ("ckv", 1), ckvf[:, 1, :], lambda b: b[:, 0:T])
            evacuate(dense, ("kr",), krr[96:128, :], lambda b: b[96:128, 0:T])
            low_rank = (("cq_norm", cqf, 3), ("ckv_norm", ckvf, 2))
            for i, (key, src, k_tiles) in enumerate(low_rank):
                for k in range(k_tiles):
                    if k == 2:
                        act.wait_ge(S["half_used"], marks[(key, 0)])
                    dense.was_read(act, (("cq", "ckv")[i], k))
                    if i == 1 and k == 0:
                        misc.filled(act, "cq_norm")
                    square(src[:, k, :], k)
            for i, (key, src, k_tiles) in enumerate(low_rank):
                bk = misc.filled(act, key)
                act.activation(rstd[:, i, :], bk[:, 0:T], ACT.Ln, bias=eps_col[:, :], scale=1.0 / (k_tiles * P))\
                    .then_inc(misc.read(key), 1)
            for i, (key, src, k_tiles) in enumerate(low_rank):
                misc.was_read(act, key)
                act.activation(rstd[:, i, :], rstd[:, i, :], ACT.Exp, scale=-0.5).then_inc(S["cq_rstd"], 1)
            evacuate(misc, ("rep",), kr4[:, 0:T], lambda b: b[:, 0:T])
            for k in range(5):
                act.wait_ge(S["cq_t"], k + 1)
                dst, src = (cq_hi[:, k, :], cqf[:, k, :]) if k < 3 else (ckv_hi[:, k - 3, 0:T], ckvf[:, k - 3, :])
                act.activation(dst, src, ACT.Copy).then_inc(S["cqhi"], 1)
            bk = misc.filled(act, ("cache",))
            act.activation(kT[:, T:TK], bk[:, 0:P], ACT.Copy)
            act.activation(kr4[:, T:TK], bk[:, P:2 * P], ACT.Copy)
            act.activation(ckv_hi[:, :, T:TK], bk[:, 2 * P:512].rearrange("p (k t) -> p k t", k=2), ACT.Copy)\
                .then_inc(S["cache_ready"], 1)
            for i in range(2):
                ahead("uq", i, end)
                for j in range(2):
                    evacuate(dense, ("qn", 2 * i + j), qn[:, 2 * i + j, :], lambda b: b[:, 0:T])
                evacuate(dense, ("qr", i), qr[:, i, :], lambda b: b[:, 0:T])
            for j in range(4):
                ahead("uk", j // 2, end)
                evacuate(dense, ("kn", j), kn[:, j, :], lambda b: b[:, :])
            split_to(end)
            for c in range(4):
                evacuate(dense, ("vm", c), vm[:, c, :], lambda b: b[:, :])
            bk = misc.filled(act, ("ctx_cache",))
            act.activation(out_k[:], bk[:, 0:P], ACT.Copy)
            act.activation(out_c[:], bk[:, P:3 * P], ACT.Copy)
            act.activation(out_r[:], bk[:, 3 * P:3 * P + 32], ACT.Copy).then_inc(misc.read(("ctx_cache",)), 1)
            misc.was_read(act, ("ctx_cache",))
            act.dma_start(O[6].rearrange("b n t h e -> (b n t) (h e)"), out_k[:]).then_inc(S["odd_sent"], 16)
            act.dma_start(O[7].rearrange("b n t h e -> (b n t) (h e)"), vt[:, 0, :]).then_inc(S["odd_sent"], 16)
            act.dma_start(O[8].rearrange("b n t e -> (b n t) e"), out_c[:]).then_inc(S["odd_sent"], 16)
            act.dma_start(O[9].rearrange("b n t e -> (b n t) e"), out_r[:]).then_inc(S["odd_sent"], 16)

            for n in range(len(jobs) + VALUE_LAG):
                if n in (3, 5):
                    split_to(split_index[number[("out1", 0)]] + (n - 1) // 2)
                m = n - TURN_LAG
                if 0 <= m < len(jobs):
                    w = len(jobs[m][1]) * jobs[m][4]
                    if m >= 2:
                        if ("pv", m - 2) in marks:
                            act.wait_ge(S["half_used"], marks[("pv", m - 2)])
                        else:
                            pvs.filled(act, ("pv", job_tile[m - 2]))
                    evacuate(misc, ("pT", m), pT[:, m % 2, 0:w], lambda b: b[:, 0:w])
                if n < len(jobs):
                    kind, heads, t, k0, nk = jobs[n]
                    scale = 64 ** -0.5 if kind == "swa" else 96 ** -0.5
                    s_, pr_ = st[:, n % PR], pr[:, n % PR]
                    act.wait_ge(S["neg_max"], n + 1)
                    if n >= PR:
                        misc.filled(act, ("pT", n - PR))
                    bk = dense.filled(act, ("s", n))
                    for i in range(len(heads)):
                        e = act.activation(pr_[:, i * nk:(i + 1) * nk], bk[:, i * nk:(i + 1) * nk], ACT.Exp,
                                           scale=scale, bias=s_[:, 1, i:i + 1], accum_out=s_[:, 2, i:i + 1])
                    if kind == "swa":
                        e = act.activation(s_[:, 3, 0:len(heads)], s_[:, 3, 0:len(heads)], ACT.Exp)
                    e.then_inc(dense.read(("s", n)), 1)
                m = n - VALUE_LAG
                if m >= 0 and ends[m][1]:
                    bk = pvs.filled(act, ("pv", job_tile[m]))
                    act.activation(mix_part(h_hi, job_tile[m]), mix_bank(bk, job_tile[m]), ACT.Copy)\
                        .then_inc(S["pv_hi"], 1)
            out_projection(1, 3)
            norm(3, 32)
            act.wait_ge(S["odd_sent"], 64)
            ffn(1, 4)
            norm(4, 0)
            for m in range(DT):
                evacuate(misc, ("y", m), xtok[:, :, m * P:(m + 1) * P],
                         lambda b: b[:, 0:T].rearrange("p (c e) -> p c e", c=NCH))
                if m % 4 == 3:
                    for i in range(m - 3, m + 1):
                        misc.was_read(act, ("y", i))
                    f = slice((m - 3) * P, (m + 1) * P)
                    act.dma_start(O[0][0][:, f], xtok[:, 0, f]).then_inc(S["y_sent"], 16)
                    act.dma_start(O[1][0].rearrange("(c p) d -> p c d", p=P)[:, :, f], xtok[:, 1:3, f])\
                        .then_inc(S["y_sent"], 16)
            act.wait_ge(S["y_sent"], 64)

        @block.vector
        def _(dve):
            own = [0]
            col = lambda name, i=None: (vec[:, ROWS[name][0]:ROWS[name][0] + ROWS[name][1]] if i is None
                                        else vec[:, ROWS[name][0] + i:ROWS[name][0] + i + 1])

            def step(ins):
                own[0] += 1
                ins.then_inc(S["dve_own"], 1)
                dve.wait_ge(S["dve_own"], own[0])

            def modulation(place, pairs=None):
                for p in (ada_pairs(place) if pairs is None else pairs):
                    bk = adas.filled(dve, ("ada", p))
                    dve.tensor_copy(ada_row[:, p % 2, :], bk[0:2, :]).then_inc(adas.read(("ada", p)), 1)
                    if p % 2:
                        l, g = p // 12, p % 12 // 2
                        bk = adas.filled(dve, ("mod", p // 2))
                        dve.tensor_tensor(mod[:, l, 8 * g:8 * g + 8, :], bk[:, 0:16].rearrange("p (j c) -> p j c", c=2),
                                          ada_b_col[:, 48 * l + 8 * g:48 * l + 8 * g + 8].unsqueeze(2)
                                          .to_broadcast([P, 8, 2]), ALU.add).then_inc(adas.read(("mod", p // 2)), 1)
                        adas.was_read(dve, ("mod", p // 2))

            def gains(n):
                l, k = n // 2, 1 + 3 * (n % 2)
                step(dve.tensor_scalar(gain[:, n], mod[:, l, 8 * k:8 * k + 8, :], 1.0, None, ALU.add))
                g = vec[:, ROWS[f"norm{n % 2 + 1}_g"][0] + 8 * l:][:, 0:8]
                step(dve.tensor_tensor(gain[:, n], gain[:, n], g.unsqueeze(2).to_broadcast([P, 8, 2]), ALU.mult))

            def norm(n, base, place):
                l, k = n // 2, 3 * (n % 2)

                def low(m):
                    dve.wait_ge(S["hhi_ready"], base + m + 1)
                    for c, a, b in ((1, 0, TC), (0, TC, T)):
                        ins = dve.scalar_tensor_tensor(h_lo[:, m, a:b], ht[:, m % 2, a:b], mod[:, l, 8 * k + m, c:c + 1],
                                                       h_hi[:, m, a:b].bitcast(F32), ALU.add, ALU.subtract)
                    ins.then_inc(S["h_ready"], 1)

                gains(n)
                dve.wait_ge(S["rstd_ready"], n + 1)
                for m in range(DT):
                    if m >= 2:
                        dve.wait_ge(S["h_ready"], base + m - 1)
                    for c, a, b in ((1, 0, TC), (0, TC, T)):
                        ins = dve.scalar_tensor_tensor(ht[:, m % 2, a:b], X[:, m, a:b], gain[:, n, m, c:c + 1],
                                                       rstd[:, 0, a:b], ALU.mult, ALU.mult)
                    ins.then_inc(S["ht_ready"], 1)
                    if m:
                        low(m - 1)
                    modulation(place, ada_pairs(place)[m:m + 1])
                low(DT - 1)

            def add_squares(n, m):
                if m == 0:
                    step(dve.tensor_tensor(sq[:, 0, :], X[:, 0, :], X[:, 0, :], ALU.mult))
                elif m < DT - 1:
                    step(dve.tensor_tensor(sq[:, 1, :], X[:, m, :], X[:, m, :], ALU.mult))
                    ins = dve.tensor_tensor(sq[:, 0, :], sq[:, 0, :], sq[:, 1, :], ALU.add)
                    if m < DT - 2:
                        step(ins)
                    else:
                        ins.then_inc(S["sq_ready"], 1)
                        dve.wait_ge(S["sq_ready"], 2 * n + 1)
                else:
                    dve.tensor_tensor(sq[:, 1, :], X[:, m, :], X[:, m, :], ALU.mult).then_inc(S["sq_ready"], 1)

            def residual(key, n, l, m, k):
                bk = dense.filled(dve, key)
                for c, a, b in ((1, 0, TC), (0, TC, T)):
                    ins = dve.scalar_tensor_tensor(X[:, m, a:b], bk[:, a:b], mod[:, l, 8 * k + m, c:c + 1],
                                                   X[:, m, a:b], ALU.mult, ALU.add)
                ins.then_inc(dense.read(key), 1)
                dense.was_read(dve, key)
                add_squares(n, m)

            def vada_product(n):
                w = vada_raw[:, n % 2, :].rearrange("p (k n) -> p k n", k=DT)
                dve.wait_ge(vada_in[n % 2], 16 * (n // 2 + 1))
                if n >= 4:
                    adas.filled(dve, ("vada", (n - 4) // 2))
                for k in range(DT):
                    for c in range(2):
                        total = vada_sum[:, n % 4, c, :]
                        done = 2 * DT * n + 2 * k + c
                        if k == 0:
                            dve.tensor_scalar(total, w[:, k, :], cond[:, k, c:c + 1], None, ALU.mult)\
                                .then_inc(S["vada_part"], 1)
                        else:
                            dve.wait_ge(S["vada_part"], done - 1)
                            ins = dve.scalar_tensor_tensor(total, w[:, k, :], cond[:, k, c:c + 1], total,
                                                           ALU.mult, ALU.add)
                            ins.then_inc(S["vada_part"], 1)
                dve.wait_ge(S["vada_part"], 2 * DT * (n + 1))
                dve.engine_nop().then_inc(S["vada_ready"], 1)

            def vada_bias(q):
                p = first_vada + q
                l, t = p // 12, 4 * (p % 12)
                bk = adas.filled(dve, ("vada", q))
                dve.tensor_tensor(mod[:, l, t:t + 4, :], bk[:, 0:8].rearrange("p (j c) -> p j c", c=2),
                                  ada_b_col[:, 48 * l + t:48 * l + t + 4].unsqueeze(2).to_broadcast([P, 4, 2]),
                                  ALU.add).then_inc(adas.read(("vada", q)), 1)
                adas.was_read(dve, ("vada", q))

            def ffn(l):
                def low_u(f):
                    dve.wait_ge(S["uhi_ready"], FT * l + f + 1)
                    dve.tensor_tensor(u_lo[:, f, :], uf[:, f % 2, :], u_hi[:, f, :].bitcast(F32), ALU.subtract)\
                        .then_inc(S["u_ready"], 1)
                for f in range(FT):
                    dense.was_read(dve, ("gate", l, f))
                    bk = dense.filled(dve, ("up", l, f))
                    if f >= 2:
                        dve.wait_ge(S["u_ready"], FT * l + f - 1)
                    dve.tensor_tensor(uf[:, f % 2, :], sa[:, f % 2, :], bk[:, 0:T], ALU.mult)\
                        .then_inc(dense.read(("up", l, f)), 1)
                    if f:
                        low_u(f - 1)
                    if l == 0:
                        if f in VADA_AT_UP:
                            vada_product(VADA_AT_UP[f])
                        if f in vada_at_up:
                            vada_bias(vada_at_up[f])
                low_u(FT - 1)
                for m in range(DT):
                    if l == 0:
                        vada_product(VADA_AT_DOWN[m])
                    residual(("down", l, m), 2 * l + 2, l, m, 5)
                    if l == 0 and m in vada_at_down:
                        vada_bias(vada_at_down[m])

            dve.memset(eps_col[:, :], EPS).then_inc(S["dve_own"], 1)
            own[0] += 1
            modulation("start", range(0, 1))
            for c in range(NCH):
                for g in range(2):
                    bk = dense.filled(dve, ("x", c, g))
                    dve.tensor_copy(X[:, 4 * g:4 * g + 4, c * P:(c + 1) * P],
                                    bk[:, :].rearrange("p (j t) -> p j t", j=4)).then_inc(dense.read(("x", c, g)), 1)
            bk = misc.filled(dve, "vec")
            dve.tensor_copy(vec[:, :], bk[:, 0:NROWS]).then_inc(misc.read("vec"), 1)
            bk = misc.filled(dve, "ada_b")
            dve.tensor_copy(ada_b_col[:, :], bk[:, 0:96]).then_inc(misc.read("ada_b"), 1)
            bk = misc.filled(dve, "rowb")
            dve.tensor_copy(rowb[:, :], bk[:, 0:32]).then_inc(misc.read("rowb"), 1)
            misc.was_read(dve, "rowb")
            step(dve.tensor_scalar(neg_sink[:, :], rowb[:, 0:8], -1.0, None, ALU.mult))
            modulation("start", range(1, 2))
            dense.was_read(dve, ("x", NCH - 1, 1))
            for m in range(DT):
                add_squares(0, m)
            b0, b1 = col("hgrn_lower_bounds")[:, 0:8], col("hgrn_lower_bounds")[:, 8:16]
            step(dve.tensor_tensor(bound_exp[:, 2, :], b0, b1, ALU.max))
            dve.tensor_tensor(bound_exp[:, 0, :], b0, bound_exp[:, 2, :], ALU.subtract)
            dve.tensor_tensor(bound_exp[:, 1, :], b1, bound_exp[:, 2, :], ALU.subtract).then_inc(S["bounds_ready"], 1)
            dve.wait_ge(S["bounds_exp"], 1)
            step(dve.tensor_tensor(bound_exp[:, 2, :], bound_exp[:, 0, :], bound_exp[:, 1, :], ALU.add))
            step(dve.reciprocal(bound_exp[:, 2, :], bound_exp[:, 2, :]))
            step(dve.tensor_tensor(lb[:, :], bound_exp[:, 0, :], bound_exp[:, 2, :], ALU.mult))
            step(dve.tensor_scalar(oml[:, :], lb[:, :], -1.0, 1.0, ALU.mult, ALU.add))
            modulation("start", range(2, 4))
            norm(0, 0, "norm0")

            for d, (f, k) in enumerate(((PF, kf), (SI, kb))):
                for h in range(H):
                    j = 4 * d + h
                    dense.was_read(dve, ("in0", 4 + j))
                    step(dve.tensor_scalar(f[:, h, :], f[:, h, :], oml[:, j:j + 1], lb[:, j:j + 1], ALU.mult, ALU.add))
                    step(dve.tensor_scalar(k[:, h, :], f[:, h, :], -1.0, 1.0, ALU.mult, ALU.add))
            dense.was_read(dve, ("in0", 3))
            dve.wait_ge(S["rest_in"], 16)

            lv = cst("levels")

            def gate_step(i):
                G5 = G.rearrange("p c (d k h) -> p c d k h", d=2, k=2)
                if i == 1:
                    bk = dense.filled(dve, "gates")
                    dve.tensor_tensor(G, bk[:, 0:48].rearrange("p (c j) -> p c j", c=NCH),
                                      rowb[:, 8:24].unsqueeze(1).to_broadcast([P, NCH, 16]), ALU.add)\
                        .then_inc(dense.read("gates"), 1)
                    dense.was_read(dve, "gates")
                    dve.engine_nop().then_inc(S["gates_ready"], 1)
                    step(dve.tensor_scalar(LF, G5[:, :, :, 1, :], 0.0, None, ALU.min))
                elif i == 2:
                    dve.wait_ge(S["gates_abs"], 1)
                    dve.tensor_tensor(LF, LF, LE, ALU.subtract).then_inc(S["gates_log"], 1)
                elif i == 3:
                    bk = dense.filled(dve, "B")
                    B4 = bk[:, 0:24].rearrange("p (c d h) -> p c d h", c=NCH, d=2)
                    dve.tensor_copy(GB[:, :, 2:4, :], B4)
                    dve.tensor_tensor(GB[:, :, 0:2, :], G5[:, :, :, 0, :], B4, ALU.subtract).then_inc(dense.read("B"), 1)
                elif 4 <= i < 7:
                    c = i - 4
                    bk = dense.filled(dve, ("rows", c))
                    b4 = bk[0:4, :].rearrange("p (k t) -> p k t", k=4)
                    dve.tensor_copy(row_M[:, :, c * P:(c + 1) * P], b4[:, 0:2])
                    dve.tensor_copy(row_B[:, :, c * P:(c + 1) * P], b4[:, 2:4]).then_inc(dense.read(("rows", c)), 1)
                else:
                    return
                if i == 6:
                    dense.was_read(dve, ("rows", 2))
                    dve.wait_ge(S["m0_in"], 16)
                    for d in range(2):
                        for lo, hi, m0 in ((0, P, 0.0), (P, T, m0_col[:, d:d + 1])):
                            r = row_M[:, d, lo:hi]
                            if d:
                                r = r[:, ::-1]
                            ins = dve.tensor_tensor_scan(r, r, r, m0, ALU.max, ALU.max)
                    step(ins)
                    step(dve.tensor_tensor(row_B, row_B, row_M, ALU.add))
                    for d, t in ((0, P - 1), (1, 0)):
                        dve.tensor_copy(m_out[:, d:d + 1], row_B[:, d, t:t + 1]).then_inc(S["rows_m"], 1)

            for i, L in enumerate(LEVELS):
                if i:
                    misc.filled(dve, ("level", i - 1, 2))
                if L == 0:
                    dve.tensor_copy(Qd[:], q[:])
                    dve.tensor_tensor(Kd[:], kf[:], kb[:], ALU.add).then_inc(S["level_ready"], 1)
                else:
                    halves = lambda t: flat(t).rearrange("p (n two l) -> p n two l", two=2, l=L)
                    (qv, fv, sv, kfv, kbv, sfv, pxv, qdv, kdv) = (halves(t) for t in
                                                                 (q, PF, SI, kf, kb, SF, PX, Qd, Kd))
                    A, B = 0, 1
                    mul = lambda o, a, b: dve.tensor_tensor(o, a, b, ALU.mult)
                    mul(qdv[:, :, B, :], qv[:, :, B, :], fv[:, :, B, :])
                    mul(qdv[:, :, A, :], qv[:, :, A, :], sv[:, :, A, :])
                    if L == 1:
                        dve.tensor_copy(kdv[:, :, A, :], kfv[:, :, A, :])
                        dve.tensor_copy(kdv[:, :, B, :], kbv[:, :, B, :]).then_inc(S["level_ready"], 1)
                        dve.tensor_copy(sfv[:, :, A, :], fv[:, :, B, :])
                        dve.memset(sfv[:, :, B, :], 1.0)
                        dve.tensor_copy(pxv[:, :, B, :], sv[:, :, A, :])
                        step(dve.memset(pxv[:, :, A, :], 1.0))
                    else:
                        mul(kdv[:, :, A, :], kfv[:, :, A, :], sfv[:, :, A, :])
                        mul(kdv[:, :, B, :], kbv[:, :, B, :], pxv[:, :, B, :]).then_inc(S["level_ready"], 1)
                        n = 1536 // (2 * L)
                        wide = lambda v: v.to_broadcast([P, n, L])
                        mul(sfv[:, :, A, :], sfv[:, :, A, :], wide(fv[:, :, B, L - 1:L]))
                        step(mul(pxv[:, :, B, :], pxv[:, :, B, :], wide(sv[:, :, A, 0:1])))
                    n = 1536 // (2 * L)
                    wide = lambda v: v.to_broadcast([P, n, L])
                    mul(fv[:, :, B, :], fv[:, :, B, :], wide(fv[:, :, A, L - 1:L]))
                    step(mul(sv[:, :, A, :], sv[:, :, A, :], wide(sv[:, :, B, 0:1])))
                for c in range(NCH):
                    bk = misc.filled(dve, ("level", i, c))
                    b3 = bk[:, :].rearrange("p (h t) -> p h t", h=H)
                    mask = lv[:, i * P:(i + 1) * P].unsqueeze(1).to_broadcast([P, H, P])
                    if i == 0:
                        dve.tensor_tensor(Am[:, c], b3, mask, ALU.mult).then_inc(misc.read(("level", i, c)), 1)
                        misc.was_read(dve, ("level", i, c))
                    else:
                        dve.copy_predicated(Am[:, c], mask.bitcast(I32), b3).then_inc(misc.read(("level", i, c)), 1)
                gate_step(i)
            step(dve.tensor_tensor(SF[:, :, 0:2 * P], SF[:, :, 0:2 * P], kf[:, :, 0:2 * P], ALU.mult))
            dve.tensor_tensor(PX[:, :, 0:P], PX[:, :, 0:P], kb[:, :, 0:P], ALU.mult).then_inc(S["kfin_ready"], 1)
            dve.tensor_tensor(PX[:, :, 2 * P:T], PX[:, :, 2 * P:T], kb[:, :, 2 * P:T], ALU.mult)\
                .then_inc(S["kfin_ready"], 1)
            for o, f in ((Qd, PF), (Kd, SI)):
                dve.tensor_tensor(o[:, :, P:T], q[:, :, P:T], f[:, :, P:T], ALU.mult).then_inc(S["qi_ready"], 1)
            dve.wait_ge(S["qi_ready"], 2)
            dve.wait_ge(S["state_in"], 16)
            for d, tot in ((0, lambda h: PF[:, h, 2 * P - 1:2 * P]), (1, lambda h: SI[:, h, 2 * P:2 * P + 1])):
                bk = misc.filled(dve, ("kv", 2 + d))
                for h in range(H):
                    ins = dve.scalar_tensor_tensor(S1[:, d, h, :], S0[:, d, h, :], tot(h), bk[:, h * P:(h + 1) * P],
                                                   ALU.mult, ALU.add)
                ins.then_inc(misc.read(("kv", 2 + d)), 1)
            for c in range(NCH):
                bk = dense.filled(dve, ("hg_o", c))
                dve.tensor_copy(o_hg[:, :, c * P:(c + 1) * P], bk[:, :].rearrange("p (h t) -> p h t", h=H))\
                    .then_inc(dense.read(("hg_o", c)), 1)
            modulation("hgrn_norm")

            def head_out(h, src, gate, g, squares, n0, base):
                dve.wait_ge(S["mo_rstd"], n0 + h + 1)
                dve.tensor_tensor(src[:, h, :], src[:, h, :], squares[:, h, :], ALU.mult).then_inc(S["mo_t"], 1)
                dve.wait_ge(S["mo_t"], n0 + h + 1)
                if h >= 2:
                    dve.wait_ge(S["h_ready"], base + h - 1)
                dve.scalar_tensor_tensor(ht[:, h % 2, :], src[:, h, :], g, gate[:, h, :], ALU.mult, ALU.mult)\
                    .then_inc(S["ht_ready"], 1)

            def head_low(h, base):
                dve.wait_ge(S["hhi_ready"], base + h + 1)
                dve.tensor_tensor(h_lo[:, base - 8 + h, :], ht[:, h % 2, :],
                                  h_hi[:, base - 8 + h, :].bitcast(F32), ALU.subtract).then_inc(S["h_ready"], 1)

            dve.wait_ge(S["s_out"], 16)

            def weights(j):
                h, d = j // 2, j % 2
                qk, A, E = QK[:, h % 2, :], Aw[:, j % 2, :], Ew[:, j % 2, :]
                dense.was_read(dve, ("M", j))
                dense.was_read(dve, ("qk10", h))
                if j >= 2:
                    misc.filled(dve, ("num", j - 2))
                if d == 0:
                    ins = dve.tensor_tensor(A, E, qk[:, 0:512], ALU.mult)
                else:
                    dve.tensor_tensor(A[:, 0:2 * P], E[:, 0:2 * P], qk[:, 0:2 * P], ALU.mult)
                    ins = dve.tensor_tensor(A[:, 2 * P:], E[:, 2 * P:], qk[:, 3 * P:5 * P], ALU.mult)
                ins.then_inc(S["A_ready"], 1)
                bk = misc.filled(dve, ("ss", j))
                dve.tensor_tensor(qs[j % 2], qm[:, h, P:T], bk[:, 0:TL], ALU.mult).then_inc(misc.read(("ss", j)), 1)
                if j >= 2:
                    misc.filled(dve, ("C", j - 2))
                if j == 0:
                    misc.was_read(dve, "k_tok")
                at = 127 if d == 0 else 0
                dve.tensor_scalar(k_in[:, j % 2, :], k_tok[:, h * P:(h + 1) * P], E[:, at:at + 1], None,
                                  ALU.mult).then_inc(S["k_in_ready"], 1)

            weights(0)
            for j in range(2 * H):
                h, d = j // 2, j % 2
                if j < 2 * H - 1:
                    weights(j + 1)
                misc.was_read(dve, ("em", j))
                dense.was_read(dve, ("den", j))
                step(dve.tensor_tensor(den, den, em, ALU.max))
                step(dve.reciprocal(den, den))
                bk = misc.filled(dve, ("num", j))
                dst = hm[:, h, :] if d == 0 else hf
                dve.tensor_tensor(dst, bk[:, 0:T], den, ALU.mult).then_inc(misc.read(("num", j)), 1)
                misc.was_read(dve, ("num", j))
                if d == 0:
                    dve.engine_nop().then_inc(S["h_done"], 1)
                else:
                    dve.tensor_tensor(hm[:, h, :], hm[:, h, :], hf, ALU.add).then_inc(S["h_done"], 1)
                    if h:
                        head_low(h - 1, 8)
                    head_out(h, o_hg, ga, col("hgrn_norm_g"), hg_sq, 0, 8)
                modulation("mlstm", ada_pairs("mlstm")[j:j + 1])
            dve.wait_ge(S["h_done"], 8)
            head_low(H - 1, 8)
            modulation("mlstm_norm")
            for h in range(H):
                head_out(h, hm, ob, col("mlstm_norm_g"), ml_sq, 4, 12)
                if h:
                    head_low(h - 1, 12)
            head_low(H - 1, 12)
            for m in range(DT):
                residual(("out", 0, m), 1, 0, m, 2)
            dense.was_read(dve, ("out", 0, 7))
            norm(1, 16, "norm1")
            dve.wait_ge(S["s_out"], 16)
            dve.wait_ge(S["m_sent"], 16)
            dve.wait_ge(S["c_sent"], 32)
            ffn(0)
            norm(2, 24, "norm2")

            def rope(i):
                x = (qc[:, i, P:T] if i < 4 else kT[:, P:T] if i == 4 else kr4[:, P:T] if i == 5
                     else qr[:, i - 6, P:T])
                kind = "swa" if i < 5 else "mla"
                if i == 4:
                    dense.was_read(dve, ("kc",))
                bk = misc.filled(dve, ("rot", i))
                dve.tensor_tensor(rt[:, 0, :], x, cst(kind + "_cos"), ALU.mult)
                dve.tensor_tensor(rt[:, 1, :], bk[:, 0:TL], cst(kind + "_sin"), ALU.mult)\
                    .then_inc(misc.read(("rot", i)), 1)
                misc.was_read(dve, ("rot", i))
                dve.tensor_tensor(x, rt[:, 0, :], rt[:, 1, :], ALU.add).then_inc(S["roped"], 1)
                dve.wait_ge(S["roped"], i + 1)

            for i in range(5):
                rope(i)
            for k in range(5):
                i = 0 if k < 3 else 1
                dve.wait_ge(S["cq_rstd"], i + 1)
                src = cqf[:, k, :] if i == 0 else ckvf[:, k - 3, :]
                g = col("mla_q_norm_g", k) if i == 0 else col("mla_kv_norm_g", k - 3)
                dve.scalar_tensor_tensor(src, src, g, rstd[:, i, :], ALU.mult, ALU.mult).then_inc(S["cq_t"], 1)
            for k in range(5):
                dve.wait_ge(S["cqhi"], k + 1)
                if k < 3:
                    dve.tensor_tensor(cq_lo[:, k, :], cqf[:, k, :], cq_hi[:, k, :].bitcast(F32), ALU.subtract)\
                        .then_inc(S["cq_ready"], 1)
                else:
                    dve.tensor_tensor(ckv_lo[:, k - 3, 0:T], ckvf[:, k - 3, :], ckv_hi[:, k - 3, 0:T].bitcast(F32),
                                      ALU.subtract).then_inc(S["ckv_ready"], 1)

            rope(5)
            dve.wait_ge(S["cache_ready"], 1)
            bk = misc.filled(dve, ("cache",))
            dve.tensor_tensor(ckv_lo[:, :, T:TK], bk[:, 2 * P:512].rearrange("p (k t) -> p k t", k=2),
                              ckv_hi[:, :, T:TK].bitcast(F32), ALU.subtract).then_inc(misc.read(("cache",)), 1)
            rope(6)
            rope(7)

            for n in range(len(jobs) + VALUE_LAG):
                if n < len(jobs):
                    kind, heads, t, k0, nk = jobs[n]
                    scale = 64 ** -0.5 if kind == "swa" else 96 ** -0.5
                    nh = len(heads)
                    s_ = st[:, n % PR]
                    bk = dense.filled(dve, ("s", n))
                    step(dve.tensor_reduce(s_[:, 0, 0:nh], bk[:, 0:nh * nk].rearrange("p (h k) -> p h k", h=nh), AX.X,
                                           ALU.max))
                    if kind == "swa":
                        hs = slice(heads[0], heads[0] + nh)
                        step(dve.scalar_tensor_tensor(s_[:, 1, 0:nh], s_[:, 0, 0:nh], -scale, neg_sink[:, hs],
                                                      ALU.mult, ALU.min))
                        dve.tensor_tensor(s_[:, 3, 0:nh], rowb[:, hs], s_[:, 1, 0:nh], ALU.add)\
                            .then_inc(S["neg_max"], 1)
                    else:
                        dve.tensor_scalar(s_[:, 1, 0:nh], s_[:, 0, 0:nh], -scale, None, ALU.mult)\
                            .then_inc(S["neg_max"], 1)
                if 1 <= n <= len(jobs):
                    kind, heads, t, k0, nk = jobs[n - 1]
                    nh = len(heads)
                    s_ = st[:, (n - 1) % PR]
                    dense.was_read(dve, ("s", n - 1))
                    if kind == "swa":
                        step(dve.tensor_tensor(s_[:, 2, 0:nh], s_[:, 2, 0:nh], s_[:, 3, 0:nh], ALU.add))
                    step(dve.reciprocal(s_[:, 4, 0:nh], s_[:, 2, 0:nh]))
                    for i in range(nh):
                        p = pr[:, (n - 1) % PR, i * nk:(i + 1) * nk]
                        ins = dve.tensor_scalar(p, p, s_[:, 4, i:i + 1], None, ALU.mult)
                    ins.then_inc(S["p_ready"], 1)
                if n >= VALUE_LAG and ends[n - VALUE_LAG][1]:
                    tile = job_tile[n - VALUE_LAG]
                    dve.wait_ge(S["pv_hi"], list(dict.fromkeys(job_tile)).index(tile) + 1)
                    bk = pvs.filled(dve, ("pv", tile))
                    dve.tensor_tensor(mix_part(h_lo, tile), mix_bank(bk, tile), mix_part(h_hi, tile).bitcast(F32),
                                      ALU.subtract).then_inc(pvs.read(("pv", tile)), 1)
            for m in range(DT):
                residual(("out", 1, m), 3, 1, m, 2)
            dense.was_read(dve, ("out", 1, 7))
            norm(3, 32, "norm3")
            dve.wait_ge(S["odd_sent"], 64)
            ffn(1)
            dense.was_read(dve, ("down", 1, 7))
            dve.wait_ge(S["rstd_ready"], 5)
            for m in range(DT):
                if m >= 2:
                    misc.filled(dve, ("y", m - 2))
                dve.scalar_tensor_tensor(ht[:, m % 2, :], X[:, m, :], col("final_norm_g", m), rstd[:, 0, :],
                                         ALU.mult, ALU.mult).then_inc(S["y_ready"], 1)


_INS = ["x_prompt", "x_sample", "state_hgrn", "state_mlstm_c", "state_mlstm_n", "state_mlstm_m",
        "cache_swa_k", "cache_swa_v", "cache_mla_ckv", "cache_mla_krope", "c", "c_ctx",
        "w_in_even", "hgrn_lower_bounds", "hgrn_norm_g", "mlstm_gate_bias", "mlstm_norm_g", "w_out_even",
        "w_in_odd", "swa_sink", "mla_q_norm_g", "mla_w_uq", "mla_kv_norm_g", "mla_w_uk", "mla_w_uv", "w_out_odd",
        "ada_w", "ada_b", "norm1_g", "norm2_g", "ffn_w1", "ffn_w3", "ffn_w2", "final_norm_g"]
_OUTS = [(1, TC, D), (1, TL, D), (1, 1, 2, H, P, P), (1, 1, 2, H, P, P), (1, 1, 2, H, P), (1, 1, 2, H),
         (1, 1, TC, 2, 64), (1, 1, TC, 2, 64), (1, 1, TC, 256), (1, 1, TC, 32)]


def kernel(**inputs):
    import concourse.bacc as _bacc
    from concourse.bass_utils import run_bass_kernel_spmd as _run

    nc = _bacc.Bacc("TRN2", target_bir_lowering=False, num_devices=1, dynamic_dma_scratch_size=4096)
    arrays, I, O = {}, {}, []
    for name in _INS + ["shape_constants"]:
        a = np.ascontiguousarray(inputs[name] if name in inputs else shape_constants())
        arrays[f"in_{name}"] = a
        I[name] = nc.dram_tensor(f"in_{name}", a.shape, mybir.dt.from_np(a.dtype), kind="ExternalInput").ap()
    for i, shape in enumerate(_OUTS):
        O.append(nc.dram_tensor(f"out_{i}", shape, F32, kind="ExternalOutput").ap())
    build(nc, I, O)
    r = _run(nc, [arrays], core_ids=[0])
    return tuple(r.results[0][f"out_{i}"] for i in range(len(_OUTS)))
```
